# Optimizing a Trainium2 kernel written in Bass

```python
import math
import jax, jax.numpy as jnp
from jax import lax
import numpy as np

'''Hybrid autoregressive decoder trunk, DEPTH consecutive layers (pattern repeats every 2 layers).
Even layer: x += W_out [FoX(4 heads) ; GatedDeltaNet(4 heads)] (one combined input projection of RMSNorm(x));
            x += SwiGLU(RMSNorm(x)).
Odd layer:  x += W_out MoBA(8 heads, rotary, QK-norm)(RMSNorm(x));
            x += top-2-of-8 expert SwiGLU(RMSNorm(x)).
Input x: (BATCH, SEQ, D_MODEL) float32. Output: (BATCH, SEQ, D_MODEL).
'''

D_MODEL = 1024
BATCH = 1
SEQ = 256
DEPTH = 2

HEAD_DIM = 128
FOX_HEADS = 4
GDN_HEADS = 4
MOBA_HEADS = D_MODEL // HEAD_DIM
FOX_WIDTH = FOX_HEADS * HEAD_DIM
GDN_WIDTH = GDN_HEADS * HEAD_DIM
MOBA_WIDTH = MOBA_HEADS * HEAD_DIM
Q_BLOCK = 128
GDN_CHUNK = 64
CONV_WIDTH = 4
MOBA_BLOCK = 256
MOBA_TOPK = 3
MOBA_Q_CHUNK = 16
D_FF_DENSE = 2816
N_EXPERTS = 8
TOP_K_EXPERTS = 2
D_FF_EXPERT = 3584
ROPE_THETA = 10000.0
EPS = 1e-6
N_EVEN = (DEPTH + 1) // 2
N_ODD = DEPTH // 2
IN_WIDTHS = (FOX_WIDTH, FOX_WIDTH, FOX_WIDTH, FOX_HEADS, GDN_WIDTH, GDN_WIDTH, GDN_WIDTH, GDN_HEADS, GDN_HEADS, GDN_WIDTH)
IN_COLS = sum(IN_WIDTHS)

kernel_name = 'hybrid_fox_gdn_moba_moe'

F32 = jnp.float32

def rms_norm(x, gain):
    xf = x.astype(F32)
    y = xf * lax.rsqrt(jnp.mean(xf * xf, axis=-1, keepdims=True) + EPS)
    return (y * gain.astype(F32)).astype(x.dtype)

def l2_normalize(x):
    xf = x.astype(F32)
    return xf * lax.rsqrt(jnp.sum(xf * xf, axis=-1, keepdims=True) + EPS)

def to_heads(t, n):
    B, S, _ = t.shape
    return t.reshape(B, S, n, HEAD_DIM).transpose(0, 2, 1, 3)

def from_heads(t):
    B, H, S, D = t.shape
    return t.transpose(0, 2, 1, 3).reshape(B, S, H * D)

def rope(x, pos):
    half = HEAD_DIM // 2
    inv = jnp.power(ROPE_THETA, -jnp.arange(half, dtype=F32) / half)
    ang = pos.astype(F32)[:, None] * inv[None, :]
    cos, sin = jnp.cos(ang), jnp.sin(ang)
    xf = x.astype(F32)
    x1, x2 = xf[..., :half], xf[..., half:]
    return jnp.concatenate([x1 * cos - x2 * sin, x2 * cos + x1 * sin], axis=-1).astype(x.dtype)

def forgetting_attention(q, k, v, log_f):
    B, H, S, D = q.shape
    F = jnp.cumsum(log_f, axis=-1)
    scale = D ** -0.5
    kpos = jnp.arange(S)

    def block(i):
        start = i * Q_BLOCK
        qb = lax.dynamic_slice_in_dim(q, start, Q_BLOCK, axis=2)
        Fq = lax.dynamic_slice_in_dim(F, start, Q_BLOCK, axis=2)
        qpos = start + jnp.arange(Q_BLOCK)
        s = jnp.einsum('bhqd,bhkd->bhqk', qb, k, preferred_element_type=F32) * scale
        s = s + Fq[..., :, None] - F[..., None, :]
        s = jnp.where(kpos[None, :] <= qpos[:, None], s, -jnp.inf)
        p = jax.nn.softmax(s, axis=-1)
        return jnp.einsum('bhqk,bhkd->bhqd', p.astype(v.dtype), v)

    out = lax.map(block, jnp.arange(S // Q_BLOCK))
    return jnp.moveaxis(out, 0, 2).reshape(B, H, S, D)

def causal_depthwise_conv(x, w):
    K, C = w.shape
    return lax.conv_general_dilated(x, w[:, None, :], window_strides=(1,), padding=[(K - 1, 0)],
                                    dimension_numbers=('NWC', 'WIO', 'NWC'), feature_group_count=C)

def gated_delta_rule(q, k, v, g, beta):
    B, H, S, Dk = q.shape
    Dv = v.shape[-1]
    C = GDN_CHUNK
    N = S // C
    q = q * Dk ** -0.5
    q, k, v = (t.reshape(B, H, N, C, t.shape[-1]) for t in (q, k, v))
    g, beta = (t.reshape(B, H, N, C) for t in (g, beta))
    gc = jnp.cumsum(g, axis=-1)
    idx = jnp.arange(C)
    strict = idx[:, None] > idx[None, :]
    incl = idx[:, None] >= idx[None, :]
    diff = gc[..., :, None] - gc[..., None, :]
    decay = jnp.where(incl, jnp.exp(jnp.where(incl, diff, 0.0)), 0.0)
    kb = k * beta[..., None]
    M = jnp.where(strict, jnp.einsum('bhncd,bhnsd->bhncs', kb, k) * decay, 0.0)
    A = jnp.eye(C, dtype=F32) + M
    rhs = jnp.concatenate([v * beta[..., None], kb * jnp.exp(gc)[..., None]], axis=-1)
    sol = lax.linalg.triangular_solve(A, rhs, left_side=True, lower=True, unit_diagonal=True)
    u, w = sol[..., :Dv], sol[..., Dv:]
    attn = jnp.einsum('bhncd,bhnsd->bhncs', q, k) * decay
    qg = q * jnp.exp(gc)[..., None]
    kg = k * jnp.exp(gc[..., -1:] - gc)[..., None]
    glast = jnp.exp(gc[..., -1])

    def step(state, xs):
        u_c, w_c, attn_c, qg_c, kg_c, gl_c = xs
        v_new = u_c - jnp.einsum('bhcd,bhde->bhce', w_c, state)
        o = jnp.einsum('bhcd,bhde->bhce', qg_c, state) + jnp.einsum('bhcs,bhse->bhce', attn_c, v_new)
        state = state * gl_c[..., None, None] + jnp.einsum('bhcd,bhce->bhde', kg_c, v_new)
        return state, o

    xs = tuple(jnp.moveaxis(t, 2, 0) for t in (u, w, attn, qg, kg, glast))
    _, o = lax.scan(step, jnp.zeros((B, H, Dk, Dv), F32), xs)
    return jnp.moveaxis(o, 0, 2).reshape(B, H, S, Dv)

def gdn_branch(gq, gk, gv, ga, gb, gg, conv_w, a_log, dt_bias, o_norm):
    B, S, _ = gq.shape
    qkv = jnp.concatenate([gq, gk, gv], axis=-1).astype(F32)
    qkv = jax.nn.silu(causal_depthwise_conv(qkv, conv_w.astype(F32)))
    q, k, v = jnp.split(qkv, 3, axis=-1)
    q = l2_normalize(to_heads(q, GDN_HEADS))
    k = l2_normalize(to_heads(k, GDN_HEADS))
    v = to_heads(v, GDN_HEADS)
    beta = jax.nn.sigmoid(gb.astype(F32)).transpose(0, 2, 1)
    g = (-jnp.exp(a_log.astype(F32)) * jax.nn.softplus(ga.astype(F32) + dt_bias.astype(F32))).transpose(0, 2, 1)
    o = gated_delta_rule(q, k, v, g, beta)
    o = rms_norm(o.transpose(0, 2, 1, 3), o_norm) * jax.nn.silu(gg.astype(F32).reshape(B, S, GDN_HEADS, HEAD_DIM))
    return o.reshape(B, S, GDN_WIDTH).astype(gq.dtype)

def even_mixer(h, w_in, fox_f_bias, fox_q_norm, fox_k_norm, gdn_conv, gdn_a_log, gdn_dt_bias, gdn_o_norm, w_out):
    z = h @ w_in
    offsets = np.cumsum(IN_WIDTHS)[:-1].tolist()
    fq, fk, fv, ff, gq, gk, gv, ga, gb, gg = jnp.split(z, offsets, axis=-1)
    q = rms_norm(to_heads(fq, FOX_HEADS), fox_q_norm)
    k = rms_norm(to_heads(fk, FOX_HEADS), fox_k_norm)
    v = to_heads(fv, FOX_HEADS)
    log_f = jax.nn.log_sigmoid(ff.astype(F32) + fox_f_bias.astype(F32)).transpose(0, 2, 1)
    fox_out = from_heads(forgetting_attention(q, k, v, log_f))
    gdn_out = gdn_branch(gq, gk, gv, ga, gb, gg, gdn_conv, gdn_a_log, gdn_dt_bias, gdn_o_norm)
    return jnp.concatenate([fox_out, gdn_out.astype(fox_out.dtype)], axis=-1) @ w_out

def moba_attention(q, k, v):
    B, H, S, D = q.shape
    nblk = -(-S // MOBA_BLOCK)
    pad = nblk * MOBA_BLOCK - S
    if pad:
        k = jnp.pad(k, ((0, 0), (0, 0), (0, pad), (0, 0)))
        v = jnp.pad(v, ((0, 0), (0, 0), (0, pad), (0, 0)))
    topk = min(MOBA_TOPK, nblk)
    scale = D ** -0.5
    kb = k.reshape(B, H, nblk, MOBA_BLOCK, D)
    vb = v.reshape(B, H, nblk, MOBA_BLOCK, D)
    kmean = jnp.mean(kb.astype(F32), axis=3)
    k_flat = kb.reshape(B * H * nblk, MOBA_BLOCK, D)
    v_flat = vb.reshape(B * H * nblk, MOBA_BLOCK, D)
    bh_off = (jnp.arange(B * H) * nblk).reshape(B, H, 1, 1)
    blk_ids = jnp.arange(nblk)
    inner = jnp.arange(MOBA_Q_CHUNK)
    kin = jnp.arange(MOBA_BLOCK)
    n_sel = topk * MOBA_BLOCK

    def chunk(ci):
        start = ci * MOBA_Q_CHUNK
        qc = lax.dynamic_slice_in_dim(q, start, MOBA_Q_CHUNK, axis=2)
        cur = start // MOBA_BLOCK
        gate = jnp.einsum('bhqd,bhnd->bhqn', qc.astype(F32), kmean)
        gate = jnp.where(blk_ids < cur, gate, -jnp.inf)
        _, sel = lax.top_k(gate, topk)
        valid = sel < cur
        ks = k_flat[bh_off + sel]
        vs = v_flat[bh_off + sel]
        s_sel = jnp.einsum('bhqd,bhqjsd->bhqjs', qc, ks, preferred_element_type=F32) * scale
        s_sel = jnp.where(valid[..., None], s_sel, -jnp.inf).reshape(B, H, MOBA_Q_CHUNK, n_sel)
        k_own = kb[:, :, cur]
        v_own = vb[:, :, cur]
        qpos_in = start - cur * MOBA_BLOCK + inner
        s_own = jnp.einsum('bhqd,bhsd->bhqs', qc, k_own, preferred_element_type=F32) * scale
        s_own = jnp.where(kin[None, :] <= qpos_in[:, None], s_own, -jnp.inf)
        p = jax.nn.softmax(jnp.concatenate([s_sel, s_own], axis=-1), axis=-1).astype(v.dtype)
        p_sel = p[..., :n_sel].reshape(B, H, MOBA_Q_CHUNK, topk, MOBA_BLOCK)
        return (jnp.einsum('bhqjs,bhqjsd->bhqd', p_sel, vs)
                + jnp.einsum('bhqs,bhsd->bhqd', p[..., n_sel:], v_own))

    out = lax.map(chunk, jnp.arange(S // MOBA_Q_CHUNK))
    return jnp.moveaxis(out, 0, 2).reshape(B, H, S, D)

def odd_mixer(h, w_qkv, q_norm, k_norm, w_out, pos):
    fq, fk, fv = jnp.split(h @ w_qkv, 3, axis=-1)
    q = rope(rms_norm(to_heads(fq, MOBA_HEADS), q_norm), pos)
    k = rope(rms_norm(to_heads(fk, MOBA_HEADS), k_norm), pos)
    v = to_heads(fv, MOBA_HEADS)
    return from_heads(moba_attention(q, k, v)) @ w_out

def swiglu(h, w_gate_up, w_down):
    gt, up = jnp.split(h @ w_gate_up, 2, axis=-1)
    return (jax.nn.silu(gt) * up) @ w_down

def moe_swiglu(h, w_router, w_gate_up, w_down):
    B, S, D = h.shape
    t = h.reshape(B * S, D)
    logits = (t @ w_router).astype(F32)
    top_v, top_i = lax.top_k(logits, TOP_K_EXPERTS)
    gates = jax.nn.softmax(top_v, axis=-1)
    combine = jnp.sum(jax.nn.one_hot(top_i, N_EXPERTS, dtype=F32) * gates[..., None], axis=1)
    out = jnp.zeros_like(t)
    for e in range(N_EXPERTS):
        out = out + combine[:, e:e + 1].astype(t.dtype) * swiglu(t, w_gate_up[e], w_down[e])
    return out.reshape(B, S, D)

def setup_inputs(seed: int = 0) -> dict:
    key = jax.random.key(seed)
    ks = jax.random.split(key, 32)

    def nrm(k, shape, scale):
        return jax.random.normal(k, shape, F32) * scale

    NE, NO = N_EVEN, N_ODD
    dinv = D_MODEL ** -0.5
    dt = jnp.exp(jax.random.uniform(ks[8], (NE, GDN_HEADS), F32, math.log(1e-3), math.log(1e-1)))
    return {
        'x': nrm(ks[0], (BATCH, SEQ, D_MODEL), 1.0),
        'e_norm1': 1.0 + nrm(ks[1], (NE, D_MODEL), 0.02),
        'e_w_in': nrm(ks[2], (NE, D_MODEL, IN_COLS), dinv),
        'e_fox_f_bias': 2.0 + nrm(ks[3], (NE, FOX_HEADS), 0.5),
        'e_fox_q_norm': 1.0 + nrm(ks[4], (NE, HEAD_DIM), 0.02),
        'e_fox_k_norm': 1.0 + nrm(ks[5], (NE, HEAD_DIM), 0.02),
        'e_gdn_conv': nrm(ks[6], (NE, CONV_WIDTH, 3 * GDN_WIDTH), CONV_WIDTH ** -0.5),
        'e_gdn_a_log': jnp.log(jax.random.uniform(ks[7], (NE, GDN_HEADS), F32, 1.0, 16.0)),
        'e_gdn_dt_bias': dt + jnp.log(-jnp.expm1(-dt)),
        'e_gdn_o_norm': 1.0 + nrm(ks[9], (NE, HEAD_DIM), 0.02),
        'e_w_out': nrm(ks[10], (NE, FOX_WIDTH + GDN_WIDTH, D_MODEL), (FOX_WIDTH + GDN_WIDTH) ** -0.5),
        'e_norm2': 1.0 + nrm(ks[11], (NE, D_MODEL), 0.02),
        'e_ffn_w_gate_up': nrm(ks[12], (NE, D_MODEL, 2 * D_FF_DENSE), dinv),
        'e_ffn_w_down': nrm(ks[13], (NE, D_FF_DENSE, D_MODEL), D_FF_DENSE ** -0.5),
        'o_norm1': 1.0 + nrm(ks[14], (NO, D_MODEL), 0.02),
        'o_w_qkv': nrm(ks[15], (NO, D_MODEL, 3 * MOBA_WIDTH), dinv),
        'o_q_norm': 1.0 + nrm(ks[16], (NO, HEAD_DIM), 0.02),
        'o_k_norm': 1.0 + nrm(ks[17], (NO, HEAD_DIM), 0.02),
        'o_w_out': nrm(ks[18], (NO, MOBA_WIDTH, D_MODEL), MOBA_WIDTH ** -0.5),
        'o_norm2': 1.0 + nrm(ks[19], (NO, D_MODEL), 0.02),
        'o_router': nrm(ks[20], (NO, D_MODEL, N_EXPERTS), dinv),
        'o_exp_w_gate_up': nrm(ks[21], (NO, N_EXPERTS, D_MODEL, 2 * D_FF_EXPERT), dinv),
        'o_exp_w_down': nrm(ks[22], (NO, N_EXPERTS, D_FF_EXPERT, D_MODEL), D_FF_EXPERT ** -0.5),
    }

def reference(x, e_norm1, e_w_in, e_fox_f_bias, e_fox_q_norm, e_fox_k_norm, e_gdn_conv, e_gdn_a_log,
              e_gdn_dt_bias, e_gdn_o_norm, e_w_out, e_norm2, e_ffn_w_gate_up, e_ffn_w_down,
              o_norm1, o_w_qkv, o_q_norm, o_k_norm, o_w_out, o_norm2, o_router, o_exp_w_gate_up, o_exp_w_down):
    pos = jnp.arange(x.shape[1])
    h = x
    for layer in range(DEPTH):
        i = layer // 2
        if layer % 2 == 0:
            h = h + even_mixer(rms_norm(h, e_norm1[i]), e_w_in[i], e_fox_f_bias[i], e_fox_q_norm[i], e_fox_k_norm[i],
                               e_gdn_conv[i], e_gdn_a_log[i], e_gdn_dt_bias[i], e_gdn_o_norm[i], e_w_out[i])
            h = h + swiglu(rms_norm(h, e_norm2[i]), e_ffn_w_gate_up[i], e_ffn_w_down[i])
        else:
            h = h + odd_mixer(rms_norm(h, o_norm1[i]), o_w_qkv[i], o_q_norm[i], o_k_norm[i], o_w_out[i], pos)
            h = h + moe_swiglu(rms_norm(h, o_norm2[i]), o_router[i], o_exp_w_gate_up[i], o_exp_w_down[i])
    return h


_drawn_inputs = setup_inputs


def setup_inputs(seed=0):
    import zlib

    import numpy as np

    out = dict(_drawn_inputs(seed))
    spreads = {}
    factors = {'e_fox_k_norm': 2.867,
     'e_gdn_o_norm': 2.878,
     'o_norm1': 3.083,
     'o_q_norm': 8.0,
     'o_k_norm': 2.797,
     'o_norm2': 4.156}
    for name, (base, spread) in spreads.items():
        noise = np.random.default_rng([zlib.crc32(name.encode()), seed]).standard_normal(out[name].shape)
        drawn = base * np.exp(spread * noise) if base else spread * noise
        out[name] = __import__('jax').numpy.asarray(drawn.astype(out[name].dtype))
    for name, factor in factors.items():
        out[name] = (out[name] * factor).astype(out[name].dtype)
    return out
```

```python
import math
from contextlib import ExitStack

import concourse.bass as bass
from concourse import mybir

P = 128
TOK = 256
NT = TOK // P
DM = 1024
KC = DM // P
HD = 128
H0 = 4
H1 = 8
FF = 2816
NE = 8
FE = 3584
EPS = 1e-6
SCALE = HD ** -0.5
BLK = 512
CH = 4 * BLK
RAW = 6
SPL = 3
NEG = -1e30

LEVELS = [1 << i for i in range(7)]
C_ID, C_U, C_L, C_US, C_ONE, C_BIAS, C_IOTA = 0, 128, 256, 384, 512, 640, 1024
C_LEV = 1152
C_COS = C_LEV + 128 * len(LEVELS)
C_SIN = C_COS + 128
C_IO8 = C_SIN + 128
NCONST = C_IO8 + 8

N_IN = 0
N_OUT = N_IN + 14
N_FFN = N_OUT + 4
N_QKV = N_FFN + 33
N_WO = N_QKV + 12
N_MOE = N_WO + 4
PER_E = 42
FS = FF // 256
ES = FE // BLK

SMALL = ["fb", "al", "dt", "qn", "kn", "on", "oq", "ok"]
SM_AT = {"fb": 0, "al": 4, "dt": 8, "qn": 16, "kn": 144, "on": 272, "oq": 400, "ok": 528}
NSMALL = 656


def shape_constants():
    import numpy as np
    c = np.zeros((P, NCONST), np.float32)
    i = np.arange(P)
    row, col = i[:, None], i[None, :]
    c[:, C_ID:C_ID + P] = row == col
    c[:, C_U:C_U + P] = row <= col
    c[:, C_L:C_L + P] = row > col
    c[:, C_US:C_US + P] = row < col
    c[:, C_ONE:C_ONE + P] = 1.0
    causal = np.where(col > row, np.float32(NEG), np.float32(0))
    c[:, C_BIAS:C_BIAS + P] = causal
    c[:, C_BIAS + 2 * P:C_BIAS + 3 * P] = causal
    c[:, C_IOTA:C_IOTA + P] = col
    for n, b in enumerate(LEVELS):
        pair = (row // (2 * b) == col // (2 * b)) & ((row // b) % 2 == 0) & ((col // b) % 2 == 1)
        c[:, C_LEV + n * P:C_LEV + (n + 1) * P] = pair
    half = HD // 2
    inv = np.power(np.float32(10000.0), -np.arange(half, dtype=np.float32) / np.float32(half))
    ang = np.arange(TOK, dtype=np.float32)[:, None] * inv[None, :]
    for t in range(NT):
        c[:, C_COS + half * t:C_COS + half * (t + 1)] = np.cos(ang[t * P:(t + 1) * P])
        c[:, C_SIN + half * t:C_SIN + half * (t + 1)] = np.sin(ang[t * P:(t + 1) * P])
    c[:, C_IO8:C_IO8 + 8] = np.arange(8)[None, :]
    return c


def build(nc, a, out, last="moe"):
    f32 = mybir.dt.float32
    f32r = mybir.dt.float32r
    u32 = mybir.dt.uint32
    i32 = mybir.dt.int32
    ALU = mybir.AluOpType
    ACT = mybir.ActivationFunctionType
    AX = mybir.AxisListType
    stages = ["in", "mix0", "ffn", "mix1", "moe"]
    upto = stages.index(last)

    ctx = ExitStack()
    with ctx:
        def sb(name, shape, dt=f32):
            return ctx.enter_context(nc.sbuf_tensor(name, shape, dt))

        raw = sb("raw", [P, RAW, CH])
        w_hi = sb("w_hi", [P, SPL, CH], f32r)
        w_lo = sb("w_lo", [P, SPL, CH], f32r)
        x_hi = sb("x_hi", [P, KC * TOK], f32r)
        x_lo = sb("x_lo", [P, KC * TOK], f32r)
        a_hi = sb("a_hi", [P, 2, BLK], f32r)
        a_lo = sb("a_lo", [P, 2, BLK], f32r)
        h = sb("h", [P, NT, DM])
        consts = sb("consts", [P, NCONST])
        small = sb("small", [P, NSMALL])
        misc = sb("misc", [P, 512])
        ws_raw = sb("ws_raw", [P, KC, 12])
        ws_hi = sb("ws_hi", [P, KC, 12], f32r)
        ws_lo = sb("ws_lo", [P, KC, 12], f32r)
        wr_raw = sb("wr_raw", [P, KC, NE])
        wr_hi = sb("wr_hi", [P, KC, NE], f32r)
        wr_lo = sb("wr_lo", [P, KC, NE], f32r)
        idx8 = sb("idx8", [P, NT, 8], u32)
        flag = sb("flag", [1, 1], i32)
        arena = sb("arena", [P, 16960])
        gain = sb("gain", [P, DM])
        bank = [ctx.enter_context(nc.psum_tensor(f"bank{i}", [P, BLK], f32)) for i in range(8)]

        xT_hi = x_hi[:, :].rearrange("p (k t) -> p k t", k=KC)
        xT_lo = x_lo[:, :].rearrange("p (k t) -> p k t", k=KC)

        def cst(at, n=P):
            return consts[:, at:at + n]

        ident = cst(C_ID)

        def smallv(name, n):
            return small[:, SM_AT[name]:SM_AT[name] + n]

        def area(at, *dims):
            n = 1
            for d in dims:
                n *= d
            v = arena[:, at:at + n]
            if len(dims) == 1:
                return v
            if len(dims) == 2:
                return v.rearrange("p (a b) -> p a b", a=dims[0])
            return v.rearrange("p (a b c) -> p a b c", a=dims[0], b=dims[1])

        gg = area(0, NT, BLK)
        zq, zk, zv = (area(1024 * (i + 1), NT, BLK) for i in range(3))
        zT = area(4096, 12, 259)
        cT = area(7204, 12, TOK)
        qT = area(10276, H0, TOK)
        kT = area(11300, H0, TOK)
        bias0 = area(12324, H0, 384)
        rows_out = area(14884, NT, DM)
        att_s = sb("att_s", [P, 2, 384])
        att_T = sb("att_T", [P, 2, 384])
        sq8 = area(4096, 8, TOK)
        Xi, Yi, Zi = (area(4096 + 1024 * i, 8, P) for i in range(3))
        bc8 = area(6144, 8, P)
        DT, MT, AT = (area(1024 * (i + 1), 8, P) for i in range(3))
        bv = area(10276, 8, P)
        kg0 = area(11300, H0, P)
        kb1 = area(11812, H0, P)
        NTl = [area(12324 + 1024 * i, 8, P) for i in range(2)]
        vn = area(12324, NT, H0 * P)
        wT1 = area(13348, H0, P)
        S1 = area(13860, H0, P)
        hn = area(10276, NT, DM)
        zq1, zk1, zv1 = (area(2048 * i, NT, DM) for i in range(3))
        tmp1 = area(6144, NT, DM)
        rows_out1 = area(8192, NT, DM)
        qT1 = area(10276, H1, TOK)
        kT1 = area(12324, H1, TOK)
        sil = area(0, 2, BLK)
        act = area(1024, 2, BLK)
        y_sb = area(2048, DM)
        perm = area(3072, NT, P)
        permc = area(3328, NT, P)
        permT = area(3584, NT, P)

        ss = misc[:, 0:8]
        rstd = misc[:, 8:16]
        m8 = misc[:, 16:32]
        pre = misc[:, 32:56].rearrange("p (t c) -> p t c", t=NT)
        gl = misc[:, 56:80].rearrange("p (t c) -> p t c", t=NT)
        coef = misc[:, 80:92]
        t24 = misc[:, 92:116].rearrange("p (t c) -> p t c", t=NT)
        u24 = misc[:, 116:140].rearrange("p (t c) -> p t c", t=NT)
        cols = misc[:, 140:160]
        e8 = misc[:, 160:168]
        beta = misc[:, 168:176].rearrange("p (t c) -> p t c", t=NT)
        be1 = misc[:, 176:180]
        hs = misc[:, 180:212]
        hr = misc[:, 212:244]
        nm = misc[:, 244:248].rearrange("p (b t) -> p b t", b=2)
        ls = misc[:, 248:252].rearrange("p (b t) -> p b t", b=2)
        rl = misc[:, 252:256].rearrange("p (b t) -> p b t", b=2)
        cw = misc[:, 256:304].rearrange("p (k c) -> p k c", k=4)
        cwr = misc[0:48, 304:432]
        lg = misc[:, 432:448].rearrange("p (t e) -> p t e", t=NT)
        rank = misc[:, 448:466].rearrange("p (t e) -> p t e", t=NT)
        comb = misc[:, 466:484].rearrange("p (t e) -> p t e", t=NT)
        g2 = misc[:, 484:492].rearrange("p (t c) -> p t c", t=NT)
        scr = misc[:, 500:501]

        names = """consts_in x_in small_in conv_in wsmall_in gain_in gain_used dve_step act_step
            hi_done lo_done chunk_used ws_split h_ready sq_done mean_done root_done rows_done tr_done xh_done
            xl_done cw_T cw_done pre_ps pre_done softplus_e softplus_l gates_done beta_done bc_done cum_ps
            cum_done z_out zT_done cT_done sq_made norm_ps norm_add norm_root norm_done qk_rows_done qk_tr
            qk_T bias_done scores_ready sc_done exp_done p_tr pT_done pv_ready o_done hs_done hr_root
            kv_tr kv_done gcb_ps diff_done decay_done kk_ps MT_done AT_done nt_done z_ps Zi_done xy_ps xy_done
            u_ps vn_done w_ps wT_done s_ps S_done o_ps go_done silu_g og_done out_ps act_sil act_done aT_hi aT_lo down_done
            lg_ps lg_done g_exp route_done rank_ps rank_done perm_done g_ps y_zero y_done permT_ps permT_done
            sc_ps sc_add a_tr h_out flag_done out_done seed""".split()
        S = {n: ctx.enter_context(nc.semaphore(n)) for n in names}
        raw_in = [ctx.enter_context(nc.semaphore(f"raw_in{i}")) for i in range(RAW)]
        block = ctx.enter_context(nc.Block())

        chunk_limit = [N_OUT, N_FFN, N_QKV, N_MOE, 1 << 30][upto]

        IN_COL = [1540, 2052, 2564, 0, 512, 1024, 3084]

        def dense_source(n):
            def quarter(w, k, c):
                return w[k * 512:(k + 1) * 512, c:c + BLK].rearrange("(k p) n -> p k n", p=P)
            if n < N_OUT:
                return quarter(a["e_w_in"][0], n % 2, IN_COL[n // 2])
            if n < N_FFN:
                return quarter(a["e_w_out"][0], (n - N_OUT) % 2, (n - N_OUT) // 2 * BLK)
            if N_QKV <= n < N_WO:
                return quarter(a["o_w_qkv"][0], (n - N_QKV) % 2, (n - N_QKV) // 2 * BLK)
            return quarter(a["o_w_out"][0], (n - N_WO) % 2, (n - N_WO) // 2 * BLK)

        @block.sync
        def _(sp):
            def load(k, src, n):
                if k >= RAW or not isinstance(n, int):
                    sp.wait_ge(S["lo_done"], n - RAW + 1)
                sp.dma_start(raw[:, k % RAW, 0:CH].rearrange("p (k n) -> p k n", k=src.shape[1]),
                             src).then_inc(raw_in[k % RAW], 16)

            sp.dma_start(consts[:, :], a["consts"]).then_inc(S["consts_in"], 16)
            for n in range(N_IN, min(N_FFN, chunk_limit)):
                load(n, dense_source(n), n)
            if upto >= 2:
                wgu, wd = a["e_ffn_w_gate_up"][0], a["e_ffn_w_down"][0]

                def ffn_gu(j, up):
                    return wgu[:, bass.ds(up * FF + j * 256, 256)].rearrange("(k p) n -> p k n", p=P)

                def ffn_d(j):
                    return wd[bass.ds(j * 256, 256), :].rearrange("(k p) n -> p k n", p=P)

                load(N_FFN, ffn_gu(0, 0), N_FFN)
                load(N_FFN + 1, ffn_gu(0, 1), N_FFN + 1)
                with sp.Fori(0, (FS - 1) // 2) as i:
                    for q in range(2):
                        for c, src in enumerate((ffn_gu(2 * i + q + 1, 0), ffn_gu(2 * i + q + 1, 1),
                                                 ffn_d(2 * i + q))):
                            k = N_FFN + 2 + 3 * q + c
                            load(k, src, i * 6 + k)
                load(N_QKV - 1, ffn_d(FS - 1), N_QKV - 1)
            for n in range(N_QKV, min(N_MOE, chunk_limit)):
                load(n, dense_source(n), n)
            if upto >= 4:
                egu, ed = a["o_exp_w_gate_up"][0], a["o_exp_w_down"][0]

                def expert_loads(e, base):
                    def gu(j, up, k):
                        c = up * FE + j * BLK
                        return egu[bass.ds(e, 1), k * 512:(k + 1) * 512, c:c + BLK]\
                            .rearrange("o (k p) n -> p (o k) n", p=P)

                    def dn(j, k):
                        r = j * BLK + k * 256
                        return ed[bass.ds(e, 1), r:r + 256, :].rearrange("o (k p) n -> p (o k) n", p=P)
                    c = 0
                    for j in range(ES):
                        srcs = [gu(j, up, k) for up in range(2) for k in range(2)]
                        if j >= 1:
                            srcs += [dn(j - 1, k) for k in range(2)]
                        if j == ES - 1:
                            srcs += [dn(j, k) for k in range(2)]
                        for src in srcs:
                            load(base + c, src, e * PER_E + (base + c))
                            c += 1
                with sp.Fori(0, NE) as e:
                    expert_loads(e, N_MOE)
                sp.wait_ge(S["flag_done"], 1)
                over = sp.value_load(flag[0:1, 0:1], min_val=0, max_val=NE)
                with sp.If(over > 0):
                    with sp.Fori(0, NE) as e:
                        expert_loads(e, N_MOE + NE * PER_E)
            sp.wait_ge(S["h_out"], 1)
            for t in range(NT):
                sp.dma_start(out[0, t * P:(t + 1) * P, :], h[:, t, :]).then_inc(S["out_done"], 16)
            sp.wait_ge(S["out_done"], 16 * NT)

        @block.gpsimd
        def _(gp):
            for t in range(NT):
                gp.dma_start(h[:, t, :], a["x"][0, t * P:(t + 1) * P, :]).then_inc(S["x_in"], 16)

            def load_gain(name):
                gp.dma_start(gain[:, :], a[name][0:1, :].to_broadcast([P, DM])).then_inc(S["gain_in"], 16)
            load_gain("e_norm1")
            gp.dma_start(cwr, a["e_gdn_conv"][0].rearrange("k (c p) -> (k c) p", p=P)).then_inc(S["conv_in"], 16)
            for n, (name, key) in enumerate(zip(SMALL, ["e_fox_f_bias", "e_gdn_a_log", "e_gdn_dt_bias", "e_fox_q_norm",
                                                        "e_fox_k_norm", "e_gdn_o_norm", "o_q_norm", "o_k_norm"])):
                w = a[key].shape[1]
                gp.dma_start(small[:, SM_AT[name]:SM_AT[name] + w], a[key][0:1, :].to_broadcast([P, w]))\
                    .then_inc(S["small_in"], 16)
            w_in = a["e_w_in"][0].rearrange("(k p) n -> p k n", p=P)
            gp.dma_start(ws_raw[:, :, 0:4], w_in[:, :, 1536:1540]).then_inc(S["wsmall_in"], 16)
            gp.dma_start(ws_raw[:, :, 4:12], w_in[:, :, 3076:3084]).then_inc(S["wsmall_in"], 16)
            gp.dma_start(wr_raw[:, :, :], a["o_router"][0].rearrange("(k p) n -> p k n", p=P))\
                .then_inc(S["wsmall_in"], 16)
            for r, name in enumerate(["e_norm2", "o_norm1", "o_norm2"]):
                if upto >= r + (2 if r else 2):
                    gp.wait_ge(S["gain_used"], r + 1)
                    load_gain(name)

        @block.tensor
        def _(pe):
            def rows_to_T(src, r, need):
                pe.wait_ge(S[need[0]], need[1])
                for b in range(4):
                    for kc in (2 * b, 2 * b + 1):
                        for t in range(NT):
                            at = (kc % 2) * TOK + t * P
                            m = pe.transpose(bank[b][:, at:at + P], src[:, t, kc * P:(kc + 1) * P], ident)
                    m.then_inc(S["tr_done"], 1)

            def passes(dst, lhs, rhs, first, final):
                pe.matmul(dst, lhs[0], rhs[0], start=first, stop=False, skip_group_check=True)
                pe.matmul(dst, lhs[1], rhs[0], start=False, stop=False, skip_group_check=True)
                return pe.matmul(dst, lhs[0], rhs[1], start=False, stop=final, skip_group_check=True)

            def split_w(k, c0, n):
                s = k % SPL
                return w_hi[:, s, c0:c0 + n], w_lo[:, s, c0:c0 + n]

            def split_x(kc, t0, n):
                return xT_hi[:, kc, t0:t0 + n], xT_lo[:, kc, t0:t0 + n]

            def row_group(n0, pair, free):
                if free:
                    pe.wait_ge(S[free[0]], free[1])
                for half in range(2):
                    pe.wait_ge(S["lo_done"], n0 + half + 1)
                    for kc in range(4):
                        for t in range(NT):
                            m = passes(bank[2 * pair + t][:, :], split_x(4 * half + kc, t * P, P),
                                       split_w(n0 + half, kc * BLK, BLK),
                                       half == 0 and kc == 0, half == 1 and kc == 3)
                    m.then_inc(S["chunk_used"], 1)

            def col_group(n0, pair, free):
                if free:
                    pe.wait_ge(S[free[0]], free[1])
                for half in range(2):
                    pe.wait_ge(S["lo_done"], n0 + half + 1)
                    for kc in range(4):
                        for c in range(4):
                            m = passes(bank[2 * pair + c // 2][:, (c % 2) * TOK:(c % 2 + 1) * TOK],
                                       split_w(n0 + half, kc * BLK + c * P, P),
                                       split_x(4 * half + kc, 0, TOK),
                                       half == 0 and kc == 0 and c % 2 == 0, half == 1 and kc == 3)
                    m.then_inc(S["chunk_used"], 1)

            def attention(heads, qTt, kTt, v, done):
                def scores(i):
                    if done + i >= 2:
                        pe.wait_ge(S["sc_done"], done + i - 1)
                    pe.matmul(bank[i % 2][:, 0:P], qTt[:, i, 0:P], kTt[:, i, 0:P], start=True, stop=True)
                    pe.matmul(bank[i % 2][:, P:3 * P], qTt[:, i, P:TOK], kTt[:, i, :],
                              start=True, stop=True).then_inc(S["scores_ready"], 1)

                def turn(i):
                    pe.wait_ge(S["exp_done"], done + i + 1)
                    if done + i >= 2:
                        pe.wait_ge(S["pT_done"], done + i - 1)
                    for b in range(3):
                        m = pe.transpose(bank[2 + i % 2][:, b * P:(b + 1) * P],
                                         att_s[:, i % 2, b * P:(b + 1) * P], ident)
                    m.then_inc(S["p_tr"], 1)

                def weigh(i):
                    pe.wait_ge(S["pT_done"], done + i + 1)
                    if done + i >= 2:
                        pe.wait_ge(S["o_done"], done + i - 1)
                    b = bank[4 + i % 2]
                    pe.matmul(b[:, 0:P], att_T[:, i % 2, 0:P], v[:, 0, i * P:(i + 1) * P], start=True, stop=True)
                    pe.matmul(b[:, P:2 * P], att_T[:, i % 2, P:2 * P], v[:, 0, i * P:(i + 1) * P],
                              start=True, stop=False)
                    pe.matmul(b[:, P:2 * P], att_T[:, i % 2, 2 * P:3 * P], v[:, 1, i * P:(i + 1) * P],
                              start=False, stop=True).then_inc(S["pv_ready"], 1)
                for i in range(heads + 2):
                    if i < heads:
                        scores(i)
                    if 1 <= i <= heads:
                        turn(i - 1)
                    if i >= 2:
                        weigh(i - 2)

            pe.wait_ge(S["consts_in"], 16)
            pe.wait_ge(S["conv_in"], 16)
            pe.transpose(bank[5][:, 0:48], cwr, ident[0:48, 0:48]).then_inc(S["cw_T"], 1)
            rows_to_T(hn, 0, ("rows_done", 1))
            pe.wait_ge(S["xl_done"], 4)
            pe.wait_ge(S["ws_split"], 2)
            for t in range(NT):
                for kc in range(KC):
                    m = passes(bank[4][:, 12 * t:12 * t + 12], split_x(kc, t * P, P),
                               (ws_hi[:, kc, :], ws_lo[:, kc, :]), kc == 0, kc == KC - 1)
            m.then_inc(S["pre_ps"], 1)
            for g in range(7):
                free = ("z_out", g - 1) if g >= 2 else None
                if g < 3:
                    col_group(N_IN + 2 * g, g % 2, free)
                else:
                    row_group(N_IN + 2 * g, g % 2, free)
            pe.wait_ge(S["gates_done"], 1)
            c4 = bank[5]
            pe.matmul(c4[:, 0:4], cst(C_U), gl[:, 0, 4:8], start=True, stop=True)
            pe.matmul(c4[:, 4:8], cst(C_U), gl[:, 1, 4:8], start=True, stop=True)
            pe.matmul(c4[:, 8:12], cst(C_U), gl[:, 0, 0:4], start=True, stop=True)
            pe.matmul(c4[:, 12:16], cst(C_ONE), gl[:, 0, 0:4], start=True, stop=False)
            pe.matmul(c4[:, 12:16], cst(C_U), gl[:, 1, 0:4], start=False, stop=True)
            pe.matmul(c4[:, 16:20], cst(C_L), gl[:, 0, 4:8], start=True, stop=True).then_inc(S["cum_ps"], 1)
            if upto < 1:
                return
            pe.wait_ge(S["bc_done"], 1)
            pe.wait_ge(S["z_out"], 7)
            for hh in range(H0):
                b = bank[6 + hh // 2][:, (hh % 2) * TOK:(hh % 2 + 1) * TOK]
                pe.matmul(b[:, 0:P], bc8[:, hh, :], cst(C_U), start=True, stop=True)
                pe.matmul(b[:, P:TOK], bc8[:, hh, :], cst(C_ONE), start=True, stop=False)
                m = pe.matmul(b[:, P:TOK], bc8[:, H0 + hh, :], cst(C_U), start=False, stop=True)
            m.then_inc(S["cum_ps"], 1)
            for w, src in enumerate((zq, zk)):
                pe.wait_ge(S["qk_rows_done"], w + 1)
                for t in range(NT):
                    for hh in range(H0):
                        m = pe.transpose(bank[2 * w + t][:, hh * P:(hh + 1) * P],
                                         src[:, t, hh * P:(hh + 1) * P], ident)
                    m.then_inc(S["qk_tr"], 1)
            pe.wait_ge(S["qk_T"], 4)
            attention(H0, qT, kT, zv, 0)
            pe.wait_ge(S["sq_made"], 1)
            pe.wait_ge(S["o_done"], H0)
            for i in range(4):
                m = pe.matmul(bank[i][:, :], cst(C_ONE), sq8[:, 2 * i:2 * i + 2, :], start=True, stop=True)
            m.then_inc(S["norm_ps"], 1)
            pe.wait_ge(S["norm_done"], 1)
            for i in range(16):
                c, t = 4 + i // 2, i % 2
                m = pe.transpose(bank[4 + i // 4][:, (i % 4) * P:(i % 4 + 1) * P], cT[:, c, t * P:(t + 1) * P], ident)
            m.then_inc(S["kv_tr"], 1)
            pe.wait_ge(S["bc_done"], 2)
            for i in range(8):
                m = pe.matmul(bank[i // 4][:, (i % 4) * P:(i % 4 + 1) * P], bc8[:, i, :], cst(C_U),
                              start=True, stop=True)
            m.then_inc(S["gcb_ps"], 1)
            pe.wait_ge(S["bc_done"], 3)
            for i in range(8):
                m = pe.matmul(bank[2 + i // 4][:, (i % 4) * P:(i % 4 + 1) * P], bc8[:, i, :], ident,
                              start=True, stop=True)
            m.then_inc(S["gcb_ps"], 1)
            pe.wait_ge(S["kv_done"], 1)
            for i in range(8):
                t, hh = divmod(i, H0)
                k = cT[:, 4 + hh, t * P:(t + 1) * P]
                m = pe.matmul(bank[4 + i // 4][:, (i % 4) * P:(i % 4 + 1) * P], k, k, start=True, stop=True)
            m.then_inc(S["kk_ps"], 1)
            for i in range(8):
                t, hh = divmod(i, H0)
                m = pe.matmul(bank[6 + i // 4][:, (i % 4) * P:(i % 4 + 1) * P], cT[:, 4 + hh, t * P:(t + 1) * P],
                              cT[:, hh, t * P:(t + 1) * P], start=True, stop=True)
            m.then_inc(S["kk_ps"], 1)
            for lv in range(len(LEVELS)):
                n = NTl[lv % 2]
                pe.wait_ge(S["nt_done"], lv + 1)
                if lv == 0:
                    pe.wait_ge(S["AT_done"], 1)
                    for i in range(8):
                        m = pe.transpose(bank[i // 4][:, (i % 4) * P:(i % 4 + 1) * P], n[:, i, :], ident)
                    m.then_inc(S["z_ps"], 1)
                    continue
                pe.wait_ge(S["xy_done"], lv)
                for i in range(8):
                    m = pe.matmul(bank[i // 4][:, (i % 4) * P:(i % 4 + 1) * P], n[:, i, :], Xi[:, i, :],
                                  start=True, stop=True)
                m.then_inc(S["z_ps"], 1)
                pe.wait_ge(S["Zi_done"], lv)
                for i in range(8):
                    m = pe.matmul(bank[2 + i // 4][:, (i % 4) * P:(i % 4 + 1) * P], Zi[:, i, :], Yi[:, i, :],
                                  start=True, stop=True)
                if lv < len(LEVELS) - 1:
                    for i in range(8):
                        m = pe.matmul(bank[4 + i // 4][:, (i % 4) * P:(i % 4 + 1) * P], Yi[:, i, :], Zi[:, i, :],
                                      start=True, stop=True)
                m.then_inc(S["xy_ps"], 1)
            pe.wait_ge(S["xy_done"], len(LEVELS))
            for t in range(NT):
                for hh in range(H0):
                    i = t * H0 + hh
                    m = pe.matmul(bank[t][:, hh * P:(hh + 1) * P], Yi[:, i, :], bv[:, i, :],
                                  start=(t == 0 or hh == 0), stop=(t == 0), skip_group_check=True)
            m.then_inc(S["u_ps"], 1)
            for hh in range(H0):
                m = pe.matmul(bank[4][:, hh * P:(hh + 1) * P], kb1[:, hh, :], Yi[:, H0 + hh, :],
                              start=True, stop=True)
            m.then_inc(S["w_ps"], 1)
            pe.wait_ge(S["vn_done"], 1)
            for hh in range(H0):
                m = pe.matmul(bank[5][:, hh * P:(hh + 1) * P], kg0[:, hh, :], vn[:, 0, hh * P:(hh + 1) * P],
                              start=True, stop=True)
            m.then_inc(S["s_ps"], 1)
            for hh in range(H0):
                m = pe.matmul(bank[2][:, hh * P:(hh + 1) * P], AT[:, hh, :], vn[:, 0, hh * P:(hh + 1) * P],
                              start=True, stop=True)
            m.then_inc(S["o_ps"], 1)
            pe.wait_ge(S["S_done"], 1)
            pe.wait_ge(S["wT_done"], 1)
            for hh in range(H0):
                m = pe.matmul(bank[1][:, hh * P:(hh + 1) * P], wT1[:, hh, :], S1[:, hh, :],
                              start=False, stop=True, skip_group_check=True)
            m.then_inc(S["u_ps"], 1)
            for hh in range(H0):
                m = pe.matmul(bank[6][:, hh * P:(hh + 1) * P], cT[:, hh, P:TOK], S1[:, hh, :],
                              start=True, stop=True)
            m.then_inc(S["o_ps"], 1)
            pe.wait_ge(S["vn_done"], 2)
            for hh in range(H0):
                m = pe.matmul(bank[3][:, hh * P:(hh + 1) * P], AT[:, H0 + hh, :], vn[:, 1, hh * P:(hh + 1) * P],
                              start=True, stop=True)
            m.then_inc(S["o_ps"], 1)
            rows_to_T(rows_out, 1, ("og_done", 1))
            pe.wait_ge(S["xl_done"], 8)
            for g in range(2):
                row_group(N_OUT + 2 * g, g, None)
            if upto < 2:
                return
            rows_to_T(hn, 2, ("rows_done", 2))
            pe.wait_ge(S["xl_done"], 12)

            def gate_up(k, n, q):
                for w in range(2):
                    pe.wait_ge(S["lo_done"], n + w + 1)
                    for c in range(2):
                        for kc in range(KC):
                            m = passes(bank[2 * q + w][:, c * TOK:(c + 1) * TOK],
                                       split_w(k + w, kc * 256 + c * P, P), split_x(kc, 0, TOK),
                                       kc == 0, kc == KC - 1)
                    m.then_inc(S["chunk_used"], 1)

            def ffn_down(k, n, q, first, final):
                pe.wait_ge(S["lo_done"], n + 1)
                for kc in range(2):
                    for t in range(NT):
                        at = kc * TOK + t * P
                        lhs = (a_hi[:, q, at:at + P], a_lo[:, q, at:at + P])
                        for half in range(2):
                            m = passes(bank[4 + 2 * t + half][:, :], lhs,
                                       split_w(k, kc * DM + half * BLK, BLK), first and kc == 0, final and kc == 1)
                m.then_inc(S["chunk_used"], 1)

            gate_up(N_FFN, N_FFN, 0)
            gate_up(N_FFN + 2, N_FFN + 2, 1)
            pe.wait_ge(S["aT_lo"], 1)
            ffn_down(N_FFN + 4, N_FFN + 4, 0, True, False)
            with pe.Fori(0, (FS - 3) // 2) as i:
                for q in range(2):
                    k = N_FFN + 5 + 3 * q
                    pe.wait_ge(S["act_done"], 2 * i + q + 1)
                    gate_up(k, i * 6 + k, q)
                    pe.wait_ge(S["aT_lo"], 2 * i + q + 2)
                    ffn_down(k + 2, i * 6 + (k + 2), 1 - q, False, False)
            k = N_FFN + 5 + 3 * (FS - 3)
            pe.wait_ge(S["act_done"], FS - 2)
            gate_up(k, k, 0)
            pe.wait_ge(S["aT_lo"], FS - 1)
            ffn_down(k + 2, k + 2, 1, False, False)
            pe.wait_ge(S["aT_lo"], FS)
            ffn_down(k + 3, k + 3, 0, False, True)
            if upto < 3:
                return
            rows_to_T(hn, 3, ("rows_done", 3))
            pe.wait_ge(S["xl_done"], 16)
            for g in range(6):
                row_group(N_QKV + 2 * g, g % 2, ("z_out", 7 + g - 1) if g >= 2 else None)
            for w, src in enumerate((zq1, zk1)):
                pe.wait_ge(S["qk_rows_done"], w + 3)
                pe.wait_ge(S["z_out"], 13)
                for hp in range(4):
                    if w == 1:
                        pe.wait_ge(S["qk_T"], 4 + hp + 1)
                    for hh in (2 * hp, 2 * hp + 1):
                        for t in range(NT):
                            at = (hh % 2) * TOK + t * P
                            m = pe.transpose(bank[hp][:, at:at + P], src[:, t, hh * P:(hh + 1) * P], ident)
                    m.then_inc(S["qk_tr"], 1)
            pe.wait_ge(S["qk_T"], 12)
            attention(H1, qT1, kT1, zv1, H0)
            rows_to_T(rows_out1, 4, ("o_done", H0 + H1))
            pe.wait_ge(S["xl_done"], 20)
            for g in range(2):
                row_group(N_WO + 2 * g, g, None)
            if upto < 4:
                return
            rows_to_T(hn, 5, ("rows_done", 4))
            pe.wait_ge(S["xl_done"], 24)
            for t in range(NT):
                for kc in range(KC):
                    m = passes(bank[4][:, 8 * t:8 * t + 8], split_x(kc, t * P, P),
                               (wr_hi[:, kc, :], wr_lo[:, kc, :]), kc == 0, kc == KC - 1)
            m.then_inc(S["lg_ps"], 1)
            pe.wait_ge(S["route_done"], 1)
            pe.matmul(bank[5][:, 0:8], cst(C_US), lg[:, 0, :], start=True, stop=True)
            pe.matmul(bank[5][:, 8:16], cst(C_ONE), lg[:, 0, :], start=True, stop=False)
            pe.matmul(bank[5][:, 8:16], cst(C_US), lg[:, 1, :], start=False, stop=True)
            pe.matmul(bank[5][:, 16:24], cst(C_ONE), lg[:, 0, :], start=True, stop=False)
            pe.matmul(bank[5][:, 16:24], cst(C_ONE), lg[:, 1, :], start=False, stop=True).then_inc(S["rank_ps"], 1)

            def gather(done):
                pe.wait_ge(S["perm_done"], done)
                for kc in range(KC):
                    b = bank[1 + 2 * (kc // 4)][:, (kc % 4) * P:(kc % 4 + 1) * P]
                    for t in range(NT):
                        m = pe.matmul(b, hn[:, t, kc * P:(kc + 1) * P], perm[:, t, :], start=(t == 0), stop=(t == 1))
                m.then_inc(S["g_ps"], 1)

            def scatter(i, done):
                t, half = divmod(i, 2)
                pe.wait_ge(S["sc_add"], done)
                pe.matmul(bank[7][:, :], permT[:, t, :], y_sb[:, half * BLK:(half + 1) * BLK],
                          start=True, stop=True).then_inc(S["sc_ps"], 1)

            def experts(p, e):
                base = N_MOE + p * NE * PER_E
                c = [0]

                def chunk():
                    k = base + c[0]
                    c[0] += 1
                    pe.wait_ge(S["lo_done"], e * PER_E + (k + 1))
                    return k

                def steps(n):
                    return e * ES + (FS + p * NE * ES + n)

                def down(j):
                    pe.wait_ge(S["aT_lo"], steps(j + 1))
                    if j == 0:
                        pe.wait_ge(S["y_done"], e + (p * (NE + 1) + 1))
                    for part in range(2):
                        k = chunk()
                        for q in range(2):
                            at = (2 * part + q) * P
                            lhs = (a_hi[:, j % 2, at:at + P], a_lo[:, j % 2, at:at + P])
                            for half in range(2):
                                m = passes(bank[4 + half][:, :], lhs, split_w(k, q * DM + half * BLK, BLK),
                                           j == 0 and part == 0 and q == 0, j == ES - 1 and part == 1 and q == 1)
                        m.then_inc(S["chunk_used"], 1)

                for j in range(ES):
                    if j == 0:
                        pe.wait_ge(S["xl_done"], e + (p * (NE + 1) + 25))
                        pe.wait_ge(S["act_done"], steps(0))
                    elif j >= 2:
                        pe.wait_ge(S["act_done"], steps(j - 1))
                    for w in range(2):
                        for half in range(2):
                            k = chunk()
                            for kc in range(4):
                                at = (4 * half + kc) * P
                                m = passes(bank[2 * w + j % 2][:, :], (x_hi[:, at:at + P], x_lo[:, at:at + P]),
                                           split_w(k, kc * BLK, BLK),
                                           half == 0 and kc == 0, half == 1 and kc == 3)
                            m.then_inc(S["chunk_used"], 1)
                    if 1 <= j <= 4:
                        scatter(j - 1, e * 4 + (p * 4 * (NE + 1) + j))
                    if j >= 1:
                        down(j - 1)
                    pe.wait_ge(S["act_done"], steps(j + 1))
                    pe.wait_ge(S["aT_lo"], steps(j))
                    for q in range(4):
                        m = pe.transpose(bank[6][:, q * P:(q + 1) * P], act[:, j % 2, q * P:(q + 1) * P], ident)
                    m.then_inc(S["a_tr"], 1)
                    if j == 5:
                        pe.wait_ge(S["sc_add"], e * 4 + (p * 4 * (NE + 1) + 5))
                        for t in range(NT):
                            m = pe.transpose(bank[7][:, t * P:(t + 1) * P], permc[:, t, :], ident)
                        m.then_inc(S["permT_ps"], 1)
                gather(e + (p * (NE + 1) + 2))
                down(ES - 1)

            def expert_pass(p):
                gather(p * (NE + 1) + 1)
                with pe.Fori(0, NE) as e:
                    experts(p, e)
                pe.wait_ge(S["y_done"], (p + 1) * (NE + 1))
                for i in range(4):
                    scatter(i, p * 4 * (NE + 1) + 4 * NE + i + 1)

            expert_pass(0)
            pe.wait_ge(S["flag_done"], 1)
            over = pe.value_load(flag[0:1, 0:1], min_val=0, max_val=NE)
            with pe.If(over > 0):
                expert_pass(1)

        U_LAST = [3] + [4 * (j + 1) + 2 * (j - 1) - 1 for j in range(1, ES)]

        @block.scalar
        def _(act_e):
            n_step = [0]

            def link(ins):
                n_step[0] += 1
                ins.then_inc(S["act_step"], 1)
                act_e.wait_ge(S["act_step"], n_step[0])

            def split_at(k, n, uses):
                act_e.wait_ge(raw_in[k % RAW], uses)
                if not (isinstance(n, int) and n < SPL):
                    act_e.wait_ge(S["chunk_used"], n - SPL + 1)
                act_e.activation(w_hi[:, k % SPL, :], raw[:, k % RAW, :], ACT.Copy).then_inc(S["hi_done"], 1)

            def split(n):
                if n < chunk_limit:
                    split_at(n, n, 16 * (n // RAW + 1))

            def norm(r):
                if r == 0:
                    act_e.wait_ge(S["x_in"], 32)
                else:
                    act_e.wait_ge(S["h_ready"], 4 * r)
                for t in range(NT):
                    act_e.activation(hn[:, t, :], h[:, t, :], ACT.Square, accum_out=ss[:, 2 * r + t:2 * r + t + 1])\
                        .then_inc(S["sq_done"], 1)
                act_e.wait_ge(S["mean_done"], r + 1)
                act_e.activation(rstd[:, 2 * r:2 * r + 2], ss[:, 2 * r:2 * r + 2], ACT.Sqrt).then_inc(S["root_done"], 1)

            def turned(r):
                for b in range(4):
                    act_e.wait_ge(S["tr_done"], 4 * r + b + 1)
                    act_e.activation(x_hi[:, b * BLK:(b + 1) * BLK], bank[b][:, :], ACT.Copy).then_inc(S["xh_done"], 1)

            def softmax(heads, done):
                def copy_T(i):
                    act_e.wait_ge(S["p_tr"], done + i + 1)
                    if done + i >= 2:
                        act_e.wait_ge(S["pv_ready"], done + i - 1)
                    act_e.activation(att_T[:, i % 2, :], bank[2 + i % 2][:, 0:384], ACT.Copy).then_inc(S["pT_done"], 1)
                for i in range(heads):
                    act_e.wait_ge(S["sc_done"], done + i + 1)
                    act_e.activation(att_s[:, i % 2, 0:P], att_s[:, i % 2, 0:P], ACT.Exp,
                                     bias=nm[:, i % 2, 0:1], accum_out=ls[:, i % 2, 0:1])
                    act_e.activation(att_s[:, i % 2, P:3 * P], att_s[:, i % 2, P:3 * P], ACT.Exp,
                                     bias=nm[:, i % 2, 1:2], accum_out=ls[:, i % 2, 1:2]).then_inc(S["exp_done"], 1)
                    if i >= 1:
                        copy_T(i - 1)
                copy_T(heads - 1)

            def head_roots(w, n):
                act_e.wait_ge(S["hs_done"], w + 1)
                o = 16 * (w % 2)
                act_e.activation(hr[:, o:o + n], hs[:, o:o + n], ACT.Sqrt).then_inc(S["hr_root"], 1)

            norm(0)
            act_e.wait_ge(S["wsmall_in"], 48)
            act_e.activation(ws_hi[:, :, :], ws_raw[:, :, :], ACT.Copy).then_inc(S["ws_split"], 1)
            act_e.activation(wr_hi[:, :, :], wr_raw[:, :, :], ACT.Copy).then_inc(S["ws_split"], 1)
            turned(0)
            for n in range(N_IN, N_OUT + SPL):
                split(n)
                if n == 1:
                    act_e.wait_ge(S["pre_done"], 1)
                    act_e.activation(u24[:, :, :], t24[:, :, :], ACT.Exp).then_inc(S["softplus_e"], 1)
                    act_e.wait_ge(S["pre_done"], 2)
                    act_e.activation(t24[:, :, :], pre[:, :, :], ACT.Ln).then_inc(S["softplus_l"], 1)
                    act_e.wait_ge(S["small_in"], 16 * len(SMALL))
                    act_e.activation(coef[:, 4:8], smallv("al", 4), ACT.Exp).then_inc(S["softplus_l"], 1)
                c = n - SPL
                if c >= 1 and c % 2 == 1:
                    g = c // 2
                    act_e.wait_ge(S["chunk_used"], 2 * g + 2)
                    for b in range(2):
                        src = bank[2 * (g % 2) + b]
                        if g < 3:
                            m = act_e.activation(zT[:, 4 * g + 2 * b:4 * g + 2 * b + 2, 3:259],
                                                 src[:, :].rearrange("p (c t) -> p c t", c=2), ACT.Copy)
                        elif g < 6:
                            m = act_e.activation((zq, zk, zv)[g - 3][:, b, :], src[:, :], ACT.Copy)
                        else:
                            m = act_e.activation(gg[:, b, :], src[:, :], ACT.Silu)
                    m.then_inc(S["z_out"], 1)
                if c in (4, 6, 8):
                    g = c // 2 - 2
                    act_e.wait_ge(S["cT_done"], g + 1)
                    act_e.activation(cT[:, 4 * g:4 * g + 4, :], cT[:, 4 * g:4 * g + 4, :], ACT.Silu)\
                        .then_inc(S["silu_g"], 1)
                if c in (9, 11):
                    head_roots(c // 2 - 4, 8)
            if upto < 1:
                return
            act_e.wait_ge(S["cum_done"], 1)
            act_e.activation(e8[:, 0:4], cols[:, 4:8], ACT.Exp)
            act_e.activation(e8[:, 4:8], cols[:, 16:20], ACT.Exp)
            act_e.activation(beta[:, :, :], gl[:, :, 8:12], ACT.Exp).then_inc(S["beta_done"], 1)
            for w, dst in enumerate((qT, kT)):
                for t in range(NT):
                    act_e.wait_ge(S["qk_tr"], 2 * w + t + 1)
                    act_e.activation(dst[:, :, t * P:(t + 1) * P],
                                     bank[2 * w + t][:, :].rearrange("p (c t) -> p c t", c=H0), ACT.Copy)\
                        .then_inc(S["qk_T"], 1)
            softmax(H0, 0)
            act_e.wait_ge(S["zT_done"], 1)
            act_e.wait_ge(S["silu_g"], 3)
            act_e.activation(sq8[:, :, :], cT[:, 0:8, :], ACT.Square).then_inc(S["sq_made"], 1)
            act_e.wait_ge(S["norm_add"], 1)
            act_e.activation(sq8[:, :, :], sq8[:, :, :], ACT.Sqrt).then_inc(S["norm_root"], 1)
            act_e.wait_ge(S["diff_done"], 1)
            act_e.activation(DT[:, :, :], DT[:, :, :], ACT.Exp).then_inc(S["decay_done"], 1)
            for lv in range(1, len(LEVELS)):
                act_e.wait_ge(S["z_ps"], lv + 1)
                for b in range(2):
                    m = act_e.activation(Zi[:, 4 * b:4 * b + 4, :],
                                         bank[b][:, :].rearrange("p (c t) -> p c t", c=4), ACT.Copy)
                m.then_inc(S["Zi_done"], 1)
            act_e.wait_ge(S["w_ps"], 1)
            act_e.activation(wT1[:, :, :], bank[4][:, :].rearrange("p (c t) -> p c t", c=4), ACT.Copy,
                             scale=-1.0).then_inc(S["wT_done"], 1)
            act_e.wait_ge(S["s_ps"], 1)
            act_e.activation(S1[:, :, :], bank[5][:, :].rearrange("p (c t) -> p c t", c=4), ACT.Copy)\
                .then_inc(S["S_done"], 1)
            head_roots(2, 8)
            turned(1)
            for n in range(N_OUT + SPL, N_FFN + SPL):
                split(n)
            if upto < 2:
                return
            norm(1)
            turned(2)

            def ffn_post(n, q, j):
                act_e.wait_ge(S["chunk_used"], n)
                act_e.activation(sil[:, q, :], bank[2 * q][:, :], ACT.Silu).then_inc(S["act_sil"], 1)
                act_e.wait_ge(S["act_done"], j + 1)
                act_e.activation(a_hi[:, q, :], act[:, q, :], ACT.Copy).then_inc(S["aT_hi"], 1)

            with act_e.Fori(0, (FS - 1) // 2) as i:
                for q in range(2):
                    for f in (3, 4, 5):
                        k = N_FFN + 3 * q + f
                        split_at(k, i * 6 + k, i * 16 + 16 * (k // RAW + 1))
                        if f == 3:
                            ffn_post(i * 6 + (N_FFN + 2 if q == 0 else N_FFN + 4), q, i * 2 + q)
            ffn_post(N_FFN + 3 * (FS - 1) + 1, 0, FS - 1)
            for n in range(N_QKV, N_QKV + SPL):
                split(n)
            if upto < 3:
                return
            norm(2)
            turned(3)
            for n in range(N_QKV + SPL, N_WO + SPL):
                split(n)
                c = n - SPL - N_QKV
                if c % 2 == 1:
                    g = c // 2
                    act_e.wait_ge(S["chunk_used"], N_QKV + 2 * g + 2)
                    for b in range(2):
                        m = act_e.activation((zq1, zk1, zv1)[g // 2][:, b, (g % 2) * BLK:(g % 2 + 1) * BLK],
                                             bank[2 * (g % 2) + b][:, :], ACT.Copy)
                    m.then_inc(S["z_out"], 1)
                if c in (5, 9):
                    head_roots(3 + (c - 5) // 4, 16)
            for w, dst in enumerate((qT1, kT1)):
                for hp in range(4):
                    act_e.wait_ge(S["qk_tr"], 4 + 4 * w + hp + 1)
                    act_e.activation(dst[:, 2 * hp:2 * hp + 2, :],
                                     bank[hp][:, :].rearrange("p (c t) -> p c t", c=2), ACT.Copy)\
                        .then_inc(S["qk_T"], 1)
            softmax(H1, H0)
            turned(4)
            for n in range(N_WO + SPL, N_MOE):
                split(n)
            if upto < 4:
                return
            norm(3)
            turned(5)
            act_e.wait_ge(S["lg_done"], 1)
            act_e.activation(g2[:, :, 0:1], g2[:, :, 1:2], ACT.Exp).then_inc(S["g_exp"], 1)

            def gathered(n, x):
                act_e.wait_ge(S["g_ps"], n)
                for b in range(2):
                    m = act_e.activation(x_hi[:, b * BLK:(b + 1) * BLK], bank[1 + 2 * b][:, :], ACT.Copy)
                m.then_inc(S["xh_done"], 1)

            def experts(p, e):
                base = N_MOE + p * NE * PER_E

                def used(c):
                    return e * PER_E + (base + c + 1)

                def steps(n):
                    return e * ES + (FS + p * NE * ES + n)

                def turn_act(j):
                    act_e.wait_ge(S["a_tr"], e * ES + (p * NE * ES + j + 1))
                    act_e.activation(a_hi[:, j % 2, :], bank[6][:, :], ACT.Copy).then_inc(S["aT_hi"], 1)
                for c in range(PER_E):
                    k = base + c
                    split_at(k, e * PER_E + k, e * (16 * PER_E // RAW) + 16 * (k // RAW + 1))
                    if c == 2:
                        act_e.wait_ge(S["y_zero"], 1)
                        for half in range(2):
                            m = act_e.activation(y_sb[:, half * BLK:(half + 1) * BLK], bank[4 + half][:, :], ACT.Copy)
                        m.then_inc(S["y_done"], 1)
                    if c - SPL in U_LAST:
                        j = U_LAST.index(c - SPL)
                        act_e.wait_ge(S["chunk_used"], used(c - SPL))
                        act_e.activation(sil[:, j % 2, :], bank[j % 2][:, :], ACT.Silu).then_inc(S["act_sil"], 1)
                        if j == 0:
                            turn_act(0)
                    if c - SPL - 2 in U_LAST[1:]:
                        turn_act(U_LAST.index(c - SPL - 2))
                turn_act(ES - 1)
                gathered(e + (p * (NE + 1) + 2), None)

            def expert_pass(p):
                gathered(p * (NE + 1) + 1, None)
                with act_e.Fori(0, NE) as e:
                    experts(p, e)
                act_e.wait_ge(S["chunk_used"], N_MOE + (p + 1) * NE * PER_E)
                for half in range(2):
                    m = act_e.activation(y_sb[:, half * BLK:(half + 1) * BLK], bank[4 + half][:, :], ACT.Copy)
                m.then_inc(S["y_done"], 1)
            expert_pass(0)
            act_e.wait_ge(S["flag_done"], 1)
            over = act_e.value_load(flag[0:1, 0:1], min_val=0, max_val=NE)
            with act_e.If(over > 0):
                expert_pass(1)

        @block.vector
        def _(dve):
            n_step = [0]

            def link(ins):
                n_step[0] += 1
                ins.then_inc(S["dve_step"], 1)
                dve.wait_ge(S["dve_step"], n_step[0])

            def split_at(k, n):
                dve.wait_ge(S["hi_done"], n + 1)
                dve.tensor_tensor(w_lo[:, k % SPL, :], raw[:, k % RAW, :], w_hi[:, k % SPL, :].bitcast(f32),
                                  ALU.subtract).then_inc(S["lo_done"], 1)

            def split(n):
                if n < chunk_limit:
                    split_at(n, n)

            def norm(r):
                dve.wait_ge(S["sq_done"], 2 * r + 2)
                s = ss[:, 2 * r:2 * r + 2]
                rs = rstd[:, 2 * r:2 * r + 2]
                dve.tensor_scalar(s, s, 1.0 / DM, EPS, ALU.mult, ALU.add).then_inc(S["mean_done"], 1)
                dve.wait_ge(S["root_done"], r + 1)
                link(dve.reciprocal(rs, rs))
                dve.wait_ge(S["gain_in"], 16 * (r + 1))
                for t in range(NT):
                    m = dve.scalar_tensor_tensor(hn[:, t, :], h[:, t, :], rstd[:, 2 * r + t:2 * r + t + 1], gain[:, :],
                                                 ALU.mult, ALU.mult)
                m.then_inc(S["rows_done"], 1)
                dve.wait_ge(S["rows_done"], r + 1)
                dve.sem_inc(S["gain_used"], 1)

            def turned(r):
                for b in range(4):
                    dve.wait_ge(S["xh_done"], 4 * r + b + 1)
                    dve.tensor_tensor(x_lo[:, b * BLK:(b + 1) * BLK], bank[b][:, :],
                                      x_hi[:, b * BLK:(b + 1) * BLK].bitcast(f32), ALU.subtract)\
                        .then_inc(S["xl_done"], 1)

            def head_norm(w, src, sq, nh, gname):
                o = 16 * (w % 2)
                s = hs[:, o:o + NT * nh].rearrange("p (t c) -> p t c", t=NT)
                v, sq4 = (r.rearrange("p t (c d) -> p t c d", d=HD) for r in (src, sq))
                link(dve.tensor_tensor(sq, src, src, ALU.mult))
                link(dve.tensor_reduce(s, sq4, axis=AX.X, op=ALU.add))
                dve.tensor_scalar(s, s, 1.0 / HD, EPS, ALU.mult, ALU.add).then_inc(S["hs_done"], 1)
                dve.wait_ge(S["hr_root"], w + 1)
                link(dve.reciprocal(hs[:, o:o + NT * nh], hr[:, o:o + NT * nh]))
                link(dve.tensor_tensor(v, v, s.unsqueeze(3).to_broadcast([P, NT, nh, HD]), ALU.mult))
                g = smallv(gname, HD).unsqueeze(1).unsqueeze(1).to_broadcast([P, NT, nh, HD])
                return dve.tensor_tensor(v, v, g, ALU.mult)

            def softmax(heads, done, bias, out_rows):
                def weighted(i):
                    dve.wait_ge(S["exp_done"], done + i + 1)
                    link(dve.reciprocal(rl[:, i % 2, :], ls[:, i % 2, :]))
                    dve.wait_ge(S["pv_ready"], done + i + 1)
                    for t in range(NT):
                        m = dve.tensor_scalar(out_rows[:, t, i * HD:(i + 1) * HD], bank[4 + i % 2][:, t * P:(t + 1) * P],
                                              rl[:, i % 2, t:t + 1], None, ALU.mult)
                    m.then_inc(S["o_done"], 1)
                for i in range(heads):
                    dve.wait_ge(S["scores_ready"], done + i + 1)
                    if done + i >= 2:
                        dve.wait_ge(S["p_tr"], done + i - 1)
                    s = att_s[:, i % 2, :]
                    link(dve.scalar_tensor_tensor(s, bank[i % 2][:, 0:384], SCALE, bias(i), ALU.mult, ALU.add))
                    dve.reduce_max(nm[:, i % 2, 0:1], s[:, 0:P], AX.X)
                    link(dve.reduce_max(nm[:, i % 2, 1:2], s[:, P:3 * P], AX.X))
                    dve.tensor_scalar(nm[:, i % 2, :], nm[:, i % 2, :], -1.0, None, ALU.mult).then_inc(S["sc_done"], 1)
                    if i >= 1:
                        weighted(i - 1)
                weighted(heads - 1)

            def add_group(n0, g):
                dve.wait_ge(S["chunk_used"], n0 + 2 * g + 2)
                for t in range(NT):
                    v = h[:, t, g * BLK:(g + 1) * BLK]
                    dve.tensor_tensor(v, v, bank[2 * g + t][:, :], ALU.add).then_inc(S["h_ready"], 1)

            link(dve.memset(zT[:, :, 0:3], 0.0))
            link(dve.memset(coef[:, :], -1.0))
            norm(0)
            dve.wait_ge(S["ws_split"], 2)
            dve.tensor_tensor(ws_lo[:, :, :], ws_raw[:, :, :], ws_hi[:, :, :].bitcast(f32), ALU.subtract)\
                .then_inc(S["ws_split"], 1)
            dve.tensor_tensor(wr_lo[:, :, :], wr_raw[:, :, :], wr_hi[:, :, :].bitcast(f32), ALU.subtract)\
                .then_inc(S["ws_split"], 1)
            dve.wait_ge(S["cw_T"], 1)
            dve.tensor_copy(misc[:, 256:304], bank[5][:, 0:48]).then_inc(S["cw_done"], 1)
            turned(0)
            dve.wait_ge(S["small_in"], 16 * len(SMALL))
            for n in range(N_IN, N_OUT + SPL):
                split(n)
                if n == 1:
                    dve.wait_ge(S["pre_ps"], 1)
                    b4 = bank[4][:, 0:24].rearrange("p (t c) -> p t c", t=NT)
                    dve.tensor_tensor(pre[:, :, 0:4], b4[:, :, 0:4], smallv("fb", 4).unsqueeze(1).to_broadcast([P, NT, 4]),
                                      ALU.add)
                    dve.tensor_tensor(pre[:, :, 4:8], b4[:, :, 4:8], smallv("dt", 4).unsqueeze(1).to_broadcast([P, NT, 4]),
                                      ALU.add)
                    link(dve.tensor_copy(pre[:, :, 8:12], b4[:, :, 8:12]))
                    dve.tensor_scalar(pre[:, :, 0:4], pre[:, :, 0:4], -1.0, None, ALU.mult)
                    link(dve.tensor_scalar(pre[:, :, 8:12], pre[:, :, 8:12], -1.0, None, ALU.mult))
                    link(dve.tensor_scalar(u24[:, :, :], pre[:, :, :], -1.0, None, ALU.mult))
                    dve.tensor_tensor(t24[:, :, :], pre[:, :, :], u24[:, :, :], ALU.min).then_inc(S["pre_done"], 1)
                    dve.wait_ge(S["pre_done"], 1)
                    link(dve.tensor_scalar(gl[:, :, :], pre[:, :, :], 0.0, None, ALU.max))
                    dve.wait_ge(S["softplus_e"], 1)
                    dve.tensor_scalar(pre[:, :, :], u24[:, :, :], 1.0, None, ALU.add).then_inc(S["pre_done"], 1)
                    dve.wait_ge(S["pre_done"], 2)
                    link(dve.scalar_tensor_tensor(u24[:, :, :], pre[:, :, :], -1.0, u24[:, :, :], ALU.add, ALU.subtract))
                    dve.wait_ge(S["softplus_l"], 1)
                    link(dve.reciprocal(pre[:, :, :], pre[:, :, :]))
                    link(dve.tensor_tensor(u24[:, :, :], u24[:, :, :], pre[:, :, :], ALU.mult))
                    link(dve.tensor_tensor(t24[:, :, :], t24[:, :, :], u24[:, :, :], ALU.subtract))
                    link(dve.tensor_tensor(gl[:, :, :], gl[:, :, :], t24[:, :, :], ALU.add))
                    dve.wait_ge(S["softplus_l"], 2)
                    link(dve.tensor_scalar(coef[:, 4:8], coef[:, 4:8], -1.0, None, ALU.mult))
                    dve.tensor_tensor(gl[:, :, :], gl[:, :, :], coef.unsqueeze(1).to_broadcast([P, NT, 12]), ALU.mult)\
                        .then_inc(S["gates_done"], 1)
                    dve.wait_ge(S["gates_done"], 1)
                c = n - SPL
                if c in (1, 3, 5):
                    g = c // 2
                    dve.wait_ge(S["z_out"], g + 1)
                    for i in range(4 * g, 4 * g + 4):
                        m = dve.tensor_scalar(cT[:, i, :], zT[:, i, 0:TOK], cw[:, 0, i:i + 1], None, ALU.mult)
                    link(m)
                    for tap in range(1, 4):
                        for i in range(4 * g, 4 * g + 4):
                            m = dve.scalar_tensor_tensor(cT[:, i, :], zT[:, i, tap:tap + TOK], cw[:, tap, i:i + 1],
                                                         cT[:, i, :], ALU.mult, ALU.add)
                        if tap < 3:
                            link(m)
                        else:
                            m.then_inc(S["cT_done"], 1)
                if c == 7:
                    dve.wait_ge(S["z_out"], 4)
                    head_norm(0, zq, area(12324, NT, BLK), H0, "qn").then_inc(S["qk_rows_done"], 1)
                if c == 9:
                    dve.wait_ge(S["z_out"], 5)
                    dve.wait_ge(S["qk_rows_done"], 1)
                    head_norm(1, zk, area(12324, NT, BLK), H0, "kn").then_inc(S["qk_rows_done"], 1)
                if c == 11:
                    dve.wait_ge(S["cT_done"], 3)
                    dve.tensor_copy(bc8.rearrange("p (t c) n -> p t c n", t=NT),
                                    gl[:, :, 0:4].unsqueeze(3).to_broadcast([P, NT, 4, P])).then_inc(S["bc_done"], 1)
            if upto < 1:
                dve.wait_ge(S["z_out"], 7)
                dve.memset(scr, 0.0).then_inc(S["h_out"], 1)
                return
            dve.wait_ge(S["cum_ps"], 1)
            dve.tensor_copy(cols, bank[5][:, 0:20]).then_inc(S["cum_done"], 1)
            dve.wait_ge(S["cum_done"], 1)
            dve.wait_ge(S["beta_done"], 1)
            link(dve.tensor_tensor(be1, beta[:, 1, :], e8[:, 0:4], ALU.mult))
            dve.wait_ge(S["cum_ps"], 2)
            for hh in range(H0):
                b = bank[6 + hh // 2][:, (hh % 2) * TOK:(hh % 2 + 1) * TOK]
                dve.scalar_tensor_tensor(bias0[:, hh, 0:P], b[:, 0:P], cols[:, 8 + hh:9 + hh], cst(C_BIAS),
                                         ALU.subtract, ALU.subtract)
                m = dve.scalar_tensor_tensor(bias0[:, hh, P:3 * P], b, cols[:, 12 + hh:13 + hh],
                                             cst(C_BIAS + P, 2 * P), ALU.subtract, ALU.subtract)
            link(m)
            dve.tensor_scalar(bias0[:, :, :], bias0[:, :, :], -1.0, None, ALU.mult).then_inc(S["bias_done"], 1)
            dve.wait_ge(S["bias_done"], 1)
            softmax(H0, 0, lambda i: bias0[:, i, :], rows_out)
            dve.wait_ge(S["silu_g"], 3)
            dve.memset(scr, 0.0).then_inc(S["zT_done"], 1)
            dve.wait_ge(S["norm_ps"], 1)
            for i in range(4):
                m = dve.tensor_scalar(sq8[:, 2 * i:2 * i + 2, :], bank[i][:, :].rearrange("p (c t) -> p c t", c=2),
                                      EPS, None, ALU.add)
            m.then_inc(S["norm_add"], 1)
            dve.wait_ge(S["norm_root"], 1)
            link(dve.reciprocal(sq8[:, :, :], sq8[:, :, :]))
            dve.tensor_tensor(cT[:, 0:8, :], cT[:, 0:8, :], sq8[:, :, :], ALU.mult).then_inc(S["norm_done"], 1)
            dve.wait_ge(S["norm_done"], 1)
            dve.tensor_copy(bc8.rearrange("p (t c) n -> p t c n", t=NT),
                            gl[:, :, 4:8].unsqueeze(3).to_broadcast([P, NT, 4, P])).then_inc(S["bc_done"], 1)
            dve.wait_ge(S["kv_tr"], 1)

            def kv_bank(c, t):
                i = 2 * c + t
                return bank[4 + i // 4][:, (i % 4) * P:(i % 4 + 1) * P]
            for hh in range(H0):
                dve.tensor_scalar(kg0[:, hh, :], kv_bank(hh, 0), e8[:, 4 + hh:5 + hh], None, ALU.mult)
                dve.tensor_scalar(kb1[:, hh, :], kv_bank(hh, 1), be1[:, hh:hh + 1], None, ALU.mult)
                for t in range(NT):
                    m = dve.tensor_scalar(bv[:, t * H0 + hh, :], kv_bank(4 + hh, t), beta[:, t, hh:hh + 1], None,
                                          ALU.mult)
            m.then_inc(S["kv_done"], 1)
            dve.wait_ge(S["gcb_ps"], 1)
            for i in range(8):
                m = dve.tensor_scalar(DT[:, i, :], bank[i // 4][:, (i % 4) * P:(i % 4 + 1) * P],
                                      cols[:, i:i + 1], 0.0, ALU.subtract, ALU.min)
            m.then_inc(S["diff_done"], 1)
            dve.tensor_copy(bc8.rearrange("p (t c) n -> p t c n", t=NT),
                            beta.unsqueeze(3).to_broadcast([P, NT, 4, P])).then_inc(S["bc_done"], 1)
            dve.wait_ge(S["decay_done"], 1)
            link(dve.tensor_tensor(DT[:, :, :], DT[:, :, :], cst(C_U).unsqueeze(1).to_broadcast([P, 8, P]), ALU.mult))
            dve.wait_ge(S["kk_ps"], 1)
            for b in range(2):
                m = dve.tensor_tensor(MT[:, 4 * b:4 * b + 4, :], bank[4 + b][:, :].rearrange("p (c t) -> p c t", c=4),
                                      DT[:, 4 * b:4 * b + 4, :], ALU.mult)
            link(m)
            dve.wait_ge(S["gcb_ps"], 2)
            for b in range(2):
                m = dve.tensor_tensor(MT[:, 4 * b:4 * b + 4, :], MT[:, 4 * b:4 * b + 4, :],
                                      bank[2 + b][:, :].rearrange("p (c t) -> p c t", c=4), ALU.mult)
            m.then_inc(S["MT_done"], 1)
            dve.wait_ge(S["kk_ps"], 2)
            for b in range(2):
                m = dve.scalar_tensor_tensor(AT[:, 4 * b:4 * b + 4, :],
                                             bank[6 + b][:, :].rearrange("p (c t) -> p c t", c=4), SCALE,
                                             DT[:, 4 * b:4 * b + 4, :], ALU.mult, ALU.mult)
            m.then_inc(S["AT_done"], 1)
            dve.wait_ge(S["MT_done"], 1)

            def level(lv):
                if lv >= 2:
                    dve.wait_ge(S["z_ps"], lv - 1)
                mask = cst(C_LEV + lv * P).unsqueeze(1).to_broadcast([P, 8, P])
                dve.tensor_tensor(NTl[lv % 2][:, :, :], MT[:, :, :], mask, ALU.mult).then_inc(S["nt_done"], 1)
            level(0)
            level(1)
            eye = ident.unsqueeze(1)
            dve.wait_ge(S["nt_done"], 1)
            link(dve.tensor_tensor(Yi[:, :, :], eye.to_broadcast([P, 8, P]), NTl[0][:, :, :], ALU.subtract))
            dve.wait_ge(S["z_ps"], 1)
            for b in range(2):
                m = dve.tensor_tensor(Xi[:, 4 * b:4 * b + 4, :], eye.to_broadcast([P, 4, P]),
                                      bank[b][:, :].rearrange("p (c t) -> p c t", c=4), ALU.subtract)
            m.then_inc(S["xy_done"], 1)
            for lv in range(1, len(LEVELS)):
                if lv + 1 < len(LEVELS):
                    level(lv + 1)
                dve.wait_ge(S["xy_done"], lv)
                dve.wait_ge(S["xy_ps"], lv)
                last_lv = lv == len(LEVELS) - 1
                for b in range(2):
                    y = Yi[:, 4 * b:4 * b + 4, :]
                    m = dve.tensor_tensor(y, y, bank[2 + b][:, :].rearrange("p (c t) -> p c t", c=4), ALU.subtract)
                    if not last_lv:
                        x = Xi[:, 4 * b:4 * b + 4, :]
                        m = dve.tensor_tensor(x, x, bank[4 + b][:, :].rearrange("p (c t) -> p c t", c=4), ALU.subtract)
                m.then_inc(S["xy_done"], 1)
            dve.wait_ge(S["u_ps"], 1)
            dve.tensor_copy(vn[:, 0, :], bank[0][:, :]).then_inc(S["vn_done"], 1)
            dve.wait_ge(S["u_ps"], 2)
            dve.tensor_copy(vn[:, 1, :], bank[1][:, :]).then_inc(S["vn_done"], 1)
            dve.wait_ge(S["o_ps"], 1)
            od = rows_out[:, :, 512:1024]
            link(dve.tensor_copy(od[:, 0, :], bank[2][:, :]))
            dve.wait_ge(S["o_ps"], 2)
            for hh in range(H0):
                m = dve.tensor_scalar(od[:, 1, hh * P:(hh + 1) * P], bank[6][:, hh * P:(hh + 1) * P],
                                      e8[:, hh:hh + 1], SCALE, ALU.mult, ALU.mult)
            link(m)
            dve.wait_ge(S["o_ps"], 3)
            link(dve.tensor_tensor(od[:, 1, :], od[:, 1, :], bank[3][:, :], ALU.add))
            link(head_norm(2, od, area(4096, NT, BLK), H0, "on"))
            dve.tensor_tensor(od, od, gg[:, :, :], ALU.mult).then_inc(S["og_done"], 1)
            turned(1)
            for n in range(N_OUT + SPL, N_FFN + SPL):
                split(n)
                c = n - SPL - N_OUT
                if c in (1, 3):
                    add_group(N_OUT, c // 2)

            def finish(n):
                dve.wait_ge(S["h_ready"], n)
                dve.memset(scr, 0.0).then_inc(S["h_out"], 1)
            if upto < 2:
                return finish(4)
            norm(1)
            turned(2)

            def ffn_post(q, j):
                dve.wait_ge(S["act_sil"], j + 1)
                dve.tensor_tensor(act[:, q, :], sil[:, q, :], bank[2 * q + 1][:, :], ALU.mult)\
                    .then_inc(S["act_done"], 1)
                dve.wait_ge(S["aT_hi"], j + 1)
                dve.tensor_tensor(a_lo[:, q, :], act[:, q, :], a_hi[:, q, :].bitcast(f32), ALU.subtract)\
                    .then_inc(S["aT_lo"], 1)
            with dve.Fori(0, (FS - 1) // 2) as i:
                for q in range(2):
                    for f in (3, 4, 5):
                        k = N_FFN + 3 * q + f
                        split_at(k, i * 6 + k)
                        if f == 3:
                            ffn_post(q, i * 2 + q)
            ffn_post(0, FS - 1)
            for n in range(N_QKV, N_QKV + SPL):
                split(n)
            dve.wait_ge(S["chunk_used"], N_QKV)
            for t in range(NT):
                for half in range(2):
                    v = h[:, t, half * BLK:(half + 1) * BLK]
                    dve.tensor_tensor(v, v, bank[4 + 2 * t + half][:, :], ALU.add).then_inc(S["h_ready"], 1)
            if upto < 3:
                return finish(8)
            norm(2)
            turned(3)

            def rotate(src):
                v = src.rearrange("p t (c d) -> p t c d", d=HD)
                half = HD // 2
                x1, x2 = v[:, :, :, 0:half], v[:, :, :, half:HD]
                cs = cst(C_COS).rearrange("p (t d) -> p t d", t=NT).unsqueeze(2).to_broadcast([P, NT, H1, half])
                sn = cst(C_SIN).rearrange("p (t d) -> p t d", t=NT).unsqueeze(2).to_broadcast([P, NT, H1, half])
                tc = tmp1.rearrange("p t (c d) -> p t c d", d=HD)
                ts = rows_out1.rearrange("p t (c d) -> p t c d", d=HD)
                dve.tensor_tensor(tc[:, :, :, 0:half], x1, cs, ALU.mult)
                dve.tensor_tensor(tc[:, :, :, half:HD], x2, cs, ALU.mult)
                dve.tensor_tensor(ts[:, :, :, 0:half], x2, sn, ALU.mult)
                link(dve.tensor_tensor(ts[:, :, :, half:HD], x1, sn, ALU.mult))
                dve.tensor_tensor(x1, tc[:, :, :, 0:half], ts[:, :, :, 0:half], ALU.subtract)
                return dve.tensor_tensor(x2, tc[:, :, :, half:HD], ts[:, :, :, half:HD], ALU.add)
            for n in range(N_QKV + SPL, N_WO + SPL):
                split(n)
                c = n - SPL - N_QKV
                if c in (3, 7):
                    w = (c - 3) // 4
                    dve.wait_ge(S["z_out"], 7 + 2 * w + 2)
                    link(head_norm(3 + w, (zq1, zk1)[w], tmp1, H1, ("oq", "ok")[w]))
                    rotate((zq1, zk1)[w]).then_inc(S["qk_rows_done"], 1)
                    dve.wait_ge(S["qk_rows_done"], 3 + w)
            softmax(H1, H0, lambda i: cst(C_BIAS, 384), rows_out1)
            turned(4)
            for n in range(N_WO + SPL, N_MOE):
                split(n)
            for g in range(2):
                add_group(N_WO, g)
            if upto < 4:
                return finish(12)
            norm(3)
            turned(5)
            dve.wait_ge(S["lg_ps"], 1)
            link(dve.tensor_copy(lg[:, :, :], bank[4][:, 0:16].rearrange("p (t e) -> p t e", t=NT)))
            for t in range(NT):
                m = dve.max(m8[:, 8 * t:8 * t + 8], lg[:, t, :])
            link(m)
            for t in range(NT):
                dve.max_index(idx8[:, t, :], m8[:, 8 * t:8 * t + 8], lg[:, t, :])
                m = dve.tensor_tensor(g2[:, t, 1:2], m8[:, 8 * t + 1:8 * t + 2], m8[:, 8 * t:8 * t + 1], ALU.subtract)
            m.then_inc(S["lg_done"], 1)
            dve.wait_ge(S["g_exp"], 1)
            link(dve.tensor_scalar(g2[:, :, 1:2], g2[:, :, 0:1], 1.0, None, ALU.add))
            link(dve.reciprocal(g2[:, :, 2:3], g2[:, :, 1:2]))
            link(dve.tensor_tensor(g2[:, :, 3:4], g2[:, :, 0:1], g2[:, :, 2:3], ALU.mult))
            idf = t24
            link(dve.tensor_copy(idf[:, :, 0:2], idx8[:, :, 0:2]))
            link(dve.memset(rank[:, :, :], -1.0))
            link(dve.memset(comb[:, :, :], 0.0))
            for t in range(NT):
                dve.tensor_scalar(lg[:, t, :], cst(C_IO8, 8), idf[:, t, 0:1], None, ALU.is_equal)
                dve.tensor_scalar(rank[:, t, 0:8], cst(C_IO8, 8), idf[:, t, 1:2], None, ALU.is_equal)
                m = dve.tensor_scalar(comb[:, t, 0:8], cst(C_IO8, 8), idf[:, t, 0:1], g2[:, t, 2:3],
                                      ALU.is_equal, ALU.mult)
            link(m)
            for t in range(NT):
                m = dve.scalar_tensor_tensor(comb[:, t, 0:8], rank[:, t, 0:8], g2[:, t, 3:4], comb[:, t, 0:8],
                                             ALU.mult, ALU.add)
            link(m)
            dve.tensor_tensor(lg[:, :, :], lg[:, :, :], rank[:, :, 0:8], ALU.add).then_inc(S["route_done"], 1)
            dve.wait_ge(S["route_done"], 1)
            dve.wait_ge(S["rank_ps"], 1)
            link(dve.tensor_scalar(rank[:, :, 0:8], bank[5][:, 0:16].rearrange("p (t e) -> p t e", t=NT), 1.0, None,
                                   ALU.add))
            link(dve.tensor_tensor(rank[:, :, 0:8], rank[:, :, 0:8], lg[:, :, :], ALU.mult))
            link(dve.tensor_scalar(rank[:, :, 0:8], rank[:, :, 0:8], -1.0, None, ALU.add))
            link(dve.reduce_max(scr[0:1, :], bank[5][0:1, 16:24], AX.X))
            link(dve.tensor_scalar(scr[0:1, :], scr[0:1, :], float(P), None, ALU.is_gt))
            dve.tensor_copy(flag[:, :], scr[0:1, :]).then_inc(S["flag_done"], 1)
            link(dve.memset(bank[4][:, :], 0.0))
            dve.memset(bank[5][:, :], 0.0).then_inc(S["y_zero"], 1)

            def permutation(e):
                for t in range(NT):
                    dve.tensor_scalar(perm[:, t, :], cst(C_IOTA), rank[:, t, bass.ds(e, 1)], None, ALU.is_equal)
                    m = dve.tensor_scalar(permc[:, t, :], cst(C_IOTA), rank[:, t, bass.ds(e, 1)],
                                          comb[:, t, bass.ds(e, 1)], ALU.is_equal, ALU.mult)
                m.then_inc(S["perm_done"], 1)

            def gathered(n):
                dve.wait_ge(S["xh_done"], n)
                for b in range(2):
                    m = dve.tensor_tensor(x_lo[:, b * BLK:(b + 1) * BLK], bank[1 + 2 * b][:, :],
                                          x_hi[:, b * BLK:(b + 1) * BLK].bitcast(f32), ALU.subtract)
                m.then_inc(S["xl_done"], 1)

            def add_scattered(i, n):
                t, half = divmod(i, 2)
                dve.wait_ge(S["sc_ps"], n)
                v = h[:, t, half * BLK:(half + 1) * BLK]
                dve.tensor_tensor(v, v, bank[7][:, :], ALU.add).then_inc(S["sc_add"], 1)

            def experts(p, e):
                base = N_MOE + p * NE * PER_E

                def turn_act(j):
                    dve.wait_ge(S["aT_hi"], e * ES + (FS + p * NE * ES + j + 1))
                    dve.tensor_tensor(a_lo[:, j % 2, :], bank[6][:, :], a_hi[:, j % 2, :].bitcast(f32), ALU.subtract)\
                        .then_inc(S["aT_lo"], 1)
                for c in range(PER_E):
                    k = base + c
                    split_at(k, e * PER_E + k)
                    if c - SPL in U_LAST:
                        j = U_LAST.index(c - SPL)
                        dve.wait_ge(S["act_sil"], e * ES + (FS + p * NE * ES + j + 1))
                        dve.tensor_tensor(act[:, j % 2, :], sil[:, j % 2, :], bank[2 + j % 2][:, :], ALU.mult)\
                            .then_inc(S["act_done"], 1)
                        if j == 0:
                            turn_act(0)
                        if 1 <= j <= 4:
                            add_scattered(j - 1, e * 4 + (p * 4 * (NE + 1) + j))
                        if j == ES - 1:
                            dve.wait_ge(S["permT_ps"], e + (p * NE + 1))
                            permutation(e + 1)
                    if c - SPL - 2 in U_LAST[1:]:
                        j = U_LAST.index(c - SPL - 2)
                        turn_act(j)
                        if j == 5:
                            dve.wait_ge(S["permT_ps"], e + (p * NE + 1))
                            dve.tensor_copy(permT[:, :, :].rearrange("p t n -> p (t n)"), bank[7][:, 0:2 * P])\
                                .then_inc(S["permT_done"], 1)
                turn_act(ES - 1)
                gathered(e + (p * (NE + 1) + 26))

            def expert_pass(p):
                dve.memset(permT[:, :, :], 0.0).then_inc(S["sc_add" if p == 0 else "seed"], 1)
                permutation(0)
                gathered(p * (NE + 1) + 25)
                with dve.Fori(0, NE) as e:
                    experts(p, e)
                for i in range(4):
                    add_scattered(i, p * 4 * (NE + 1) + 4 * NE + i + 1)
            expert_pass(0)
            over = dve.value_load(flag[0:1, 0:1], min_val=0, max_val=NE)
            with dve.If(over > 0):
                link(dve.tensor_scalar(rank[:, :, 0:8], rank[:, :, 0:8], -float(P), None, ALU.add))
                expert_pass(1)
            dve.drain().then_inc(S["h_out"], 1)


INPUTS = ["x", "e_norm1", "e_w_in", "e_fox_f_bias", "e_fox_q_norm", "e_fox_k_norm", "e_gdn_conv", "e_gdn_a_log",
          "e_gdn_dt_bias", "e_gdn_o_norm", "e_w_out", "e_norm2", "e_ffn_w_gate_up", "e_ffn_w_down", "o_norm1",
          "o_w_qkv", "o_q_norm", "o_k_norm", "o_w_out", "o_norm2", "o_router", "o_exp_w_gate_up", "o_exp_w_down"]


LAST = "moe"


def kernel(**inputs):
    import numpy as np
    import concourse.bacc as bacc
    from concourse import mybir
    from concourse.bass_utils import run_bass_kernel_spmd

    nc = bacc.Bacc("TRN2", target_bir_lowering=False, num_devices=1,
                   dynamic_dma_scratch_size=4096)
    arrays, aps = {}, {}
    for name in INPUTS:
        v = np.ascontiguousarray(inputs[name])
        arrays[f"in_{name}_dram"] = v
        aps[name] = nc.dram_tensor(f"in_{name}_dram", v.shape, mybir.dt.from_np(v.dtype), kind="ExternalInput").ap()
    c = shape_constants()
    arrays["consts_dram"] = c
    aps["consts"] = nc.dram_tensor("consts_dram", c.shape, mybir.dt.from_np(c.dtype), kind="ExternalInput").ap()
    out = nc.dram_tensor("out_dram", (1, TOK, DM), mybir.dt.float32, kind="ExternalOutput").ap()
    build(nc, aps, out, LAST)
    r = run_bass_kernel_spmd(nc, [arrays], core_ids=[0])
    return r.results[0]["out_dram"]
```

```python
import math
from contextlib import ExitStack

import concourse.bass as bass
from concourse import mybir

P = 128
TOK = 256
NT = TOK // P
DM = 1024
KC = DM // P
HD = 128
H0 = 4
H1 = 8
FF = 2816
NE = 8
FE = 3584
EPS = 1e-6
SCALE = HD ** -0.5
BLK = 512
CH = 4 * BLK
RAW = 6
SPL = 3
NEG = -1e30

LEVELS = [1 << i for i in range(7)]
C_ID, C_U, C_L, C_US, C_ONE, C_BIAS, C_IOTA = 0, 128, 256, 384, 512, 640, 1024
C_LEV = 1152
C_COS = C_LEV + 128 * len(LEVELS)
C_SIN = C_COS + 128
C_IO8 = C_SIN + 128
NCONST = C_IO8 + 8

N_IN = 0
N_OUT = N_IN + 14
N_FFN = N_OUT + 4
N_QKV = N_FFN + 33
N_WO = N_QKV + 12
N_MOE = N_WO + 4
PER_E = 42
FS = FF // 256
ES = FE // BLK

SMALL = ["fb", "al", "dt", "qn", "kn", "on", "oq", "ok"]
SM_AT = {"fb": 0, "al": 4, "dt": 8, "qn": 16, "kn": 144, "on": 272, "oq": 400, "ok": 528}
NSMALL = 656


def shape_constants():
    import numpy as np
    c = np.zeros((P, NCONST), np.float32)
    i = np.arange(P)
    row, col = i[:, None], i[None, :]
    c[:, C_ID:C_ID + P] = row == col
    c[:, C_U:C_U + P] = row <= col
    c[:, C_L:C_L + P] = row > col
    c[:, C_US:C_US + P] = row < col
    c[:, C_ONE:C_ONE + P] = 1.0
    causal = np.where(col > row, np.float32(NEG), np.float32(0))
    c[:, C_BIAS:C_BIAS + P] = causal
    c[:, C_BIAS + 2 * P:C_BIAS + 3 * P] = causal
    c[:, C_IOTA:C_IOTA + P] = col
    for n, b in enumerate(LEVELS):
        pair = (row // (2 * b) == col // (2 * b)) & ((row // b) % 2 == 0) & ((col // b) % 2 == 1)
        c[:, C_LEV + n * P:C_LEV + (n + 1) * P] = pair
    half = HD // 2
    inv = np.power(np.float32(10000.0), -np.arange(half, dtype=np.float32) / np.float32(half))
    ang = np.arange(TOK, dtype=np.float32)[:, None] * inv[None, :]
    for t in range(NT):
        c[:, C_COS + half * t:C_COS + half * (t + 1)] = np.cos(ang[t * P:(t + 1) * P])
        c[:, C_SIN + half * t:C_SIN + half * (t + 1)] = np.sin(ang[t * P:(t + 1) * P])
    c[:, C_IO8:C_IO8 + 8] = np.arange(8)[None, :]
    return c


def build(nc, a, out, last="moe"):
    f32 = mybir.dt.float32
    f32r = mybir.dt.float32r
    u32 = mybir.dt.uint32
    i32 = mybir.dt.int32
    ALU = mybir.AluOpType
    ACT = mybir.ActivationFunctionType
    AX = mybir.AxisListType
    stages = ["in", "mix0", "ffn", "mix1", "moe"]
    upto = stages.index(last)

    ctx = ExitStack()
    with ctx:
        def sb(name, shape, dt=f32):
            return ctx.enter_context(nc.sbuf_tensor(name, shape, dt))

        raw = sb("raw", [P, RAW, CH])
        w_hi = sb("w_hi", [P, SPL, CH], f32r)
        w_lo = sb("w_lo", [P, SPL, CH], f32r)
        x_hi = sb("x_hi", [P, KC * TOK], f32r)
        x_lo = sb("x_lo", [P, KC * TOK], f32r)
        a_hi = sb("a_hi", [P, 2, BLK], f32r)
        a_lo = sb("a_lo", [P, 2, BLK], f32r)
        h = sb("h", [P, NT, DM])
        consts = sb("consts", [P, NCONST])
        small = sb("small", [P, NSMALL])
        misc = sb("misc", [P, 512])
        ws_raw = sb("ws_raw", [P, KC, 12])
        ws_hi = sb("ws_hi", [P, KC, 12], f32r)
        ws_lo = sb("ws_lo", [P, KC, 12], f32r)
        wr_raw = sb("wr_raw", [P, KC, NE])
        wr_hi = sb("wr_hi", [P, KC, NE], f32r)
        wr_lo = sb("wr_lo", [P, KC, NE], f32r)
        idx8 = sb("idx8", [P, NT, 8], u32)
        flag = sb("flag", [1, 1], i32)
        arena = sb("arena", [P, 16960])
        gain = sb("gain", [P, DM])
        bank = [ctx.enter_context(nc.psum_tensor(f"bank{i}", [P, BLK], f32)) for i in range(8)]

        xT_hi = x_hi[:, :].rearrange("p (k t) -> p k t", k=KC)
        xT_lo = x_lo[:, :].rearrange("p (k t) -> p k t", k=KC)

        def cst(at, n=P):
            return consts[:, at:at + n]

        ident = cst(C_ID)

        def smallv(name, n):
            return small[:, SM_AT[name]:SM_AT[name] + n]

        def area(at, *dims):
            n = 1
            for d in dims:
                n *= d
            v = arena[:, at:at + n]
            if len(dims) == 1:
                return v
            if len(dims) == 2:
                return v.rearrange("p (a b) -> p a b", a=dims[0])
            return v.rearrange("p (a b c) -> p a b c", a=dims[0], b=dims[1])

        gg = area(0, NT, BLK)
        zq, zk, zv = (area(1024 * (i + 1), NT, BLK) for i in range(3))
        zT = area(4096, 12, 259)
        cT = area(7204, 12, TOK)
        qT = area(10276, H0, TOK)
        kT = area(11300, H0, TOK)
        bias0 = area(12324, H0, 384)
        rows_out = area(14884, NT, DM)
        att_s = sb("att_s", [P, 2, 384])
        att_T = sb("att_T", [P, 2, 384])
        prob = [att_s[:, 0, :], att_s[:, 1, :], gain[:, 0:384]]
        sq8 = area(4096, 8, TOK)
        bc8 = area(6144, 8, P)
        Xi, Yi = (area(10276 + 1024 * i, 8, P) for i in range(2))
        Zi = area(6144, 8, P)
        DT, MT, AT = (area(1024 * (i + 1), 8, P) for i in range(3))
        bv = area(4096, 8, P)
        kg0 = area(5120, H0, P)
        kb1 = area(5632, H0, P)
        NTl = [area(12324 + 1024 * i, 8, P) for i in range(2)]
        vn = area(10276, NT, H0 * P)
        wT1 = area(12324, H0, P)
        S1 = area(12836, H0, P)
        rot = [area(14372 + 512 * i, 4, NT, HD // 2) for i in range(2)]
        sq1 = area(12324, NT, DM)
        hn = area(10276, NT, DM)
        zq1, zk1, zv1 = (area(2048 * i, NT, DM) for i in range(3))
        tmp1 = area(6144, NT, DM)
        rows_out1 = area(8192, NT, DM)
        qT1 = area(10276, H1, TOK)
        kT1 = area(12324, H1, TOK)
        sil = area(0, 2, BLK)
        act = area(1024, 2, BLK)
        y_sb = area(2048, DM)
        perm = area(3072, NT, P)
        permc = area(3328, NT, P)
        permT = area(3584, NT, P)

        ss = misc[:, 0:16].rearrange("p (r c) -> p r c", r=4)
        m8 = misc[:, 16:32]
        pre = misc[:, 32:56].rearrange("p (t c) -> p t c", t=NT)
        gl = misc[:, 56:80].rearrange("p (t c) -> p t c", t=NT)
        coef = misc[:, 80:92]
        t24 = misc[:, 92:116].rearrange("p (t c) -> p t c", t=NT)
        u24 = misc[:, 116:140].rearrange("p (t c) -> p t c", t=NT)
        cols = misc[:, 140:160]
        e8 = misc[:, 160:168]
        beta = misc[:, 168:176].rearrange("p (t c) -> p t c", t=NT)
        be1 = misc[:, 176:180]
        hs = misc[:, 180:212]
        half_neg = misc[:, 212:228]
        rstd = misc[:, 228:236]
        rqk = misc[:, 484:500]
        okq = misc[:, 236:244].rearrange("p (t c) -> p t c", t=NT)
        kgs = misc[:, 304:308]
        kbs = misc[:, 308:312]
        e1q = misc[:, 312:316]
        betar = misc[:, 316:324].rearrange("p (t c) -> p t c", t=NT)
        nm = misc[:, 244:250].rearrange("p (b t) -> p b t", b=3)
        ls = misc[:, 250:256].rearrange("p (b t) -> p b t", b=3)
        rl = misc[:, 324:330].rearrange("p (b t) -> p b t", b=3)
        cw = misc[:, 256:304].rearrange("p (k c) -> p k c", k=4)
        cwr = misc[0:48, 304:432]
        lg = misc[:, 432:448].rearrange("p (t e) -> p t e", t=NT)
        rank = misc[:, 448:466].rearrange("p (t e) -> p t e", t=NT)
        comb = misc[:, 466:484].rearrange("p (t e) -> p t e", t=NT)
        g2 = misc[:, 484:492].rearrange("p (t c) -> p t c", t=NT)
        scr = misc[:, 500:501]

        names = """consts_in x_in small_in conv_in wsmall_in wr_in gain_in dve_step act_step
            hi_done lo_done chunk_used ws_split h_ready sq_done mean_done root_done rows_done head_sq tr_done xh_done
            xl_done cw_T cw_done pre_ps pre_done softplus_e softplus_l gates_done beta_done bc_done cum_ps
            cum_done z_out zT_done cT_done sq_made norm_ps norm_add norm_root norm_done consts_done rot_done qk_rows_done qk_tr
            qk_T bias_done scores_ready sc_done exp_done p_tr pT_done pv_ready o_done hs_done hr_root
            kv_tr kv_done gcb_ps diff_done decay_done kk_ps MT_done AT_done nt_done z_ps Zi_done xy_ps xy_done
            u_ps vn_done w_ps wT_done s_ps S_done o_ps go_done silu_g og_done out_ps act_sil act_done aT_hi aT_lo down_done
            lg_ps lg_done g_exp route_done rank_ps rank_done perm_done g_ps y_zero y_done permT_ps permT_done
            sc_ps sc_add a_tr h_out flag_done out_done seed""".split()
        S = {n: ctx.enter_context(nc.semaphore(n)) for n in names}
        raw_in = [ctx.enter_context(nc.semaphore(f"raw_in{i}")) for i in range(RAW)]
        block = ctx.enter_context(nc.Block())

        chunk_limit = [N_OUT, N_FFN, N_QKV, N_MOE, 1 << 30][upto]

        IN_COL = [1540, 2052, 2564, 0, 512, 1024, 3084]

        def dense_source(n):
            def quarter(w, k, c):
                return w[k * 512:(k + 1) * 512, c:c + BLK].rearrange("(k p) n -> p k n", p=P)
            if n < N_OUT:
                return quarter(a["e_w_in"][0], n % 2, IN_COL[n // 2])
            if n < N_FFN:
                return quarter(a["e_w_out"][0], (n - N_OUT) % 2, (n - N_OUT) // 2 * BLK)
            if N_QKV <= n < N_WO:
                return quarter(a["o_w_qkv"][0], (n - N_QKV) % 2, (n - N_QKV) // 2 * BLK)
            return quarter(a["o_w_out"][0], (n - N_WO) % 2, (n - N_WO) // 2 * BLK)

        @block.sync
        def _(sp):
            def load(k, src, n):
                if k >= RAW or not isinstance(n, int):
                    sp.wait_ge(S["lo_done"], n - RAW + 1)
                sp.dma_start(raw[:, k % RAW, 0:CH].rearrange("p (k n) -> p k n", k=src.shape[1]),
                             src).then_inc(raw_in[k % RAW], 16)

            for t in range(NT):
                sp.dma_start(h[:, t, :], a["x"][0, t * P:(t + 1) * P, :]).then_inc(S["x_in"], 16)
            sp.dma_start(consts[:, :], a["consts"]).then_inc(S["consts_in"], 16)
            for n in range(N_IN, min(N_FFN, chunk_limit)):
                load(n, dense_source(n), n)
            if upto >= 2:
                wgu, wd = a["e_ffn_w_gate_up"][0], a["e_ffn_w_down"][0]

                def ffn_gu(j, up):
                    return wgu[:, bass.ds(up * FF + j * 256, 256)].rearrange("(k p) n -> p k n", p=P)

                def ffn_d(j):
                    return wd[bass.ds(j * 256, 256), :].rearrange("(k p) n -> p k n", p=P)

                load(N_FFN, ffn_gu(0, 0), N_FFN)
                load(N_FFN + 1, ffn_gu(0, 1), N_FFN + 1)
                with sp.Fori(0, (FS - 1) // 2) as i:
                    for q in range(2):
                        for c, src in enumerate((ffn_gu(2 * i + q + 1, 0), ffn_gu(2 * i + q + 1, 1),
                                                 ffn_d(2 * i + q))):
                            k = N_FFN + 2 + 3 * q + c
                            load(k, src, i * 6 + k)
                load(N_QKV - 1, ffn_d(FS - 1), N_QKV - 1)
            for n in range(N_QKV, min(N_MOE, chunk_limit)):
                load(n, dense_source(n), n)
            if upto >= 4:
                egu, ed = a["o_exp_w_gate_up"][0], a["o_exp_w_down"][0]

                def expert_loads(e, base):
                    def gu(j, up, k):
                        c = up * FE + j * BLK
                        return egu[bass.ds(e, 1), k * 512:(k + 1) * 512, c:c + BLK]\
                            .rearrange("o (k p) n -> p (o k) n", p=P)

                    def dn(j, k):
                        r = j * BLK + k * 256
                        return ed[bass.ds(e, 1), r:r + 256, :].rearrange("o (k p) n -> p (o k) n", p=P)
                    c = 0
                    for j in range(ES):
                        srcs = [gu(j, up, k) for up in range(2) for k in range(2)]
                        if j >= 1:
                            srcs += [dn(j - 1, k) for k in range(2)]
                        if j == ES - 1:
                            srcs += [dn(j, k) for k in range(2)]
                        for src in srcs:
                            load(base + c, src, e * PER_E + (base + c))
                            c += 1
                with sp.Fori(0, NE) as e:
                    expert_loads(e, N_MOE)
                sp.wait_ge(S["flag_done"], 1)
                over = sp.value_load(flag[0:1, 0:1], min_val=0, max_val=NE)
                with sp.If(over > 0):
                    with sp.Fori(0, NE) as e:
                        expert_loads(e, N_MOE + NE * PER_E)
            sp.wait_ge(S["h_out"], 1)
            for t in range(NT):
                sp.dma_start(out[0, t * P:(t + 1) * P, :], h[:, t, :]).then_inc(S["out_done"], 16)
            sp.wait_ge(S["out_done"], 16 * NT)

        @block.gpsimd
        def _(gp):
            gp.memset(half_neg, -0.5).then_inc(S["consts_done"], 1)

            def load_gain(name):
                gp.dma_start(gain[:, :], a[name][0:1, :].to_broadcast([P, DM])).then_inc(S["gain_in"], 16)

            def inverse_root(out, x, done):
                gp.tensor_tensor(out, x, half_neg[:, 0:out.shape[1]], ALU.pow).then_inc(S[done], 1)

            def norm(r):
                gp.wait_ge(S["mean_done"], r + 1)
                inverse_root(rstd[:, 2 * r:2 * r + 2], ss[:, r, 0:2], "root_done")

            def head_root(w, n):
                gp.wait_ge(S["hs_done"], w + 1)
                o = 16 * (w % 2)
                inverse_root(hs[:, o:o + n], hs[:, o:o + n], "hr_root")

            load_gain("e_norm1")
            w_in = a["e_w_in"][0].rearrange("(k p) n -> p k n", p=P)
            gp.dma_start(ws_raw[:, :, 0:4], w_in[:, :, 1536:1540]).then_inc(S["wsmall_in"], 16)
            gp.dma_start(ws_raw[:, :, 4:12], w_in[:, :, 3076:3084]).then_inc(S["wsmall_in"], 16)
            gp.wait_ge(S["consts_done"], 1)
            norm(0)
            for name, key in zip(SMALL, ["e_fox_f_bias", "e_gdn_a_log", "e_gdn_dt_bias", "e_fox_q_norm",
                                         "e_fox_k_norm", "e_gdn_o_norm", "o_q_norm", "o_k_norm"]):
                w = a[key].shape[1]
                gp.dma_start(small[:, SM_AT[name]:SM_AT[name] + w], a[key][0:1, :].to_broadcast([P, w]))\
                    .then_inc(S["small_in"], 16)
            gp.dma_start(cwr, a["e_gdn_conv"][0].rearrange("k (c p) -> (k c) p", p=P)).then_inc(S["conv_in"], 16)
            gp.dma_start(wr_raw[:, :, :], a["o_router"][0].rearrange("(k p) n -> p k n", p=P))\
                .then_inc(S["wr_in"], 16)
            head_root(0, 8)
            gp.wait_ge(S["norm_add"], 1)
            inverse_root(rqk, rqk, "norm_root")
            head_root(1, 8)
            if upto < 1:
                return
            gp.wait_ge(S["o_done"], H0)
            load_gain("e_norm2")
            head_root(2, 8)
            if upto < 2:
                return
            norm(1)
            gp.wait_ge(S["rows_done"], 4)
            if upto < 3:
                return
            load_gain("o_norm1")
            norm(2)
            head_root(3, 16)
            head_root(4, 16)
            gp.wait_ge(S["o_done"], H0 + H1)
            if upto < 4:
                return
            load_gain("o_norm2")
            norm(3)

        @block.tensor
        def _(pe):
            def rows_to_T(src, sem_name, counts):
                for t in range(NT):
                    pe.wait_ge(S[sem_name], counts[t])
                    for kc in range(KC):
                        at = (kc % 2) * TOK + t * P
                        m = pe.transpose(bank[kc // 2][:, at:at + P], src[:, t, kc * P:(kc + 1) * P], ident)
                        if t == NT - 1 and kc % 2 == 1:
                            m.then_inc(S["tr_done"], 1)

            def passes(dst, lhs, rhs, first, final):
                pe.matmul(dst, lhs[0], rhs[0], start=first, stop=False, skip_group_check=True)
                pe.matmul(dst, lhs[1], rhs[0], start=False, stop=False, skip_group_check=True)
                return pe.matmul(dst, lhs[0], rhs[1], start=False, stop=final, skip_group_check=True)

            def split_w(k, c0, n):
                s = k % SPL
                return w_hi[:, s, c0:c0 + n], w_lo[:, s, c0:c0 + n]

            def split_x(kc, t0, n):
                return xT_hi[:, kc, t0:t0 + n], xT_lo[:, kc, t0:t0 + n]

            def row_group(n0, pair, free):
                if free:
                    pe.wait_ge(S[free[0]], free[1])
                for half in range(2):
                    pe.wait_ge(S["lo_done"], n0 + half + 1)
                    for kc in range(4):
                        for t in range(NT):
                            m = passes(bank[2 * pair + t][:, :], split_x(4 * half + kc, t * P, P),
                                       split_w(n0 + half, kc * BLK, BLK),
                                       half == 0 and kc == 0, half == 1 and kc == 3)
                    m.then_inc(S["chunk_used"], 1)

            def col_group(n0, pair, free):
                if free:
                    pe.wait_ge(S[free[0]], free[1])
                for half in range(2):
                    pe.wait_ge(S["lo_done"], n0 + half + 1)
                    for kc in range(4):
                        for c in range(4):
                            m = passes(bank[2 * pair + c // 2][:, (c % 2) * TOK:(c % 2 + 1) * TOK],
                                       split_w(n0 + half, kc * BLK + c * P, P),
                                       split_x(4 * half + kc, 0, TOK),
                                       half == 0 and kc == 0 and c % 2 == 0, half == 1 and kc == 3)
                    m.then_inc(S["chunk_used"], 1)

            def attention(heads, qTt, kTt, v, done):
                def scores(i):
                    if i >= 3:
                        pe.wait_ge(S["sc_done"], done + i - 2)
                    b = bank[i % 3]
                    pe.matmul(b[:, 0:P], qTt[:, i, 0:P], kTt[:, i, 0:P], start=True, stop=True)
                    pe.matmul(b[:, P:3 * P], qTt[:, i, P:TOK], kTt[:, i, :],
                              start=True, stop=True).then_inc(S["scores_ready"], 1)

                def turn(i):
                    pe.wait_ge(S["exp_done"], done + i + 1)
                    if i >= 2:
                        pe.wait_ge(S["pT_done"], done + i - 1)
                    for b in range(3):
                        m = pe.transpose(bank[3 + i % 2][:, b * P:(b + 1) * P],
                                         prob[i % 3][:, b * P:(b + 1) * P], ident)
                    m.then_inc(S["p_tr"], 1)

                def weigh(i):
                    pe.wait_ge(S["pT_done"], done + i + 1)
                    if i >= 2:
                        pe.wait_ge(S["o_done"], done + i - 1)
                    b = bank[5 + i % 2]
                    pe.matmul(b[:, 0:P], att_T[:, i % 2, 0:P], v[:, 0, i * P:(i + 1) * P], start=True, stop=True)
                    pe.matmul(b[:, P:2 * P], att_T[:, i % 2, P:2 * P], v[:, 0, i * P:(i + 1) * P],
                              start=True, stop=False)
                    pe.matmul(b[:, P:2 * P], att_T[:, i % 2, 2 * P:3 * P], v[:, 1, i * P:(i + 1) * P],
                              start=False, stop=True).then_inc(S["pv_ready"], 1)
                scores(0)
                scores(1)
                for i in range(heads + 1):
                    if i + 2 < heads:
                        scores(i + 2)
                    if i < heads:
                        turn(i)
                    if i >= 1:
                        weigh(i - 1)

            pe.wait_ge(S["consts_in"], 16)
            rows_to_T(hn, "rows_done", (1, 2))
            pe.wait_ge(S["conv_in"], 16)
            pe.transpose(bank[6][:, 0:48], cwr, ident[0:48, 0:48]).then_inc(S["cw_T"], 1)
            pe.wait_ge(S["xl_done"], 4)
            for g in range(7):
                free = ("z_out", g - 1) if g >= 2 else None
                if g < 3:
                    col_group(N_IN + 2 * g, g % 2, free)
                else:
                    row_group(N_IN + 2 * g, g % 2, free)
                if g == 0:
                    pe.wait_ge(S["ws_split"], 2)
                    for t in range(NT):
                        for kc in range(KC):
                            m = passes(bank[4][:, 12 * t:12 * t + 12], split_x(kc, t * P, P),
                                       (ws_hi[:, kc, :], ws_lo[:, kc, :]), kc == 0, kc == KC - 1)
                    m.then_inc(S["pre_ps"], 1)
                if g == 3:
                    pe.wait_ge(S["gates_done"], 1)
                    c4 = bank[5]
                    pe.matmul(c4[:, 0:4], cst(C_U), gl[:, 0, 4:8], start=True, stop=True)
                    pe.matmul(c4[:, 4:8], cst(C_U), gl[:, 1, 4:8], start=True, stop=True)
                    pe.matmul(c4[:, 8:12], cst(C_U), gl[:, 0, 0:4], start=True, stop=True)
                    pe.matmul(c4[:, 12:16], cst(C_ONE), gl[:, 0, 0:4], start=True, stop=False)
                    pe.matmul(c4[:, 12:16], cst(C_U), gl[:, 1, 0:4], start=False, stop=True)
                    pe.matmul(c4[:, 16:20], cst(C_L), gl[:, 0, 4:8], start=True, stop=True)\
                        .then_inc(S["cum_ps"], 1)
                if g == 4:
                    pe.wait_ge(S["sq_made"], 1)
                    pe.wait_ge(S["cum_done"], 1)
                    for i in range(16):
                        c, t = divmod(i, 2)
                        m = pe.matmul(bank[5][:, 20 + i:21 + i], sq8[:, c, t * P:(t + 1) * P], cst(C_ONE, 1),
                                      start=True, stop=True)
                    m.then_inc(S["norm_ps"], 1)
                    pe.wait_ge(S["bc_done"], 1)
                    for hh in range(H0):
                        b = bank[6 + hh // 2][:, (hh % 2) * TOK:(hh % 2 + 1) * TOK]
                        pe.matmul(b[:, 0:P], bc8[:, hh, :], cst(C_U), start=True, stop=True)
                        pe.matmul(b[:, P:TOK], bc8[:, hh, :], cst(C_ONE), start=True, stop=False)
                        m = pe.matmul(b[:, P:TOK], bc8[:, H0 + hh, :], cst(C_U), start=False, stop=True)
                    m.then_inc(S["cum_ps"], 1)
            if upto < 1:
                return
            pe.wait_ge(S["norm_add"], 1)
            pe.wait_ge(S["bias_done"], 1)
            for w, src in enumerate((zq, zk)):
                pe.wait_ge(S["qk_rows_done"], w + 1)
                for t in range(NT):
                    for hh in range(H0):
                        m = pe.transpose(bank[4 + 2 * w + t][:, hh * P:(hh + 1) * P],
                                         src[:, t, hh * P:(hh + 1) * P], ident)
                    m.then_inc(S["qk_tr"], 1)
            pe.wait_ge(S["z_out"], 7)
            pe.wait_ge(S["bc_done"], 2)
            for i in range(8):
                m = pe.matmul(bank[i // 4][:, (i % 4) * P:(i % 4 + 1) * P], bc8[:, i, :], cst(C_U),
                              start=True, stop=True)
            m.then_inc(S["gcb_ps"], 1)
            pe.wait_ge(S["silu_g"], 3)
            pe.wait_ge(S["qk_T"], 2)
            for i in range(16):
                c, t = 4 + i // 2, i % 2
                m = pe.transpose(bank[2 + i // 4][:, (i % 4) * P:(i % 4 + 1) * P], cT[:, c, t * P:(t + 1) * P], ident)
            m.then_inc(S["kv_tr"], 1)
            pe.wait_ge(S["qk_T"], 4)
            pe.wait_ge(S["diff_done"], 1)
            pe.wait_ge(S["kv_done"], 1)
            attention(H0, qT, kT, zv, 0)
            pe.wait_ge(S["bc_done"], 3)
            pe.wait_ge(S["o_done"], H0)
            for i in range(8):
                t, hh = divmod(i, H0)
                k = cT[:, 4 + hh, t * P:(t + 1) * P]
                m = pe.matmul(bank[4 + i // 4][:, (i % 4) * P:(i % 4 + 1) * P], k, k, start=True, stop=True)
            m.then_inc(S["kk_ps"], 1)
            for i in range(8):
                m = pe.matmul(bank[2 + i // 4][:, (i % 4) * P:(i % 4 + 1) * P], bc8[:, i, :], ident,
                              start=True, stop=True)
            m.then_inc(S["gcb_ps"], 1)
            for i in range(8):
                t, hh = divmod(i, H0)
                m = pe.matmul(bank[6 + i // 4][:, (i % 4) * P:(i % 4 + 1) * P], cT[:, 4 + hh, t * P:(t + 1) * P],
                              cT[:, hh, t * P:(t + 1) * P], start=True, stop=True)
            m.then_inc(S["kk_ps"], 1)
            for lv in range(len(LEVELS)):
                n = NTl[lv % 2]
                pe.wait_ge(S["nt_done"], lv + 1)

                def four(dst, t, lhs, rhs):
                    for hh in range(H0):
                        i = t * H0 + hh
                        m = pe.matmul(bank[dst + t][:, hh * P:(hh + 1) * P], lhs[:, i, :], rhs[:, i, :],
                                      start=True, stop=True)
                    return m
                if lv == 0:
                    for i in range(8):
                        m = pe.transpose(bank[i // 4][:, (i % 4) * P:(i % 4 + 1) * P], n[:, i, :], ident)
                    m.then_inc(S["z_ps"], 2)
                    continue
                for t in range(NT):
                    pe.wait_ge(S["xy_done"], 2 * (lv - 1) + t + 1)
                    four(0, t, n, Xi).then_inc(S["z_ps"], 1)
                for t in range(NT):
                    pe.wait_ge(S["Zi_done"], 2 * (lv - 1) + t + 1)
                    m = four(2, t, Zi, Yi)
                    if lv < len(LEVELS) - 1:
                        m = four(4, t, Yi, Zi)
                    m.then_inc(S["xy_ps"], 1)
            pe.wait_ge(S["xy_done"], 2 * len(LEVELS))
            for t in range(NT):
                for hh in range(H0):
                    i = t * H0 + hh
                    m = pe.matmul(bank[t][:, hh * P:(hh + 1) * P], Yi[:, i, :], bv[:, i, :],
                                  start=(t == 0 or hh == 0), stop=(t == 0), skip_group_check=True)
            m.then_inc(S["u_ps"], 1)
            for hh in range(H0):
                m = pe.matmul(bank[4][:, hh * P:(hh + 1) * P], kb1[:, hh, :], Yi[:, H0 + hh, :],
                              start=True, stop=True)
            m.then_inc(S["w_ps"], 1)
            pe.wait_ge(S["vn_done"], 1)
            for hh in range(H0):
                m = pe.matmul(bank[5][:, hh * P:(hh + 1) * P], kg0[:, hh, :], vn[:, 0, hh * P:(hh + 1) * P],
                              start=True, stop=True)
            m.then_inc(S["s_ps"], 1)
            for hh in range(H0):
                m = pe.matmul(bank[2][:, hh * P:(hh + 1) * P], AT[:, hh, :], vn[:, 0, hh * P:(hh + 1) * P],
                              start=True, stop=True)
            m.then_inc(S["o_ps"], 1)
            pe.wait_ge(S["S_done"], 1)
            pe.wait_ge(S["wT_done"], 1)
            for hh in range(H0):
                m = pe.matmul(bank[1][:, hh * P:(hh + 1) * P], wT1[:, hh, :], S1[:, hh, :],
                              start=False, stop=True, skip_group_check=True)
            m.then_inc(S["u_ps"], 1)
            for hh in range(H0):
                m = pe.matmul(bank[6][:, hh * P:(hh + 1) * P], cT[:, hh, P:TOK], S1[:, hh, :],
                              start=True, stop=True)
            m.then_inc(S["o_ps"], 1)
            pe.wait_ge(S["vn_done"], 2)
            for hh in range(H0):
                m = pe.matmul(bank[3][:, hh * P:(hh + 1) * P], AT[:, H0 + hh, :], vn[:, 1, hh * P:(hh + 1) * P],
                              start=True, stop=True)
            m.then_inc(S["o_ps"], 1)
            rows_to_T(rows_out, "og_done", (1, 1))
            pe.wait_ge(S["xl_done"], 8)
            for g in range(2):
                row_group(N_OUT + 2 * g, g, None)
            if upto < 2:
                return
            rows_to_T(hn, "rows_done", (3, 4))
            pe.wait_ge(S["xl_done"], 12)

            def gate_up(k, n, q):
                for w in range(2):
                    pe.wait_ge(S["lo_done"], n + w + 1)
                    for c in range(2):
                        for kc in range(KC):
                            m = passes(bank[2 * q + w][:, c * TOK:(c + 1) * TOK],
                                       split_w(k + w, kc * 256 + c * P, P), split_x(kc, 0, TOK),
                                       kc == 0, kc == KC - 1)
                    m.then_inc(S["chunk_used"], 1)

            def ffn_down(k, n, q, first, final):
                pe.wait_ge(S["lo_done"], n + 1)
                for kc in range(2):
                    for t in range(NT):
                        at = kc * TOK + t * P
                        lhs = (a_hi[:, q, at:at + P], a_lo[:, q, at:at + P])
                        for half in range(2):
                            m = passes(bank[4 + 2 * t + half][:, :], lhs,
                                       split_w(k, kc * DM + half * BLK, BLK), first and kc == 0, final and kc == 1)
                m.then_inc(S["chunk_used"], 1)

            gate_up(N_FFN, N_FFN, 0)
            gate_up(N_FFN + 2, N_FFN + 2, 1)
            pe.wait_ge(S["aT_lo"], 1)
            ffn_down(N_FFN + 4, N_FFN + 4, 0, True, False)
            with pe.Fori(0, (FS - 3) // 2) as i:
                for q in range(2):
                    k = N_FFN + 5 + 3 * q
                    pe.wait_ge(S["act_done"], 2 * i + q + 1)
                    gate_up(k, i * 6 + k, q)
                    pe.wait_ge(S["aT_lo"], 2 * i + q + 2)
                    ffn_down(k + 2, i * 6 + (k + 2), 1 - q, False, False)
            k = N_FFN + 5 + 3 * (FS - 3)
            pe.wait_ge(S["act_done"], FS - 2)
            gate_up(k, k, 0)
            pe.wait_ge(S["aT_lo"], FS - 1)
            ffn_down(k + 2, k + 2, 1, False, False)
            pe.wait_ge(S["aT_lo"], FS)
            ffn_down(k + 3, k + 3, 0, False, True)
            if upto < 3:
                return
            rows_to_T(hn, "rows_done", (5, 6))
            pe.wait_ge(S["xl_done"], 16)
            for g in range(6):
                row_group(N_QKV + 2 * g, g % 2, ("z_out", 7 + g - 1) if g >= 2 else None)
            for w, src in enumerate((zq1, zk1)):
                pe.wait_ge(S["qk_rows_done"], w + 3)
                pe.wait_ge(S["z_out"], 13)
                for hp in range(4):
                    for hh in (2 * hp, 2 * hp + 1):
                        for t in range(NT):
                            at = (hh % 2) * TOK + t * P
                            m = pe.transpose(bank[4 * w + hp][:, at:at + P], src[:, t, hh * P:(hh + 1) * P], ident)
                    m.then_inc(S["qk_tr"], 1)
            pe.wait_ge(S["qk_T"], 12)
            attention(H1, qT1, kT1, zv1, H0)
            rows_to_T(rows_out1, "o_done", (H0 + H1, H0 + H1))
            pe.wait_ge(S["xl_done"], 20)
            for g in range(2):
                row_group(N_WO + 2 * g, g, None)
            if upto < 4:
                return
            rows_to_T(hn, "rows_done", (7, 8))
            pe.wait_ge(S["xl_done"], 24)
            for t in range(NT):
                for kc in range(KC):
                    m = passes(bank[4][:, 8 * t:8 * t + 8], split_x(kc, t * P, P),
                               (wr_hi[:, kc, :], wr_lo[:, kc, :]), kc == 0, kc == KC - 1)
            m.then_inc(S["lg_ps"], 1)
            pe.wait_ge(S["route_done"], 1)
            pe.matmul(bank[5][:, 0:8], cst(C_US), lg[:, 0, :], start=True, stop=True)
            pe.matmul(bank[5][:, 8:16], cst(C_ONE), lg[:, 0, :], start=True, stop=False)
            pe.matmul(bank[5][:, 8:16], cst(C_US), lg[:, 1, :], start=False, stop=True)
            pe.matmul(bank[5][:, 16:24], cst(C_ONE), lg[:, 0, :], start=True, stop=False)
            pe.matmul(bank[5][:, 16:24], cst(C_ONE), lg[:, 1, :], start=False, stop=True).then_inc(S["rank_ps"], 1)

            def gather(done):
                pe.wait_ge(S["perm_done"], done)
                for kc in range(KC):
                    b = bank[1 + 2 * (kc // 4)][:, (kc % 4) * P:(kc % 4 + 1) * P]
                    for t in range(NT):
                        m = pe.matmul(b, hn[:, t, kc * P:(kc + 1) * P], perm[:, t, :], start=(t == 0), stop=(t == 1))
                m.then_inc(S["g_ps"], 1)

            def scatter(i, done):
                t, half = divmod(i, 2)
                pe.wait_ge(S["sc_add"], done)
                pe.matmul(bank[7][:, :], permT[:, t, :], y_sb[:, half * BLK:(half + 1) * BLK],
                          start=True, stop=True).then_inc(S["sc_ps"], 1)

            def experts(p, e):
                base = N_MOE + p * NE * PER_E
                c = [0]

                def chunk():
                    k = base + c[0]
                    c[0] += 1
                    pe.wait_ge(S["lo_done"], e * PER_E + (k + 1))
                    return k

                def steps(n):
                    return e * ES + (FS + p * NE * ES + n)

                def down(j):
                    pe.wait_ge(S["aT_lo"], steps(j + 1))
                    if j == 0:
                        pe.wait_ge(S["y_done"], e + (p * (NE + 1) + 1))
                    for part in range(2):
                        k = chunk()
                        for q in range(2):
                            at = (2 * part + q) * P
                            lhs = (a_hi[:, j % 2, at:at + P], a_lo[:, j % 2, at:at + P])
                            for half in range(2):
                                m = passes(bank[4 + half][:, :], lhs, split_w(k, q * DM + half * BLK, BLK),
                                           j == 0 and part == 0 and q == 0, j == ES - 1 and part == 1 and q == 1)
                        m.then_inc(S["chunk_used"], 1)

                def turn_act(j):
                    pe.wait_ge(S["act_done"], steps(j + 1))
                    pe.wait_ge(S["aT_lo"], steps(j))
                    for q in range(4):
                        m = pe.transpose(bank[6][:, q * P:(q + 1) * P], act[:, j % 2, q * P:(q + 1) * P], ident)
                    m.then_inc(S["a_tr"], 1)

                for j in range(ES):
                    if j == 0:
                        pe.wait_ge(S["xl_done"], e + (p * (NE + 1) + 25))
                        pe.wait_ge(S["act_done"], steps(0))
                    elif j >= 2:
                        pe.wait_ge(S["act_done"], steps(j - 1))
                    for w in range(2):
                        for half in range(2):
                            k = chunk()
                            if w == 1 and half == 0 and j == 1:
                                turn_act(0)
                            for kc in range(4):
                                at = (4 * half + kc) * P
                                m = passes(bank[2 * w + j % 2][:, :], (x_hi[:, at:at + P], x_lo[:, at:at + P]),
                                           split_w(k, kc * BLK, BLK),
                                           half == 0 and kc == 0, half == 1 and kc == 3)
                            m.then_inc(S["chunk_used"], 1)
                    if 1 <= j <= 4:
                        scatter(j - 1, e * 4 + (p * 4 * (NE + 1) + j))
                    if j >= 1:
                        down(j - 1)
                    if j >= 1:
                        turn_act(j)
                    if j == 5:
                        pe.wait_ge(S["sc_add"], e * 4 + (p * 4 * (NE + 1) + 5))
                        for t in range(NT):
                            m = pe.transpose(bank[7][:, t * P:(t + 1) * P], permc[:, t, :], ident)
                        m.then_inc(S["permT_ps"], 1)
                gather(e + (p * (NE + 1) + 2))
                down(ES - 1)

            def expert_pass(p):
                gather(p * (NE + 1) + 1)
                with pe.Fori(0, NE) as e:
                    experts(p, e)
                pe.wait_ge(S["y_done"], (p + 1) * (NE + 1))
                for i in range(4):
                    scatter(i, p * 4 * (NE + 1) + 4 * NE + i + 1)

            expert_pass(0)
            pe.wait_ge(S["flag_done"], 1)
            over = pe.value_load(flag[0:1, 0:1], min_val=0, max_val=NE)
            with pe.If(over > 0):
                expert_pass(1)

        U_LAST = [3] + [4 * (j + 1) + 2 * (j - 1) - 1 for j in range(1, ES)]

        @block.scalar
        def _(act_e):
            n_step = [0]

            def link(ins):
                n_step[0] += 1
                ins.then_inc(S["act_step"], 1)
                act_e.wait_ge(S["act_step"], n_step[0])

            def split_at(k, n, uses):
                act_e.wait_ge(raw_in[k % RAW], uses)
                if not (isinstance(n, int) and n < SPL):
                    act_e.wait_ge(S["chunk_used"], n - SPL + 1)
                act_e.activation(w_hi[:, k % SPL, :], raw[:, k % RAW, :], ACT.Copy).then_inc(S["hi_done"], 1)

            def split(n):
                if n < chunk_limit:
                    split_at(n, n, 16 * (n // RAW + 1))

            def squares(r, half):
                for t in range(NT):
                    if r == 0:
                        act_e.wait_ge(S["x_in"], 32)
                    else:
                        act_e.wait_ge(S["h_ready"], 4 * (r - 1) + 2 * half + t + 1)
                    cs = slice(half * BLK, (half + 1) * BLK)
                    act_e.activation(hn[:, t, cs], h[:, t, cs], ACT.Square,
                                     accum_out=ss[:, r, 2 * half + t:2 * half + t + 1]).then_inc(S["sq_done"], 1)

            def turned(r):
                for b in range(4):
                    act_e.wait_ge(S["tr_done"], 4 * r + b + 1)
                    act_e.activation(x_hi[:, b * BLK:(b + 1) * BLK], bank[b][:, :], ACT.Copy).then_inc(S["xh_done"], 1)

            def softmax(heads, done):
                def copy_T(i):
                    act_e.wait_ge(S["p_tr"], done + i + 1)
                    if i >= 2:
                        act_e.wait_ge(S["pv_ready"], done + i - 1)
                    act_e.activation(att_T[:, i % 2, :], bank[3 + i % 2][:, 0:384], ACT.Copy).then_inc(S["pT_done"], 1)
                for i in range(heads):
                    s = prob[i % 3]
                    act_e.wait_ge(S["sc_done"], done + i + 1)
                    act_e.activation(s[:, 0:P], s[:, 0:P], ACT.Exp,
                                     bias=nm[:, i % 3, 0:1], accum_out=ls[:, i % 3, 0:1])
                    act_e.activation(s[:, P:3 * P], s[:, P:3 * P], ACT.Exp,
                                     bias=nm[:, i % 3, 1:2], accum_out=ls[:, i % 3, 1:2]).then_inc(S["exp_done"], 1)
                    if i >= 1:
                        copy_T(i - 1)
                copy_T(heads - 1)

            for half in range(2):
                squares(0, half)
            turned(0)
            for n in range(N_IN, N_OUT + SPL):
                split(n)
                if n == 2:
                    act_e.wait_ge(S["wsmall_in"], 32)
                    act_e.activation(ws_hi[:, :, :], ws_raw[:, :, :], ACT.Copy).then_inc(S["ws_split"], 1)
                if n == 4:
                    act_e.wait_ge(S["pre_done"], 1)
                    act_e.activation(u24[:, :, :], t24[:, :, :], ACT.Exp).then_inc(S["softplus_e"], 1)
                    act_e.wait_ge(S["pre_done"], 2)
                    act_e.activation(t24[:, :, :], pre[:, :, :], ACT.Ln).then_inc(S["softplus_l"], 1)
                    act_e.wait_ge(S["small_in"], 16 * len(SMALL))
                    act_e.activation(coef[:, 4:8], smallv("al", 4), ACT.Exp).then_inc(S["softplus_l"], 1)
                c = n - SPL
                if c >= 1 and c % 2 == 1:
                    g = c // 2
                    act_e.wait_ge(S["chunk_used"], 2 * g + 2)
                    for b in range(2):
                        src = bank[2 * (g % 2) + b]
                        if g < 3:
                            m = act_e.activation(zT[:, 4 * g + 2 * b:4 * g + 2 * b + 2, 3:259],
                                                 src[:, :].rearrange("p (c t) -> p c t", c=2), ACT.Copy)
                        elif g < 6:
                            m = act_e.activation((zq, zk, zv)[g - 3][:, b, :], src[:, :], ACT.Copy)
                        else:
                            m = act_e.activation(gg[:, b, :], src[:, :], ACT.Silu)
                    m.then_inc(S["z_out"], 1)
                if c in (3, 5, 6):
                    g = (3, 5, 6).index(c)
                    act_e.wait_ge(S["cT_done"], g + 1)
                    act_e.activation(cT[:, 4 * g:4 * g + 4, :], cT[:, 4 * g:4 * g + 4, :], ACT.Silu)\
                        .then_inc(S["silu_g"], 1)
                if c == 6:
                    act_e.wait_ge(S["silu_g"], 2)
                    act_e.activation(sq8[:, :, :], cT[:, 0:8, :], ACT.Square).then_inc(S["sq_made"], 1)
                if c == 7:
                    act_e.wait_ge(S["cum_done"], 1)
                    act_e.activation(e8[:, 0:4], cols[:, 4:8], ACT.Exp)
                    act_e.activation(e8[:, 4:8], cols[:, 16:20], ACT.Exp)
                    act_e.activation(beta[:, :, :], gl[:, :, 8:12], ACT.Exp).then_inc(S["beta_done"], 1)
                if c in (7, 9):
                    w = (c - 7) // 2
                    act_e.wait_ge(S["z_out"], 4 + w)
                    if w == 1:
                        act_e.wait_ge(S["qk_rows_done"], 1)
                    act_e.activation(area(12324, NT, BLK), (zq, zk)[w][:, :, :], ACT.Square).then_inc(S["head_sq"], 1)
                if c == 11:
                    act_e.wait_ge(S["wr_in"], 16)
                    act_e.activation(wr_hi[:, :, :], wr_raw[:, :, :], ACT.Copy).then_inc(S["ws_split"], 1)
            if upto < 1:
                return
            for w, dst in enumerate((qT, kT)):
                for t in range(NT):
                    act_e.wait_ge(S["qk_tr"], 2 * w + t + 1)
                    act_e.activation(dst[:, :, t * P:(t + 1) * P],
                                     bank[4 + 2 * w + t][:, :].rearrange("p (c t) -> p c t", c=H0), ACT.Copy)\
                        .then_inc(S["qk_T"], 1)
            act_e.wait_ge(S["kv_tr"], 1)
            act_e.wait_ge(S["norm_done"], 1)

            def kv_bank(c, t):
                i = 2 * c + t
                return bank[2 + i // 4][:, (i % 4) * P:(i % 4 + 1) * P]
            for hh in range(H0):
                act_e.activation(kg0[:, hh, :], kv_bank(hh, 0), ACT.Copy, scale=kgs[:, hh:hh + 1])
                act_e.activation(kb1[:, hh, :], kv_bank(hh, 1), ACT.Copy, scale=kbs[:, hh:hh + 1])
                for t in range(NT):
                    m = act_e.activation(bv[:, t * H0 + hh, :], kv_bank(4 + hh, t), ACT.Copy,
                                         scale=beta[:, t, hh:hh + 1])
            m.then_inc(S["kv_done"], 1)
            act_e.wait_ge(S["diff_done"], 1)
            act_e.activation(DT[:, :, :], DT[:, :, :], ACT.Exp).then_inc(S["decay_done"], 1)
            softmax(H0, 0)
            for lv in range(1, len(LEVELS)):
                for b in range(2):
                    act_e.wait_ge(S["z_ps"], 2 * lv + b + 1)
                    act_e.activation(Zi[:, 4 * b:4 * b + 4, :],
                                     bank[b][:, :].rearrange("p (c t) -> p c t", c=4), ACT.Copy)\
                        .then_inc(S["Zi_done"], 1)
            act_e.wait_ge(S["w_ps"], 1)
            act_e.activation(wT1[:, :, :], bank[4][:, :].rearrange("p (c t) -> p c t", c=4), ACT.Copy,
                             scale=-1.0).then_inc(S["wT_done"], 1)
            act_e.wait_ge(S["s_ps"], 1)
            act_e.activation(S1[:, :, :], bank[5][:, :].rearrange("p (c t) -> p c t", c=4), ACT.Copy)\
                .then_inc(S["S_done"], 1)
            turned(1)
            for n in range(N_OUT + SPL, N_FFN + SPL):
                split(n)
                if n == N_OUT + SPL + 1 and upto >= 2:
                    squares(1, 0)
            if upto < 2:
                return
            squares(1, 1)
            turned(2)

            def ffn_post(n, q, j):
                act_e.wait_ge(S["chunk_used"], n)
                act_e.activation(sil[:, q, :], bank[2 * q][:, :], ACT.Silu).then_inc(S["act_sil"], 1)
                act_e.wait_ge(S["act_done"], j + 1)
                act_e.activation(a_hi[:, q, :], act[:, q, :], ACT.Copy).then_inc(S["aT_hi"], 1)

            with act_e.Fori(0, (FS - 1) // 2) as i:
                for q in range(2):
                    for f in (3, 4, 5):
                        k = N_FFN + 3 * q + f
                        split_at(k, i * 6 + k, i * 16 + 16 * (k // RAW + 1))
                        if f == 3:
                            ffn_post(i * 6 + (N_FFN + 2 if q == 0 else N_FFN + 4), q, i * 2 + q)
            ffn_post(N_FFN + 3 * (FS - 1) + 1, 0, FS - 1)
            for n in range(N_QKV, N_QKV + SPL):
                split(n)
            if upto < 3:
                return
            squares(2, 0)
            squares(2, 1)
            turned(3)
            for n in range(N_QKV + SPL, N_WO + SPL):
                split(n)
                c = n - SPL - N_QKV
                if c % 2 == 1:
                    g = c // 2
                    act_e.wait_ge(S["chunk_used"], N_QKV + 2 * g + 2)
                    for b in range(2):
                        m = act_e.activation((zq1, zk1, zv1)[g // 2][:, b, (g % 2) * BLK:(g % 2 + 1) * BLK],
                                             bank[2 * (g % 2) + b][:, :], ACT.Copy)
                    m.then_inc(S["z_out"], 1)
                if c in (3, 7):
                    w = (c - 3) // 4
                    act_e.wait_ge(S["z_out"], 7 + 2 * w + 2)
                    if w == 1:
                        act_e.wait_ge(S["hs_done"], 4)
                    act_e.activation(sq1, (zq1, zk1)[w][:, :, :], ACT.Square).then_inc(S["head_sq"], 1)
            for w, dst in enumerate((qT1, kT1)):
                for hp in range(4):
                    act_e.wait_ge(S["qk_tr"], 4 + 4 * w + hp + 1)
                    act_e.activation(dst[:, 2 * hp:2 * hp + 2, :],
                                     bank[4 * w + hp][:, :].rearrange("p (c t) -> p c t", c=2), ACT.Copy)\
                        .then_inc(S["qk_T"], 1)
            softmax(H1, H0)
            turned(4)
            for n in range(N_WO + SPL, N_MOE):
                split(n)
            if upto < 4:
                return
            squares(3, 0)
            squares(3, 1)
            turned(5)
            act_e.wait_ge(S["lg_done"], 1)
            act_e.activation(g2[:, :, 0:1], g2[:, :, 1:2], ACT.Exp).then_inc(S["g_exp"], 1)

            def gathered(n, x):
                act_e.wait_ge(S["g_ps"], n)
                for b in range(2):
                    m = act_e.activation(x_hi[:, b * BLK:(b + 1) * BLK], bank[1 + 2 * b][:, :], ACT.Copy)
                m.then_inc(S["xh_done"], 1)

            def experts(p, e):
                base = N_MOE + p * NE * PER_E

                def used(c):
                    return e * PER_E + (base + c + 1)

                def steps(n):
                    return e * ES + (FS + p * NE * ES + n)

                def turn_act(j):
                    act_e.wait_ge(S["a_tr"], e * ES + (p * NE * ES + j + 1))
                    act_e.activation(a_hi[:, j % 2, :], bank[6][:, :], ACT.Copy).then_inc(S["aT_hi"], 1)
                for c in range(PER_E):
                    k = base + c
                    split_at(k, e * PER_E + k, e * (16 * PER_E // RAW) + 16 * (k // RAW + 1))
                    if c == 2:
                        act_e.wait_ge(S["y_zero"], 1)
                        for half in range(2):
                            m = act_e.activation(y_sb[:, half * BLK:(half + 1) * BLK], bank[4 + half][:, :], ACT.Copy)
                        m.then_inc(S["y_done"], 1)
                    if c - SPL in U_LAST:
                        j = U_LAST.index(c - SPL)
                        act_e.wait_ge(S["chunk_used"], used(c - SPL))
                        act_e.activation(sil[:, j % 2, :], bank[j % 2][:, :], ACT.Silu).then_inc(S["act_sil"], 1)
                    if c - SPL - 2 in U_LAST:
                        turn_act(U_LAST.index(c - SPL - 2))
                turn_act(ES - 1)
                gathered(e + (p * (NE + 1) + 2), None)

            def expert_pass(p):
                gathered(p * (NE + 1) + 1, None)
                with act_e.Fori(0, NE) as e:
                    experts(p, e)
                act_e.wait_ge(S["chunk_used"], N_MOE + (p + 1) * NE * PER_E)
                for half in range(2):
                    m = act_e.activation(y_sb[:, half * BLK:(half + 1) * BLK], bank[4 + half][:, :], ACT.Copy)
                m.then_inc(S["y_done"], 1)
            expert_pass(0)
            act_e.wait_ge(S["flag_done"], 1)
            over = act_e.value_load(flag[0:1, 0:1], min_val=0, max_val=NE)
            with act_e.If(over > 0):
                expert_pass(1)

        @block.vector
        def _(dve):
            n_step = [0]

            def link(ins):
                n_step[0] += 1
                ins.then_inc(S["dve_step"], 1)
                dve.wait_ge(S["dve_step"], n_step[0])

            def split_at(k, n):
                dve.wait_ge(S["hi_done"], n + 1)
                dve.tensor_tensor(w_lo[:, k % SPL, :], raw[:, k % RAW, :], w_hi[:, k % SPL, :].bitcast(f32),
                                  ALU.subtract).then_inc(S["lo_done"], 1)

            def split(n):
                if n < chunk_limit:
                    split_at(n, n)

            def norm(r):
                dve.wait_ge(S["sq_done"], 4 * r + 4)
                link(dve.tensor_tensor(ss[:, r, 0:2], ss[:, r, 0:2], ss[:, r, 2:4], ALU.add))
                dve.tensor_scalar(ss[:, r, 0:2], ss[:, r, 0:2], 1.0 / DM, EPS, ALU.mult, ALU.add)\
                    .then_inc(S["mean_done"], 1)
                dve.wait_ge(S["gain_in"], 16 * (r + 1))
                dve.wait_ge(S["root_done"], r + 1)
                for t in range(NT):
                    dve.scalar_tensor_tensor(hn[:, t, :], h[:, t, :], rstd[:, 2 * r + t:2 * r + t + 1], gain[:, :],
                                             ALU.mult, ALU.mult).then_inc(S["rows_done"], 1)

            def turned(r):
                for b in range(4):
                    dve.wait_ge(S["xh_done"], 4 * r + b + 1)
                    dve.tensor_tensor(x_lo[:, b * BLK:(b + 1) * BLK], bank[b][:, :],
                                      x_hi[:, b * BLK:(b + 1) * BLK].bitcast(f32), ALU.subtract)\
                        .then_inc(S["xl_done"], 1)

            def head_sums(w, sq, nh):
                o = 16 * (w % 2)
                s = hs[:, o:o + NT * nh].rearrange("p (t c) -> p t c", t=NT)
                link(dve.tensor_reduce(s, sq.rearrange("p t (c d) -> p t c d", d=HD), axis=AX.X, op=ALU.add))
                dve.tensor_scalar(s, s, 1.0 / HD, EPS, ALU.mult, ALU.add).then_inc(S["hs_done"], 1)

            def head_scale(w, src, nh):
                o = 16 * (w % 2)
                s = hs[:, o:o + NT * nh].rearrange("p (t c) -> p t c", t=NT)
                dve.wait_ge(S["hr_root"], w + 1)
                v = src.rearrange("p t (c d) -> p t c d", d=HD)
                link(dve.tensor_tensor(v, v, s.unsqueeze(3).to_broadcast([P, NT, nh, HD]), ALU.mult))

            def head_gain(src, nh, gname):
                v = src.rearrange("p t (c d) -> p t c d", d=HD)
                g = smallv(gname, HD).unsqueeze(1).unsqueeze(1).to_broadcast([P, NT, nh, HD])
                return dve.tensor_tensor(v, v, g, ALU.mult)

            def softmax(heads, done, bias, out_rows):
                def weighted(i):
                    dve.wait_ge(S["exp_done"], done + i + 1)
                    link(dve.reciprocal(rl[:, i % 3, :], ls[:, i % 3, :]))
                    dve.wait_ge(S["pv_ready"], done + i + 1)
                    for t in range(NT):
                        m = dve.tensor_scalar(out_rows[:, t, i * HD:(i + 1) * HD], bank[5 + i % 2][:, t * P:(t + 1) * P],
                                              rl[:, i % 3, t:t + 1], None, ALU.mult)
                    m.then_inc(S["o_done"], 1)
                for i in range(heads):
                    dve.wait_ge(S["scores_ready"], done + i + 1)
                    if i >= 3:
                        dve.wait_ge(S["p_tr"], done + i - 2)
                    s = prob[i % 3]
                    link(dve.scalar_tensor_tensor(s, bank[i % 3][:, 0:384], SCALE, bias(i), ALU.mult, ALU.add))
                    dve.reduce_max(nm[:, i % 3, 0:1], s[:, 0:P], AX.X)
                    link(dve.reduce_max(nm[:, i % 3, 1:2], s[:, P:3 * P], AX.X))
                    dve.tensor_scalar(nm[:, i % 3, :], nm[:, i % 3, :], -1.0, None, ALU.mult).then_inc(S["sc_done"], 1)
                    if i >= 2:
                        weighted(i - 2)
                weighted(heads - 2)
                weighted(heads - 1)

            def add_group(n0, g):
                dve.wait_ge(S["chunk_used"], n0 + 2 * g + 2)
                for t in range(NT):
                    v = h[:, t, g * BLK:(g + 1) * BLK]
                    dve.tensor_tensor(v, v, bank[2 * g + t][:, :], ALU.add).then_inc(S["h_ready"], 1)

            link(dve.memset(zT[:, :, 0:3], 0.0))
            link(dve.memset(coef[:, :], -1.0))
            norm(0)
            turned(0)
            for n in range(N_IN, N_OUT + SPL):
                split(n)
                if n == 0:
                    dve.wait_ge(S["cw_T"], 1)
                    dve.tensor_copy(misc[:, 256:304], bank[6][:, 0:48]).then_inc(S["cw_done"], 1)
                if n == 2:
                    dve.wait_ge(S["ws_split"], 1)
                    dve.tensor_tensor(ws_lo[:, :, :], ws_raw[:, :, :], ws_hi[:, :, :].bitcast(f32), ALU.subtract)\
                        .then_inc(S["ws_split"], 1)
                if n == 4:
                    dve.wait_ge(S["cw_done"], 1)
                    dve.wait_ge(S["small_in"], 16 * len(SMALL))
                    dve.wait_ge(S["pre_ps"], 1)
                    b4 = bank[4][:, 0:24].rearrange("p (t c) -> p t c", t=NT)
                    dve.tensor_tensor(pre[:, :, 0:4], b4[:, :, 0:4], smallv("fb", 4).unsqueeze(1).to_broadcast([P, NT, 4]),
                                      ALU.add)
                    dve.tensor_tensor(pre[:, :, 4:8], b4[:, :, 4:8], smallv("dt", 4).unsqueeze(1).to_broadcast([P, NT, 4]),
                                      ALU.add)
                    link(dve.tensor_copy(pre[:, :, 8:12], b4[:, :, 8:12]))
                    dve.tensor_scalar(pre[:, :, 0:4], pre[:, :, 0:4], -1.0, None, ALU.mult)
                    link(dve.tensor_scalar(pre[:, :, 8:12], pre[:, :, 8:12], -1.0, None, ALU.mult))
                    link(dve.tensor_scalar(u24[:, :, :], pre[:, :, :], -1.0, None, ALU.mult))
                    dve.tensor_tensor(t24[:, :, :], pre[:, :, :], u24[:, :, :], ALU.min).then_inc(S["pre_done"], 1)
                    dve.wait_ge(S["pre_done"], 1)
                    link(dve.tensor_scalar(gl[:, :, :], pre[:, :, :], 0.0, None, ALU.max))
                    dve.wait_ge(S["softplus_e"], 1)
                    dve.tensor_scalar(pre[:, :, :], u24[:, :, :], 1.0, None, ALU.add).then_inc(S["pre_done"], 1)
                    dve.wait_ge(S["pre_done"], 2)
                    link(dve.scalar_tensor_tensor(u24[:, :, :], pre[:, :, :], -1.0, u24[:, :, :], ALU.add, ALU.subtract))
                    dve.wait_ge(S["softplus_l"], 1)
                    link(dve.reciprocal(pre[:, :, :], pre[:, :, :]))
                    link(dve.tensor_tensor(u24[:, :, :], u24[:, :, :], pre[:, :, :], ALU.mult))
                    link(dve.tensor_tensor(t24[:, :, :], t24[:, :, :], u24[:, :, :], ALU.subtract))
                    link(dve.tensor_tensor(gl[:, :, :], gl[:, :, :], t24[:, :, :], ALU.add))
                    dve.wait_ge(S["softplus_l"], 2)
                    link(dve.tensor_scalar(coef[:, 4:8], coef[:, 4:8], -1.0, None, ALU.mult))
                    dve.tensor_tensor(gl[:, :, :], gl[:, :, :], coef.unsqueeze(1).to_broadcast([P, NT, 12]), ALU.mult)\
                        .then_inc(S["gates_done"], 1)
                    dve.wait_ge(S["gates_done"], 1)
                c = n - SPL
                if c in (1, 3, 5):
                    g = c // 2
                    dve.wait_ge(S["z_out"], g + 1)
                    for i in range(4 * g, 4 * g + 4):
                        m = dve.tensor_scalar(cT[:, i, :], zT[:, i, 0:TOK], cw[:, 0, i:i + 1], None, ALU.mult)
                    link(m)
                    for tap in range(1, 4):
                        for i in range(4 * g, 4 * g + 4):
                            m = dve.scalar_tensor_tensor(cT[:, i, :], zT[:, i, tap:tap + TOK], cw[:, tap, i:i + 1],
                                                         cT[:, i, :], ALU.mult, ALU.add)
                        if tap < 3:
                            link(m)
                        else:
                            m.then_inc(S["cT_done"], 1)
                if c == 6:
                    dve.wait_ge(S["cT_done"], 3)
                    dve.tensor_copy(bc8.rearrange("p (t c) n -> p t c n", t=NT),
                                    gl[:, :, 0:4].unsqueeze(3).to_broadcast([P, NT, 4, P])).then_inc(S["bc_done"], 1)
                if c == 7:
                    dve.wait_ge(S["cum_ps"], 1)
                    dve.tensor_copy(cols, bank[5][:, 0:20]).then_inc(S["cum_done"], 1)
                    dve.wait_ge(S["head_sq"], 1)
                    head_sums(0, area(12324, NT, BLK), H0)
                if c == 8:
                    head_scale(0, zq, H0)
                    head_gain(zq, H0, "qn").then_inc(S["qk_rows_done"], 1)
                if c == 9:
                    dve.wait_ge(S["norm_ps"], 1)
                    dve.tensor_scalar(rqk, bank[5][:, 20:36], EPS, None, ALU.add).then_inc(S["norm_add"], 1)
                    dve.wait_ge(S["head_sq"], 2)
                    head_sums(1, area(12324, NT, BLK), H0)
                    dve.wait_ge(S["cum_ps"], 2)
                    dve.tensor_copy(bc8.rearrange("p (t c) n -> p t c n", t=NT),
                                    gl[:, :, 4:8].unsqueeze(3).to_broadcast([P, NT, 4, P])).then_inc(S["bc_done"], 1)
                if c == 10:
                    head_scale(1, zk, H0)
                    head_gain(zk, H0, "kn").then_inc(S["qk_rows_done"], 1)
                if c == 11:
                    dve.wait_ge(S["norm_root"], 1)
                    dve.wait_ge(S["beta_done"], 1)
                    r4 = rqk.rearrange("p (w c t) -> p w t c", w=2, t=NT)
                    link(dve.tensor_tensor(be1, beta[:, 1, :], e8[:, 0:4], ALU.mult))
                    dve.tensor_tensor(kgs, e8[:, 4:8], r4[:, 1, 0, :], ALU.mult)
                    dve.tensor_tensor(kbs, be1, r4[:, 1, 1, :], ALU.mult)
                    dve.tensor_tensor(betar[:, :, :], beta[:, :, :], r4[:, 1, :, :], ALU.mult)
                    link(dve.tensor_scalar(okq[:, :, :], r4[:, 0, :, :], SCALE, None, ALU.mult))
                    dve.tensor_tensor(e1q, okq[:, 1, :], e8[:, 0:4], ALU.mult).then_inc(S["norm_done"], 1)
                if c == 12:
                    dve.wait_ge(S["cum_ps"], 2)
                    for hh in range(H0):
                        b = bank[6 + hh // 2][:, (hh % 2) * TOK:(hh % 2 + 1) * TOK]
                        dve.scalar_tensor_tensor(bias0[:, hh, 0:P], b[:, 0:P], cols[:, 8 + hh:9 + hh], cst(C_BIAS),
                                                 ALU.subtract, ALU.subtract)
                        m = dve.scalar_tensor_tensor(bias0[:, hh, P:3 * P], b, cols[:, 12 + hh:13 + hh],
                                                     cst(C_BIAS + P, 2 * P), ALU.subtract, ALU.subtract)
                    link(m)
                    dve.tensor_scalar(bias0[:, :, :], bias0[:, :, :], -1.0, None, ALU.mult).then_inc(S["bias_done"], 1)
                    dve.wait_ge(S["bias_done"], 1)
                if c == 13:
                    dve.wait_ge(S["ws_split"], 3)
                    dve.tensor_tensor(wr_lo[:, :, :], wr_raw[:, :, :], wr_hi[:, :, :].bitcast(f32), ALU.subtract)\
                        .then_inc(S["ws_split"], 1)
            if upto < 1:
                dve.wait_ge(S["z_out"], 7)
                dve.memset(scr, 0.0).then_inc(S["h_out"], 1)
                return
            dve.wait_ge(S["gcb_ps"], 1)
            for i in range(8):
                m = dve.tensor_scalar(DT[:, i, :], bank[i // 4][:, (i % 4) * P:(i % 4 + 1) * P],
                                      cols[:, i:i + 1], 0.0, ALU.subtract, ALU.min)
            m.then_inc(S["diff_done"], 1)
            dve.tensor_copy(bc8.rearrange("p (t c) n -> p t c n", t=NT),
                            betar.unsqueeze(3).to_broadcast([P, NT, 4, P])).then_inc(S["bc_done"], 1)
            softmax(H0, 0, lambda i: bias0[:, i, :], rows_out)
            dve.wait_ge(S["decay_done"], 1)
            link(dve.tensor_tensor(DT[:, :, :], DT[:, :, :], cst(C_U).unsqueeze(1).to_broadcast([P, 8, P]), ALU.mult))

            def rk(i):
                c = 2 * (4 + i % H0) + i // H0
                return rqk[:, c:c + 1]
            dve.wait_ge(S["kk_ps"], 1)
            for i in range(8):
                m = dve.scalar_tensor_tensor(MT[:, i, :], bank[4 + i // 4][:, (i % 4) * P:(i % 4 + 1) * P], rk(i),
                                             DT[:, i, :], ALU.mult, ALU.mult)
            link(m)
            dve.wait_ge(S["gcb_ps"], 2)
            for b in range(2):
                m = dve.tensor_tensor(MT[:, 4 * b:4 * b + 4, :], MT[:, 4 * b:4 * b + 4, :],
                                      bank[2 + b][:, :].rearrange("p (c t) -> p c t", c=4), ALU.mult)
            m.then_inc(S["MT_done"], 1)
            dve.wait_ge(S["MT_done"], 1)

            def level(lv):
                if lv >= 2:
                    dve.wait_ge(S["z_ps"], 2 * (lv - 1))
                mask = cst(C_LEV + lv * P).unsqueeze(1).to_broadcast([P, 8, P])
                dve.tensor_tensor(NTl[lv % 2][:, :, :], MT[:, :, :], mask, ALU.mult).then_inc(S["nt_done"], 1)
            level(0)
            level(1)
            eye = ident.unsqueeze(1)
            dve.wait_ge(S["nt_done"], 1)
            link(dve.tensor_tensor(Yi[:, :, :], eye.to_broadcast([P, 8, P]), NTl[0][:, :, :], ALU.subtract))
            dve.wait_ge(S["z_ps"], 2)
            for b in range(2):
                dve.tensor_tensor(Xi[:, 4 * b:4 * b + 4, :], eye.to_broadcast([P, 4, P]),
                                  bank[b][:, :].rearrange("p (c t) -> p c t", c=4), ALU.subtract)\
                    .then_inc(S["xy_done"], 1)
            dve.wait_ge(S["kk_ps"], 2)
            for i in range(8):
                m = dve.scalar_tensor_tensor(AT[:, i, :], bank[6 + i // 4][:, (i % 4) * P:(i % 4 + 1) * P], rk(i),
                                             DT[:, i, :], ALU.mult, ALU.mult)
            m.then_inc(S["AT_done"], 1)
            for lv in range(1, len(LEVELS)):
                if lv + 1 < len(LEVELS):
                    level(lv + 1)
                last_lv = lv == len(LEVELS) - 1
                for b in range(2):
                    dve.wait_ge(S["xy_done"], 2 * (lv - 1) + b + 1)
                    dve.wait_ge(S["xy_ps"], 2 * (lv - 1) + b + 1)
                    y = Yi[:, 4 * b:4 * b + 4, :]
                    m = dve.tensor_tensor(y, y, bank[2 + b][:, :].rearrange("p (c t) -> p c t", c=4), ALU.subtract)
                    if not last_lv:
                        x = Xi[:, 4 * b:4 * b + 4, :]
                        link(m)
                        m = dve.tensor_tensor(x, x, bank[4 + b][:, :].rearrange("p (c t) -> p c t", c=4), ALU.subtract)
                    m.then_inc(S["xy_done"], 1)
            dve.wait_ge(S["u_ps"], 1)
            dve.tensor_copy(vn[:, 0, :], bank[0][:, :]).then_inc(S["vn_done"], 1)
            dve.wait_ge(S["u_ps"], 2)
            dve.tensor_copy(vn[:, 1, :], bank[1][:, :]).then_inc(S["vn_done"], 1)
            dve.wait_ge(S["o_ps"], 1)
            od = rows_out[:, :, 512:1024]
            for hh in range(H0):
                cs = slice(hh * P, (hh + 1) * P)
                m = dve.tensor_scalar(od[:, 0, cs], bank[2][:, cs], okq[:, 0, hh:hh + 1], None, ALU.mult)
            link(m)
            dve.wait_ge(S["o_ps"], 2)
            for hh in range(H0):
                cs = slice(hh * P, (hh + 1) * P)
                m = dve.tensor_scalar(od[:, 1, cs], bank[6][:, cs], e1q[:, hh:hh + 1], None, ALU.mult)
            link(m)
            dve.wait_ge(S["o_ps"], 3)
            for hh in range(H0):
                cs = slice(hh * P, (hh + 1) * P)
                m = dve.scalar_tensor_tensor(od[:, 1, cs], bank[3][:, cs], okq[:, 1, hh:hh + 1], od[:, 1, cs],
                                             ALU.mult, ALU.add)
            link(m)
            osq = area(4096, NT, BLK)
            link(dve.tensor_tensor(osq, od, od, ALU.mult))
            head_sums(2, osq, H0)
            link(head_gain(od, H0, "on"))
            link(dve.tensor_tensor(od, od, gg[:, :, :], ALU.mult))
            head_scale(2, od, H0)
            dve.memset(scr, 0.0).then_inc(S["og_done"], 1)
            turned(1)
            for n in range(N_OUT + SPL, N_FFN + SPL):
                split(n)
                c = n - SPL - N_OUT
                if c in (1, 3):
                    add_group(N_OUT, c // 2)

            def finish(n):
                dve.wait_ge(S["h_ready"], n)
                dve.memset(scr, 0.0).then_inc(S["h_out"], 1)
            if upto < 2:
                return finish(4)
            norm(1)
            turned(2)

            def ffn_post(q, j):
                dve.wait_ge(S["act_sil"], j + 1)
                dve.tensor_tensor(act[:, q, :], sil[:, q, :], bank[2 * q + 1][:, :], ALU.mult)\
                    .then_inc(S["act_done"], 1)
                dve.wait_ge(S["aT_hi"], j + 1)
                dve.tensor_tensor(a_lo[:, q, :], act[:, q, :], a_hi[:, q, :].bitcast(f32), ALU.subtract)\
                    .then_inc(S["aT_lo"], 1)
            with dve.Fori(0, (FS - 1) // 2) as i:
                for q in range(2):
                    for f in (3, 4, 5):
                        k = N_FFN + 3 * q + f
                        split_at(k, i * 6 + k)
                        if f == 3:
                            ffn_post(q, i * 2 + q)
            ffn_post(0, FS - 1)
            for n in range(N_QKV, N_QKV + SPL):
                split(n)
            dve.wait_ge(S["chunk_used"], N_QKV)
            for half in range(2):
                for t in range(NT):
                    v = h[:, t, half * BLK:(half + 1) * BLK]
                    dve.tensor_tensor(v, v, bank[4 + 2 * t + half][:, :], ALU.add).then_inc(S["h_ready"], 1)
            if upto < 3:
                return finish(8)
            norm(2)
            turned(3)

            half = HD // 2

            def heads_halves(v):
                v = v.rearrange("p t (c d) -> p t c d", d=HD)
                return v[:, :, :, 0:half], v[:, :, :, half:HD]
            by_cos, by_sin = heads_halves(tmp1), heads_halves(rows_out1)

            def rotary_table(w, part):
                return rot[w][:, part, :, :].unsqueeze(2).to_broadcast([P, NT, H1, half])

            def rotate_products(w, part):
                x = heads_halves((zq1, zk1)[w])
                dve.tensor_tensor(by_cos[part], x[part], rotary_table(w, part), ALU.mult)
                return dve.tensor_tensor(by_sin[part], x[1 - part], rotary_table(w, 2 + 1 - part), ALU.mult)

            def rotate_sums(w):
                x = heads_halves((zq1, zk1)[w])
                dve.tensor_tensor(x[0], by_cos[0], by_sin[0], ALU.subtract)
                dve.tensor_tensor(x[1], by_cos[1], by_sin[1], ALU.add).then_inc(S["qk_rows_done"], 1)
                dve.wait_ge(S["qk_rows_done"], 3 + w)

            for w, gname in enumerate(("oq", "ok")):
                for part in range(4):
                    g = smallv(gname, HD)[:, (part % 2) * half:(part % 2 + 1) * half].unsqueeze(1)\
                        .to_broadcast([P, NT, half])
                    m = dve.tensor_tensor(rot[w][:, part, :, :], cst(C_COS if part < 2 else C_SIN)
                                          .rearrange("p (t d) -> p t d", t=NT), g, ALU.mult)
            m.then_inc(S["rot_done"], 1)
            dve.wait_ge(S["rot_done"], 1)
            for n in range(N_QKV + SPL, N_WO + SPL):
                split(n)
                c = n - SPL - N_QKV
                w = 0 if c < 8 else 1
                if c in (3, 7):
                    dve.wait_ge(S["z_out"], 7 + 2 * (c // 4) + 2)
                if c in (4, 8):
                    if w == 1:
                        rotate_sums(0)
                    dve.wait_ge(S["head_sq"], 3 + w)
                    head_sums(3 + w, sq1, H1)
                if c in (5, 9):
                    head_scale(3 + w, (zq1, zk1)[w], H1)
                if c in (6, 10):
                    link(rotate_products(w, 0))
                if c in (7, 11):
                    link(rotate_products(w, 1))
            rotate_sums(1)
            softmax(H1, H0, lambda i: cst(C_BIAS, 384), rows_out1)
            turned(4)
            for n in range(N_WO + SPL, N_MOE):
                split(n)
            for g in range(2):
                add_group(N_WO, g)
            if upto < 4:
                return finish(12)
            norm(3)
            turned(5)
            dve.wait_ge(S["lg_ps"], 1)
            link(dve.tensor_copy(lg[:, :, :], bank[4][:, 0:16].rearrange("p (t e) -> p t e", t=NT)))
            for t in range(NT):
                m = dve.max(m8[:, 8 * t:8 * t + 8], lg[:, t, :])
            link(m)
            for t in range(NT):
                dve.max_index(idx8[:, t, :], m8[:, 8 * t:8 * t + 8], lg[:, t, :])
                m = dve.tensor_tensor(g2[:, t, 1:2], m8[:, 8 * t + 1:8 * t + 2], m8[:, 8 * t:8 * t + 1], ALU.subtract)
            m.then_inc(S["lg_done"], 1)
            dve.wait_ge(S["g_exp"], 1)
            link(dve.tensor_scalar(g2[:, :, 1:2], g2[:, :, 0:1], 1.0, None, ALU.add))
            link(dve.reciprocal(g2[:, :, 2:3], g2[:, :, 1:2]))
            link(dve.tensor_tensor(g2[:, :, 3:4], g2[:, :, 0:1], g2[:, :, 2:3], ALU.mult))
            idf = t24
            link(dve.tensor_copy(idf[:, :, 0:2], idx8[:, :, 0:2]))
            link(dve.memset(rank[:, :, :], -1.0))
            link(dve.memset(comb[:, :, :], 0.0))
            for t in range(NT):
                dve.tensor_scalar(lg[:, t, :], cst(C_IO8, 8), idf[:, t, 0:1], None, ALU.is_equal)
                dve.tensor_scalar(rank[:, t, 0:8], cst(C_IO8, 8), idf[:, t, 1:2], None, ALU.is_equal)
                m = dve.tensor_scalar(comb[:, t, 0:8], cst(C_IO8, 8), idf[:, t, 0:1], g2[:, t, 2:3],
                                      ALU.is_equal, ALU.mult)
            link(m)
            for t in range(NT):
                m = dve.scalar_tensor_tensor(comb[:, t, 0:8], rank[:, t, 0:8], g2[:, t, 3:4], comb[:, t, 0:8],
                                             ALU.mult, ALU.add)
            link(m)
            dve.tensor_tensor(lg[:, :, :], lg[:, :, :], rank[:, :, 0:8], ALU.add).then_inc(S["route_done"], 1)
            dve.wait_ge(S["route_done"], 1)
            dve.wait_ge(S["rank_ps"], 1)
            link(dve.tensor_scalar(rank[:, :, 0:8], bank[5][:, 0:16].rearrange("p (t e) -> p t e", t=NT), 1.0, None,
                                   ALU.add))
            link(dve.tensor_tensor(rank[:, :, 0:8], rank[:, :, 0:8], lg[:, :, :], ALU.mult))
            link(dve.tensor_scalar(rank[:, :, 0:8], rank[:, :, 0:8], -1.0, None, ALU.add))
            link(dve.reduce_max(scr[0:1, :], bank[5][0:1, 16:24], AX.X))
            link(dve.tensor_scalar(scr[0:1, :], scr[0:1, :], float(P), None, ALU.is_gt))
            dve.tensor_copy(flag[:, :], scr[0:1, :]).then_inc(S["flag_done"], 1)
            link(dve.memset(bank[4][:, :], 0.0))
            dve.memset(bank[5][:, :], 0.0).then_inc(S["y_zero"], 1)

            def permutation(e):
                for t in range(NT):
                    dve.tensor_scalar(perm[:, t, :], cst(C_IOTA), rank[:, t, bass.ds(e, 1)], None, ALU.is_equal)
                    m = dve.tensor_scalar(permc[:, t, :], cst(C_IOTA), rank[:, t, bass.ds(e, 1)],
                                          comb[:, t, bass.ds(e, 1)], ALU.is_equal, ALU.mult)
                m.then_inc(S["perm_done"], 1)

            def gathered(n):
                dve.wait_ge(S["xh_done"], n)
                for b in range(2):
                    m = dve.tensor_tensor(x_lo[:, b * BLK:(b + 1) * BLK], bank[1 + 2 * b][:, :],
                                          x_hi[:, b * BLK:(b + 1) * BLK].bitcast(f32), ALU.subtract)
                m.then_inc(S["xl_done"], 1)

            def add_scattered(i, n):
                t, half = divmod(i, 2)
                dve.wait_ge(S["sc_ps"], n)
                v = h[:, t, half * BLK:(half + 1) * BLK]
                dve.tensor_tensor(v, v, bank[7][:, :], ALU.add).then_inc(S["sc_add"], 1)

            def experts(p, e):
                base = N_MOE + p * NE * PER_E

                def turn_act(j):
                    dve.wait_ge(S["aT_hi"], e * ES + (FS + p * NE * ES + j + 1))
                    dve.tensor_tensor(a_lo[:, j % 2, :], bank[6][:, :], a_hi[:, j % 2, :].bitcast(f32), ALU.subtract)\
                        .then_inc(S["aT_lo"], 1)
                for c in range(PER_E):
                    k = base + c
                    split_at(k, e * PER_E + k)
                    if c - SPL in U_LAST:
                        j = U_LAST.index(c - SPL)
                        dve.wait_ge(S["act_sil"], e * ES + (FS + p * NE * ES + j + 1))
                        dve.tensor_tensor(act[:, j % 2, :], sil[:, j % 2, :], bank[2 + j % 2][:, :], ALU.mult)\
                            .then_inc(S["act_done"], 1)
                        if 1 <= j <= 4:
                            add_scattered(j - 1, e * 4 + (p * 4 * (NE + 1) + j))
                        if j == ES - 1:
                            dve.wait_ge(S["permT_ps"], e + (p * NE + 1))
                            permutation(e + 1)
                    if c - SPL - 2 in U_LAST:
                        j = U_LAST.index(c - SPL - 2)
                        turn_act(j)
                        if j == 5:
                            dve.wait_ge(S["permT_ps"], e + (p * NE + 1))
                            dve.tensor_copy(permT[:, :, :].rearrange("p t n -> p (t n)"), bank[7][:, 0:2 * P])\
                                .then_inc(S["permT_done"], 1)
                turn_act(ES - 1)
                gathered(e + (p * (NE + 1) + 26))

            def expert_pass(p):
                dve.memset(permT[:, :, :], 0.0).then_inc(S["sc_add" if p == 0 else "seed"], 1)
                permutation(0)
                gathered(p * (NE + 1) + 25)
                with dve.Fori(0, NE) as e:
                    experts(p, e)
                for i in range(4):
                    add_scattered(i, p * 4 * (NE + 1) + 4 * NE + i + 1)
            expert_pass(0)
            over = dve.value_load(flag[0:1, 0:1], min_val=0, max_val=NE)
            with dve.If(over > 0):
                link(dve.tensor_scalar(rank[:, :, 0:8], rank[:, :, 0:8], -float(P), None, ALU.add))
                expert_pass(1)
            dve.drain().then_inc(S["h_out"], 1)


INPUTS = ["x", "e_norm1", "e_w_in", "e_fox_f_bias", "e_fox_q_norm", "e_fox_k_norm", "e_gdn_conv", "e_gdn_a_log",
          "e_gdn_dt_bias", "e_gdn_o_norm", "e_w_out", "e_norm2", "e_ffn_w_gate_up", "e_ffn_w_down", "o_norm1",
          "o_w_qkv", "o_q_norm", "o_k_norm", "o_w_out", "o_norm2", "o_router", "o_exp_w_gate_up", "o_exp_w_down"]


LAST = "moe"


def kernel(**inputs):
    import numpy as np
    import concourse.bacc as bacc
    from concourse import mybir
    from concourse.bass_utils import run_bass_kernel_spmd

    nc = bacc.Bacc("TRN2", target_bir_lowering=False, num_devices=1,
                   dynamic_dma_scratch_size=4096)
    arrays, aps = {}, {}
    for name in INPUTS:
        v = np.ascontiguousarray(inputs[name])
        arrays[f"in_{name}_dram"] = v
        aps[name] = nc.dram_tensor(f"in_{name}_dram", v.shape, mybir.dt.from_np(v.dtype), kind="ExternalInput").ap()
    c = shape_constants()
    arrays["consts_dram"] = c
    aps["consts"] = nc.dram_tensor("consts_dram", c.shape, mybir.dt.from_np(c.dtype), kind="ExternalInput").ap()
    out = nc.dram_tensor("out_dram", (1, TOK, DM), mybir.dt.float32, kind="ExternalOutput").ap()
    build(nc, aps, out, LAST)
    r = run_bass_kernel_spmd(nc, [arrays], core_ids=[0])
    return r.results[0]["out_dram"]
```

```python
import math
from contextlib import ExitStack

import concourse.bass as bass
from concourse import mybir

P = 128
TOK = 256
NT = TOK // P
DM = 1024
KC = DM // P
HD = 128
H0 = 4
H1 = 8
FF = 2816
NE = 8
FE = 3584
EPS = 1e-6
SCALE = HD ** -0.5
BLK = 512
CH = 4 * BLK
RAW = 6
SPL = 3
NEG = -1e30

LEVELS = [1 << i for i in range(7)]
C_ID, C_U, C_L, C_US, C_ONE, C_BIAS, C_IOTA = 0, 128, 256, 384, 512, 640, 1024
C_LEV = 1152
C_COS = C_LEV + 128 * len(LEVELS)
C_SIN = C_COS + 128
C_IO8 = C_SIN + 128
NCONST = C_IO8 + 8

N_IN = 0
N_OUT = N_IN + 14
N_FFN = N_OUT + 4
N_QKV = N_FFN + 33
N_WO = N_QKV + 12
N_MOE = N_WO + 4
PER_E = 42
FS = FF // 256
ES = FE // BLK

SMALL = ["fb", "al", "dt", "on", "oq", "ok"]
SM_AT = {"fb": 0, "al": 4, "dt": 8, "on": 16, "oq": 144, "ok": 272}
NSMALL = 400


def shape_constants():
    import numpy as np
    c = np.zeros((P, NCONST), np.float32)
    i = np.arange(P)
    row, col = i[:, None], i[None, :]
    c[:, C_ID:C_ID + P] = row == col
    c[:, C_U:C_U + P] = row <= col
    c[:, C_L:C_L + P] = row > col
    c[:, C_US:C_US + P] = row < col
    c[:, C_ONE:C_ONE + P] = 1.0
    causal = np.where(col > row, np.float32(NEG), np.float32(0))
    c[:, C_BIAS:C_BIAS + P] = causal
    c[:, C_BIAS + 2 * P:C_BIAS + 3 * P] = causal
    c[:, C_IOTA:C_IOTA + P] = col
    for n, b in enumerate(LEVELS):
        pair = (row // (2 * b) == col // (2 * b)) & ((row // b) % 2 == 0) & ((col // b) % 2 == 1)
        c[:, C_LEV + n * P:C_LEV + (n + 1) * P] = pair
    half = HD // 2
    inv = np.power(np.float32(10000.0), -np.arange(half, dtype=np.float32) / np.float32(half))
    ang = np.arange(TOK, dtype=np.float32)[:, None] * inv[None, :]
    for t in range(NT):
        c[:, C_COS + half * t:C_COS + half * (t + 1)] = np.cos(ang[t * P:(t + 1) * P])
        c[:, C_SIN + half * t:C_SIN + half * (t + 1)] = np.sin(ang[t * P:(t + 1) * P])
    c[:, C_IO8:C_IO8 + 8] = np.arange(8)[None, :]
    return c


def build(nc, a, out, last="moe"):
    f32 = mybir.dt.float32
    f32r = mybir.dt.float32r
    u32 = mybir.dt.uint32
    i32 = mybir.dt.int32
    ALU = mybir.AluOpType
    ACT = mybir.ActivationFunctionType
    AX = mybir.AxisListType
    stages = ["in", "mix0", "ffn", "mix1", "moe"]
    upto = stages.index(last)

    ctx = ExitStack()
    with ctx:
        def sb(name, shape, dt=f32):
            return ctx.enter_context(nc.sbuf_tensor(name, shape, dt))

        raw = sb("raw", [P, RAW, CH])
        w_hi = sb("w_hi", [P, SPL, CH], f32r)
        w_lo = sb("w_lo", [P, SPL, CH], f32r)
        x_hi = sb("x_hi", [P, KC * TOK], f32r)
        x_lo = sb("x_lo", [P, KC * TOK], f32r)
        a_hi = sb("a_hi", [P, 2, BLK], f32r)
        a_lo = sb("a_lo", [P, 2, BLK], f32r)
        h = sb("h", [P, NT, DM])
        consts = sb("consts", [P, NCONST])
        small = sb("small", [P, NSMALL])
        misc = sb("misc", [P, 512])
        ws_raw = sb("ws_raw", [P, KC, 12])
        ws_hi = sb("ws_hi", [P, KC, 12], f32r)
        ws_lo = sb("ws_lo", [P, KC, 12], f32r)
        wr_raw = sb("wr_raw", [P, KC, NE])
        wr_hi = sb("wr_hi", [P, KC, NE], f32r)
        wr_lo = sb("wr_lo", [P, KC, NE], f32r)
        idx8 = sb("idx8", [P, NT, 8], u32)
        flag = sb("flag", [1, 1], i32)
        arena = sb("arena", [P, 16960])
        gain = sb("gain", [P, DM])
        bank = [ctx.enter_context(nc.psum_tensor(f"bank{i}", [P, BLK], f32)) for i in range(8)]

        xT_hi = x_hi[:, :].rearrange("p (k t) -> p k t", k=KC)
        xT_lo = x_lo[:, :].rearrange("p (k t) -> p k t", k=KC)

        def cst(at, n=P):
            return consts[:, at:at + n]

        ident = cst(C_ID)

        def smallv(name, n):
            return small[:, SM_AT[name]:SM_AT[name] + n]

        def area(at, *dims):
            n = 1
            for d in dims:
                n *= d
            v = arena[:, at:at + n]
            if len(dims) == 1:
                return v
            if len(dims) == 2:
                return v.rearrange("p (a b) -> p a b", a=dims[0])
            return v.rearrange("p (a b c) -> p a b c", a=dims[0], b=dims[1])

        gg = area(0, NT, BLK)
        zq, zk, zv = (area(1024 * (i + 1), NT, BLK) for i in range(3))
        zT = area(4096, 12, 259)
        cT = area(7204, 12, TOK)
        qT = area(10276, H0, TOK)
        kT = area(11300, H0, TOK)
        bias0 = area(12324, H0, 384)
        rows_out = area(14884, NT, DM)
        col_rows = area(14884, P)[0:82]
        turned_small = area(15140, TOK)[0:12]
        diag = area(15396, NT, P)
        r_bc = area(15652, TOK)
        att_s = sb("att_s", [P, 2, 384])
        att_T = sb("att_T", [P, 2, 384])
        prob = [att_s[:, 0, :], att_s[:, 1, :], gain[:, 0:384]]
        sq8 = area(4096, 8, TOK)
        bc8 = area(6144, 8, P)
        Xi, Yi = (area(10276 + 1024 * i, 8, P) for i in range(2))
        Zi = area(6144, 8, P)
        DT, MT, AT = (area(1024 * (i + 1), 8, P) for i in range(3))
        bv = area(4096, 8, P)
        kg0 = area(5120, H0, P)
        kb1 = area(5632, H0, P)
        NTl = [area(12324 + 1024 * i, 8, P) for i in range(2)]
        vn = area(10276, NT, H0 * P)
        wT1 = area(12324, H0, P)
        S1 = area(12836, H0, P)
        rot = [area(14372 + 512 * i, 4, NT, HD // 2) for i in range(2)]
        sq1 = area(12324, NT, DM)
        hn = area(10276, NT, DM)
        zq1, zk1, zv1 = (area(2048 * i, NT, DM) for i in range(3))
        tmp1 = area(6144, NT, DM)
        rows_out1 = area(8192, NT, DM)
        qT1 = area(10276, H1, TOK)
        kT1 = area(12324, H1, TOK)
        sil = area(0, 2, BLK)
        act = area(1024, 2, BLK)
        y_sb = area(2048, DM)
        perm = area(3072, NT, P)
        permc = area(3328, NT, P)
        permT = area(3584, NT, P)

        half_head = HD // 2

        def heads_halves(v):
            v = v.rearrange("p t (c d) -> p t c d", d=HD)
            return v[:, :, :, 0:half_head], v[:, :, :, half_head:HD]
        by_cos, by_sin = heads_halves(tmp1), heads_halves(rows_out1)

        def rotary_table(w, part):
            return rot[w][:, part, :, :].unsqueeze(2).to_broadcast([P, NT, H1, half_head])

        ss = misc[:, 0:16].rearrange("p (r c) -> p r c", r=4)
        m8 = misc[:, 16:32]
        pre = misc[:, 32:56].rearrange("p (t c) -> p t c", t=NT)
        gl = misc[:, 56:80].rearrange("p (t c) -> p t c", t=NT)
        coef = misc[:, 80:92]
        t24 = misc[:, 92:116].rearrange("p (t c) -> p t c", t=NT)
        u24 = misc[:, 116:140].rearrange("p (t c) -> p t c", t=NT)
        cols = misc[:, 140:160]
        e8 = misc[:, 160:168]
        beta = misc[:, 168:176].rearrange("p (t c) -> p t c", t=NT)
        be1 = misc[:, 176:180]
        hs = misc[:, 180:212]
        half_neg = misc[:, 212:228]
        rstd = misc[:, 228:236]
        rqk = misc[:, 484:500]
        okq = misc[:, 236:244].rearrange("p (t c) -> p t c", t=NT)
        kgs = misc[:, 304:308]
        kbs = misc[:, 308:312]
        e1q = misc[:, 312:316]
        betar = misc[:, 316:324].rearrange("p (t c) -> p t c", t=NT)
        nm = misc[:, 244:250].rearrange("p (b t) -> p b t", b=3)
        ls = misc[:, 250:256].rearrange("p (b t) -> p b t", b=3)
        rl = misc[:, 324:330].rearrange("p (b t) -> p b t", b=3)
        col_all = misc[:, 332:414]
        qk_gain = misc[:, 414:415]
        q_scale = misc[:, 256:272].rearrange("p (t c) -> p t c", t=NT)
        cw = col_all[:, 0:48].rearrange("p (k c) -> p k c", k=4)
        gcol = misc[:, 380:412].rearrange("p (r k) -> p r k", r=4)
        lg = misc[:, 432:448].rearrange("p (t e) -> p t e", t=NT)
        rank = misc[:, 448:466].rearrange("p (t e) -> p t e", t=NT)
        comb = misc[:, 466:484].rearrange("p (t e) -> p t e", t=NT)
        g2 = misc[:, 484:492].rearrange("p (t c) -> p t c", t=NT)
        scr = misc[:, 500:501]

        names = """consts_in ident_in small_in col_in wsmall_in wr_in gain_in dve_step act_step act_norm rbc_ps rbc_done diag_done narrow_ps narrow_done
            hi_done lo_done chunk_used ws_split h_ready sq_done mean_done root_done rows_done head_sq tr_done xh_done
            xl_done col_T col_done sums_half tap_done up_norm kq_ps v_done sin_done cos_done rl_done first_hi first_lo pre_ps pre_done softplus_e softplus_l gates_done beta_done bc_done cum_ps
            cum_done z_out zT_out cT_done sq_made norm_ps norm_add norm_root norm_done consts_done rot_done qk_rows_done qk_tr
            qk_T bias_done scores_ready sc_done exp_done p_tr pT_done pv_ready o_done hs_done hr_root
            kv_tr kv_done gcb_ps diff_done decay_done kk_ps MT_done AT_done nt_done z_ps Zi_done xy_ps xy_done
            u_ps vn_done w_ps wT_done s_ps S_done o_ps go_done silu_g og_done out_ps act_sil act_done aT_hi aT_lo down_done
            lg_ps lg_done g_exp route_done rank_ps rank_done perm_done g_ps y_zero y_done permT_ps permT_done
            sc_ps sc_add a_tr h_out flag_done out_done seed""".split()
        S = {n: ctx.enter_context(nc.semaphore(n)) for n in names}
        x_in = [ctx.enter_context(nc.semaphore(f"x_in{t}")) for t in range(NT)]
        raw_in = [ctx.enter_context(nc.semaphore(f"raw_in{i}")) for i in range(RAW)]
        block = ctx.enter_context(nc.Block())

        chunk_limit = [N_OUT, N_FFN, N_QKV, N_MOE, 1 << 30][upto]

        IN_COL = [1540, 2052, 2564, 0, 512, 1024, 3084]

        def dense_source(n):
            def quarter(w, k, c):
                return w[k * 512:(k + 1) * 512, c:c + BLK].rearrange("(k p) n -> p k n", p=P)
            if n < N_OUT:
                return quarter(a["e_w_in"][0], n % 2, IN_COL[n // 2])
            if n < N_FFN:
                return quarter(a["e_w_out"][0], (n - N_OUT) // 2, (n - N_OUT) % 2 * BLK)
            if N_QKV <= n < N_WO:
                return quarter(a["o_w_qkv"][0], (n - N_QKV) % 2, (n - N_QKV) // 2 * BLK)
            return quarter(a["o_w_out"][0], (n - N_WO) // 2, (n - N_WO) % 2 * BLK)

        @block.sync
        def _(sp):
            def load(k, src, n):
                if k >= RAW or not isinstance(n, int):
                    sp.wait_ge(S["lo_done"], n - RAW + 1)
                sp.dma_start(raw[:, k % RAW, 0:CH].rearrange("p (k n) -> p k n", k=src.shape[1]),
                             src).then_inc(raw_in[k % RAW], 16)

            sp.dma_start(consts[:, 0:P], a["consts"][:, 0:P]).then_inc(S["ident_in"], 16)
            for t in range(NT):
                sp.dma_start(h[:, t, :], a["x"][0, t * P:(t + 1) * P, :]).then_inc(x_in[t], 16)
            for r, name in enumerate(("e_norm1", "e_norm2", "o_norm1", "o_norm2")):
                sp.dma_start(col_rows[48 + 8 * r:56 + 8 * r, :], a[name].rearrange("o (k p) -> (o k) p", p=P))\
                    .then_inc(S["col_in"], 16)
            sp.dma_start(col_rows[0:48, :], a["e_gdn_conv"][0].rearrange("k (c p) -> (k c) p", p=P))\
                .then_inc(S["col_in"], 16)
            for r, name in enumerate(("e_fox_q_norm", "e_fox_k_norm")):
                sp.dma_start(col_rows[80 + r:81 + r, :], a[name]).then_inc(S["col_in"], 16)
            for n in range(N_IN, min(N_FFN, chunk_limit)):
                load(n, dense_source(n), n)
                if n == 1:
                    sp.dma_start(consts[:, P:NCONST], a["consts"][:, P:NCONST]).then_inc(S["consts_in"], 16)
            if upto >= 2:
                wgu, wd = a["e_ffn_w_gate_up"][0], a["e_ffn_w_down"][0]

                def ffn_gu(j, up):
                    return wgu[:, bass.ds(up * FF + j * 256, 256)].rearrange("(k p) n -> p k n", p=P)

                def ffn_d(j):
                    return wd[bass.ds(j * 256, 256), :].rearrange("(k p) n -> p k n", p=P)

                load(N_FFN, ffn_gu(0, 0), N_FFN)
                load(N_FFN + 1, ffn_gu(0, 1), N_FFN + 1)
                with sp.Fori(0, (FS - 1) // 2) as i:
                    for q in range(2):
                        for c, src in enumerate((ffn_gu(2 * i + q + 1, 0), ffn_gu(2 * i + q + 1, 1),
                                                 ffn_d(2 * i + q))):
                            k = N_FFN + 2 + 3 * q + c
                            load(k, src, i * 6 + k)
                load(N_QKV - 1, ffn_d(FS - 1), N_QKV - 1)
            for n in range(N_QKV, min(N_MOE, chunk_limit)):
                load(n, dense_source(n), n)
            if upto >= 4:
                egu, ed = a["o_exp_w_gate_up"][0], a["o_exp_w_down"][0]

                def expert_loads(e, base):
                    def gu(j, up, k):
                        c = up * FE + j * BLK
                        return egu[bass.ds(e, 1), k * 512:(k + 1) * 512, c:c + BLK]\
                            .rearrange("o (k p) n -> p (o k) n", p=P)

                    def dn(j, k):
                        r = j * BLK + k * 256
                        return ed[bass.ds(e, 1), r:r + 256, :].rearrange("o (k p) n -> p (o k) n", p=P)
                    c = 0
                    for j in range(ES):
                        srcs = [gu(j, up, k) for up in range(2) for k in range(2)]
                        if j >= 1:
                            srcs += [dn(j - 1, k) for k in range(2)]
                        if j == ES - 1:
                            srcs += [dn(j, k) for k in range(2)]
                        for src in srcs:
                            load(base + c, src, e * PER_E + (base + c))
                            c += 1
                with sp.Fori(0, NE) as e:
                    expert_loads(e, N_MOE)
                sp.wait_ge(S["flag_done"], 1)
                over = sp.value_load(flag[0:1, 0:1], min_val=0, max_val=NE)
                with sp.If(over > 0):
                    with sp.Fori(0, NE) as e:
                        expert_loads(e, N_MOE + NE * PER_E)
            sp.wait_ge(S["h_out"], 1)
            for t in range(NT):
                sp.dma_start(out[0, t * P:(t + 1) * P, :], h[:, t, :]).then_inc(S["out_done"], 16)
            sp.wait_ge(S["out_done"], 16 * NT)

        @block.gpsimd
        def _(gp):
            gp.memset(half_neg, -0.5).then_inc(S["consts_done"], 1)

            def load_gain(name):
                gp.dma_start(gain[:, :], a[name][0:1, :].to_broadcast([P, DM])).then_inc(S["gain_in"], 16)

            def inverse_root(out, x, done):
                gp.tensor_tensor(out, x, half_neg[:, 0:out.shape[1]], ALU.pow).then_inc(S[done], 1)

            def norm(r):
                gp.wait_ge(S["mean_done"], r + 1)
                inverse_root(rstd[:, 2 * r:2 * r + 2], ss[:, r, 0:2], "root_done")

            def head_root(w, at, n):
                gp.wait_ge(S["hs_done"], w + 1)
                inverse_root(hs[:, at:at + n], hs[:, at:at + n], "hr_root")

            w_in = a["e_w_in"][0].rearrange("(k p) n -> p k n", p=P)
            gp.dma_start(ws_raw[:, :, 0:4], w_in[:, :, 1536:1540]).then_inc(S["wsmall_in"], 16)
            gp.dma_start(ws_raw[:, :, 4:12], w_in[:, :, 3076:3084]).then_inc(S["wsmall_in"], 16)
            gp.wait_ge(S["consts_done"], 1)
            norm(0)
            for name, key in zip(SMALL, ["e_fox_f_bias", "e_gdn_a_log", "e_gdn_dt_bias", "e_gdn_o_norm", "o_q_norm", "o_k_norm"]):
                w = a[key].shape[1]
                gp.dma_start(small[:, SM_AT[name]:SM_AT[name] + w], a[key][0:1, :].to_broadcast([P, w]))\
                    .then_inc(S["small_in"], 16)
            gp.dma_start(wr_raw[:, :, :], a["o_router"][0].rearrange("(k p) n -> p k n", p=P))\
                .then_inc(S["wr_in"], 16)
            head_root(0, 0, 8)
            gp.wait_ge(S["norm_add"], 1)
            inverse_root(rqk, rqk, "norm_root")
            head_root(1, 16, 8)
            if upto < 1:
                return
            head_root(2, 0, 4)
            head_root(3, 4, 4)
            if upto < 2:
                return
            norm(1)
            if upto < 3:
                return
            norm(2)
            gp.wait_ge(S["rot_done"], 1)
            for w in range(2):
                gp.wait_ge(S["z_out"], 6 + 2 * w)
                if w == 1:
                    gp.wait_ge(S["qk_rows_done"], 2)
                x = heads_halves((zq1, zk1)[w])
                for part in range(2):
                    m = gp.tensor_tensor(by_sin[part], x[1 - part], rotary_table(w, 3 - part), ALU.mult)
                m.then_inc(S["sin_done"], 1)
                head_root(4 + w, 16 - 16 * w, 16)
            gp.wait_ge(S["o_done"], H0 + H1)
            if upto < 4:
                return
            load_gain("o_norm2")
            norm(3)

        @block.tensor
        def _(pe):
            def turn_rows(src, tb, half, waits=None):
                for t in range(NT):
                    if waits:
                        pe.wait_ge(*waits[t])
                    for kc in range(4 * half, 4 * half + 4):
                        at = (kc % 2) * TOK + t * P
                        m = pe.transpose(bank[tb + kc // 2][:, at:at + P], src[:, t, kc * P:(kc + 1) * P], ident)
                        if t == NT - 1 and kc % 2 == 1:
                            m.then_inc(S["tr_done"], 1)

            def h_waits(r, half):
                return [(S["h_ready"], 4 * (r - 1) + 2 * half + t + 1) for t in range(NT)]

            def x_ready(r, kc):
                pe.wait_ge(S["xl_done"], 8 * r + kc + 1)

            def passes(dst, lhs, rhs, first, final):
                pe.matmul(dst, lhs[0], rhs[0], start=first, stop=False, skip_group_check=True)
                pe.matmul(dst, lhs[1], rhs[0], start=False, stop=False, skip_group_check=True)
                return pe.matmul(dst, lhs[0], rhs[1], start=False, stop=final, skip_group_check=True)

            def split_w(k, c0, n):
                s = k % SPL
                return w_hi[:, s, c0:c0 + n], w_lo[:, s, c0:c0 + n]

            def split_x(kc, t0, n):
                return xT_hi[:, kc, t0:t0 + n], xT_lo[:, kc, t0:t0 + n]

            def row_part(n, half, banks, kcs, used=True):
                pe.wait_ge(S["lo_done"], n + 1)
                for kc in kcs:
                    for t in range(NT):
                        m = passes(bank[banks + t][:, :], split_x(4 * half + kc, t * P, P),
                                   split_w(n, kc * BLK, BLK), half == 0 and kc == 0, half == 1 and kc == 3)
                if used:
                    m.then_inc(S["chunk_used"], 1)

            def row_group(n0, pair, free, fresh=None, hooks=None):
                if free:
                    pe.wait_ge(S[free[0]], free[1])
                for half in range(2):
                    pe.wait_ge(S["lo_done"], n0 + half + 1)
                    for kc in range(4):
                        if hooks and (half, kc) in hooks:
                            hooks[half, kc]()
                        if fresh is not None:
                            x_ready(fresh, 4 * half + kc)
                        for t in range(NT):
                            m = passes(bank[2 * pair + t][:, :], split_x(4 * half + kc, t * P, P),
                                       split_w(n0 + half, kc * BLK, BLK),
                                       half == 0 and kc == 0, half == 1 and kc == 3)
                    m.then_inc(S["chunk_used"], 1)

            def col_group(n0, pair, free, fresh=None):
                if free:
                    pe.wait_ge(S[free[0]], free[1])
                for half in range(2):
                    if fresh is None or half == 1:
                        pe.wait_ge(S["lo_done"], n0 + half + 1)
                    for kc in range(4):
                        if fresh is not None:
                            x_ready(fresh, 4 * half + kc)
                            if half == 0:
                                pe.wait_ge(*((S["first_lo"], kc + 1) if kc < 3 else (S["lo_done"], 1)))
                        for c in range(4):
                            m = passes(bank[2 * pair + c // 2][:, (c % 2) * TOK:(c % 2 + 1) * TOK],
                                       split_w(n0 + half, kc * BLK + c * P, P),
                                       split_x(4 * half + kc, 0, TOK),
                                       half == 0 and kc == 0 and c % 2 == 0, half == 1 and kc == 3)
                    m.then_inc(S["chunk_used"], 1)

            def attention(heads, qTt, kTt, v, done, fill, before=None):
                def scores(i):
                    if i >= 2:
                        pe.wait_ge(S["sc_done"], done + i - 1)
                    b = bank[i % 2]
                    pe.matmul(b[:, 0:P], qTt[:, i, 0:P], kTt[:, i, 0:P], start=True, stop=True)
                    pe.matmul(b[:, P:3 * P], qTt[:, i, P:TOK], kTt[:, i, :],
                              start=True, stop=True).then_inc(S["scores_ready"], 1)

                def turn(i):
                    pe.wait_ge(S["exp_done"], done + i + 1)
                    if i >= 2:
                        pe.wait_ge(S["pT_done"], done + i - 1)
                    for b in range(3):
                        m = pe.transpose(bank[2 + i % 2][:, b * P:(b + 1) * P],
                                         prob[i % 3][:, b * P:(b + 1) * P], ident)
                    m.then_inc(S["p_tr"], 1)

                def weigh(i):
                    pe.wait_ge(S["pT_done"], done + i + 1)
                    if i >= 2:
                        pe.wait_ge(S["o_done"], done + i - 1)
                    b = bank[4 + i % 2]
                    pe.matmul(b[:, 0:P], att_T[:, i % 2, 0:P], v[:, 0, i * P:(i + 1) * P], start=True, stop=True)
                    pe.matmul(b[:, P:2 * P], att_T[:, i % 2, P:2 * P], v[:, 0, i * P:(i + 1) * P],
                              start=True, stop=False)
                    pe.matmul(b[:, P:2 * P], att_T[:, i % 2, 2 * P:3 * P], v[:, 1, i * P:(i + 1) * P],
                              start=False, stop=True).then_inc(S["pv_ready"], 1)
                scores(0)
                scores(1)
                if before:
                    before()
                for i in range(heads + 1):
                    if i + 2 < heads:
                        scores(i + 2)
                    if i < heads:
                        turn(i)
                    if i >= 1:
                        weigh(i - 1)
                    if i in fill:
                        fill[i]()

            def spread_roots(r):
                pe.wait_ge(S["diag_done"], r + 1)
                for t in range(NT):
                    m = pe.matmul(bank[7 if r == 0 else 3][:, t * P:(t + 1) * P], cst(C_ONE), diag[:, t, :],
                                  start=True, stop=True)
                m.then_inc(S["rbc_ps"], 1)

            def narrow(dst, w, hi, lo):
                for kc in range(KC):
                    m = passes(dst, (hi[:, kc, :], lo[:, kc, :]), (xT_hi[:, kc, :], xT_lo[:, kc, :]),
                               kc == 0, kc == KC - 1)
                m.then_inc(S["narrow_ps"], 1)

            pe.wait_ge(S["ident_in"], 16)
            turn_rows(h, 4, 0, [(x_in[t], 16) for t in range(NT)])
            pe.wait_ge(S["col_in"], 16 * 7)
            pe.transpose(bank[0][:, 0:82], col_rows[:, :], ident[0:82, 0:82]).then_inc(S["col_T"], 1)
            turn_rows(h, 4, 1)
            pe.wait_ge(S["col_done"], 1)
            for g in range(7):
                free = (None, None, ("zT_out", 1), ("zT_out", 2), ("zT_out", 3), ("z_out", 1), ("z_out", 2))[g]
                if g < 3:
                    col_group(N_IN + 2 * g, g % 2, free, 0 if g == 0 else None)
                else:
                    row_group(N_IN + 2 * g, g % 2, free)
                if g == 0:
                    pe.wait_ge(S["consts_in"], 16)
                    spread_roots(0)
                    pe.wait_ge(S["ws_split"], 2)
                    narrow(bank[4][0:12, 0:TOK], 12, ws_hi, ws_lo)
                if g == 1:
                    pe.wait_ge(S["narrow_done"], 1)
                    for t in range(NT):
                        m = pe.transpose(bank[6][:, 12 * t:12 * t + 12], turned_small[:, t * P:(t + 1) * P],
                                         ident[0:12, 0:12])
                    m.then_inc(S["pre_ps"], 1)
                if g == 4:
                    pe.wait_ge(S["sq_made"], 1)
                    for i in range(16):
                        c, t = divmod(i, 2)
                        m = pe.matmul(bank[4][:, 256 + i:257 + i], sq8[:, c, t * P:(t + 1) * P], cst(C_ONE, 1),
                                      start=True, stop=True)
                    m.then_inc(S["norm_ps"], 1)
                    pe.wait_ge(S["gates_done"], 1)
                    c4 = bank[5]
                    pe.matmul(c4[:, 0:4], cst(C_U), gl[:, 0, 4:8], start=True, stop=True)
                    pe.matmul(c4[:, 4:8], cst(C_U), gl[:, 1, 4:8], start=True, stop=True)
                    pe.matmul(c4[:, 8:12], cst(C_U), gl[:, 0, 0:4], start=True, stop=True)
                    pe.matmul(c4[:, 12:16], cst(C_ONE), gl[:, 0, 0:4], start=True, stop=False)
                    pe.matmul(c4[:, 12:16], cst(C_U), gl[:, 1, 0:4], start=False, stop=True)
                    pe.matmul(c4[:, 16:20], cst(C_L), gl[:, 0, 4:8], start=True, stop=True)\
                        .then_inc(S["cum_ps"], 1)
                    pe.wait_ge(S["bc_done"], 1)
                    for hh in range(H0):
                        b = bank[6 + hh // 2][:, (hh % 2) * TOK:(hh % 2 + 1) * TOK]
                        pe.matmul(b[:, 0:P], bc8[:, hh, :], cst(C_U), start=True, stop=True)
                        pe.matmul(b[:, P:TOK], bc8[:, hh, :], cst(C_ONE), start=True, stop=False)
                        m = pe.matmul(b[:, P:TOK], bc8[:, H0 + hh, :], cst(C_U), start=False, stop=True)
                    m.then_inc(S["cum_ps"], 1)
            if upto < 1:
                return
            pe.wait_ge(S["norm_add"], 1)
            for w, src in enumerate((zq, zk)):
                if w == 1:
                    pe.wait_ge(S["bias_done"], 1)
                    pe.wait_ge(S["qk_rows_done"], 1)
                for t in range(NT):
                    for hh in range(H0):
                        m = pe.transpose(bank[4 + 2 * w + t][:, hh * P:(hh + 1) * P],
                                         src[:, t, hh * P:(hh + 1) * P], ident)
                    m.then_inc(S["qk_tr"], 1)
            pe.wait_ge(S["z_out"], 4)
            pe.wait_ge(S["bc_done"], 2)
            for i in range(8):
                m = pe.matmul(bank[i // 4][:, (i % 4) * P:(i % 4 + 1) * P], bc8[:, i, :], cst(C_U),
                              start=True, stop=True)
            m.then_inc(S["gcb_ps"], 1)
            pe.wait_ge(S["silu_g"], 3)
            pe.wait_ge(S["qk_T"], 2)
            for i in range(16):
                c, t = 4 + i // 2, i % 2
                m = pe.transpose(bank[2 + i // 4][:, (i % 4) * P:(i % 4 + 1) * P], cT[:, c, t * P:(t + 1) * P], ident)
            m.then_inc(S["kv_tr"], 1)
            pe.wait_ge(S["qk_T"], 4)
            pe.wait_ge(S["diff_done"], 1)

            def key_query():
                for i in range(8):
                    t, hh = divmod(i, H0)
                    m = pe.matmul(bank[6 + i // 4][:, (i % 4) * P:(i % 4 + 1) * P], cT[:, 4 + hh, t * P:(t + 1) * P],
                                  cT[:, hh, t * P:(t + 1) * P], start=True, stop=True)
                m.then_inc(S["kq_ps"], 1)
            def strengths(t):
                if t == 0:
                    pe.wait_ge(S["bc_done"], 3)
                else:
                    pe.wait_ge(S["pT_done"], H0)
                for hh in range(H0):
                    m = pe.matmul(bank[2 + t][:, hh * P:(hh + 1) * P], bc8[:, t * H0 + hh, :], ident,
                                  start=True, stop=True)
                m.then_inc(S["gcb_ps"], 1)
            attention(H0, qT, kT, zv, 0, {0: lambda: pe.wait_ge(S["v_done"], 1), 1: key_query,
                                          3: lambda: strengths(0), 4: lambda: strengths(1)},
                      lambda: pe.wait_ge(S["kv_done"], 1))
            pe.wait_ge(S["o_done"], H0)
            for i in range(8):
                t, hh = divmod(i, H0)
                k = cT[:, 4 + hh, t * P:(t + 1) * P]
                m = pe.matmul(bank[4 + i // 4][:, (i % 4) * P:(i % 4 + 1) * P], k, k, start=True, stop=True)
            m.then_inc(S["kk_ps"], 1)
            for lv in range(len(LEVELS)):
                n = NTl[lv % 2]
                pe.wait_ge(S["nt_done"], lv + 1)

                def four(dst, t, lhs, rhs):
                    for hh in range(H0):
                        i = t * H0 + hh
                        m = pe.matmul(bank[dst + t][:, hh * P:(hh + 1) * P], lhs[:, i, :], rhs[:, i, :],
                                      start=True, stop=True)
                    return m
                if lv == 0:
                    for i in range(8):
                        m = pe.transpose(bank[i // 4][:, (i % 4) * P:(i % 4 + 1) * P], n[:, i, :], ident)
                    m.then_inc(S["z_ps"], 2)
                    continue
                for t in range(NT):
                    pe.wait_ge(S["xy_done"], 2 * (lv - 1) + t + 1)
                    four(0, t, n, Xi).then_inc(S["z_ps"], 1)
                for t in range(NT):
                    pe.wait_ge(S["Zi_done"], 2 * (lv - 1) + t + 1)
                    m = four(2, t, Zi, Yi)
                    if lv < len(LEVELS) - 1:
                        m = four(4, t, Yi, Zi)
                    m.then_inc(S["xy_ps"], 1)
                if lv == 1:
                    pe.wait_ge(S["AT_done"], 1)
                    turn_rows(rows_out, 6, 0)
            pe.wait_ge(S["xy_done"], 2 * len(LEVELS))
            for t in range(NT):
                for hh in range(H0):
                    i = t * H0 + hh
                    m = pe.matmul(bank[t][:, hh * P:(hh + 1) * P], Yi[:, i, :], bv[:, i, :],
                                  start=(t == 0 or hh == 0), stop=(t == 0), skip_group_check=True)
            m.then_inc(S["u_ps"], 1)
            for hh in range(H0):
                m = pe.matmul(bank[4][:, hh * P:(hh + 1) * P], kb1[:, hh, :], Yi[:, H0 + hh, :],
                              start=True, stop=True)
            m.then_inc(S["w_ps"], 1)
            x_ready(1, 3)
            row_part(N_OUT, 0, 6, (0,), used=False)
            pe.wait_ge(S["vn_done"], 1)
            for hh in range(H0):
                m = pe.matmul(bank[5][:, hh * P:(hh + 1) * P], kg0[:, hh, :], vn[:, 0, hh * P:(hh + 1) * P],
                              start=True, stop=True)
            m.then_inc(S["s_ps"], 1)
            for hh in range(H0):
                m = pe.matmul(bank[2][:, hh * P:(hh + 1) * P], AT[:, hh, :], vn[:, 0, hh * P:(hh + 1) * P],
                              start=True, stop=True)
            m.then_inc(S["o_ps"], 1)
            row_part(N_OUT, 0, 6, (1,), used=False)
            pe.wait_ge(S["S_done"], 1)
            pe.wait_ge(S["wT_done"], 1)
            for hh in range(H0):
                m = pe.matmul(bank[1][:, hh * P:(hh + 1) * P], wT1[:, hh, :], S1[:, hh, :],
                              start=False, stop=True, skip_group_check=True)
            m.then_inc(S["u_ps"], 1)
            for hh in range(H0):
                m = pe.matmul(bank[0][:, hh * P:(hh + 1) * P], cT[:, hh, P:TOK], S1[:, hh, :],
                              start=True, stop=True)
            m.then_inc(S["o_ps"], 1)
            pe.wait_ge(S["vn_done"], 2)
            for hh in range(H0):
                m = pe.matmul(bank[3][:, hh * P:(hh + 1) * P], AT[:, H0 + hh, :], vn[:, 1, hh * P:(hh + 1) * P],
                              start=True, stop=True)
            m.then_inc(S["o_ps"], 1)
            row_part(N_OUT, 0, 6, (2, 3))
            row_part(N_OUT + 1, 0, 4, (0, 1, 2), used=False)
            pe.wait_ge(S["og_done"], 1)
            turn_rows(rows_out, 0, 1)
            row_part(N_OUT + 1, 0, 4, (3,))
            x_ready(1, KC - 1)
            row_part(N_OUT + 2, 1, 6, range(4))
            row_part(N_OUT + 3, 1, 4, (0, 1), used=False)
            if upto >= 2:
                turn_rows(h, 2, 0, h_waits(1, 0))
            row_part(N_OUT + 3, 1, 4, (2, 3))
            if upto < 2:
                return

            def gate_up(k, n, q, parts=(0, 1)):
                for w in parts:
                    pe.wait_ge(S["lo_done"], n + w + 1)
                    for c in range(2):
                        for kc in range(KC):
                            m = passes(bank[2 * q + w][:, c * TOK:(c + 1) * TOK],
                                       split_w(k + w, kc * 256 + c * P, P), split_x(kc, 0, TOK),
                                       kc == 0, kc == KC - 1)
                    m.then_inc(S["chunk_used"], 1)

            def ffn_down(k, n, q, first, final):
                pe.wait_ge(S["lo_done"], n + 1)
                for half in range(2):
                    for kc in range(2):
                        for t in range(NT):
                            at = kc * TOK + t * P
                            m = passes(bank[4 + 2 * half + t][:, :], (a_hi[:, q, at:at + P], a_lo[:, q, at:at + P]),
                                       split_w(k, kc * DM + half * BLK, BLK), first and kc == 0, final and kc == 1)
                    if final and half == 0:
                        m.then_inc(S["sums_half"], 1)
                m.then_inc(S["chunk_used"], 1)

            pe.wait_ge(S["lo_done"], N_FFN + 1)
            for half in range(2):
                if half == 1:
                    turn_rows(h, 4, 1, h_waits(1, 1))
                for kc in range(4 * half, 4 * half + 4):
                    x_ready(2, kc)
                    for c in range(2):
                        m = passes(bank[0][:, c * TOK:(c + 1) * TOK], split_w(N_FFN, kc * 256 + c * P, P),
                                   split_x(kc, 0, TOK), kc == 0 and c == 0, kc == KC - 1)
            m.then_inc(S["chunk_used"], 1)
            gate_up(N_FFN, N_FFN, 0, (1,))
            spread_roots(1)
            pe.wait_ge(S["rbc_done"], 2)
            gate_up(N_FFN + 2, N_FFN + 2, 1)
            pe.wait_ge(S["aT_lo"], 1)
            ffn_down(N_FFN + 4, N_FFN + 4, 0, True, False)
            with pe.Fori(0, (FS - 3) // 2) as i:
                for q in range(2):
                    k = N_FFN + 5 + 3 * q
                    pe.wait_ge(S["act_done"], 2 * i + q + 1)
                    gate_up(k, i * 6 + k, q)
                    pe.wait_ge(S["aT_lo"], 2 * i + q + 2)
                    ffn_down(k + 2, i * 6 + (k + 2), 1 - q, False, False)
            k = N_FFN + 5 + 3 * (FS - 3)
            pe.wait_ge(S["act_done"], FS - 2)
            gate_up(k, k, 0)
            pe.wait_ge(S["aT_lo"], FS - 1)
            ffn_down(k + 2, k + 2, 1, False, False)
            pe.wait_ge(S["aT_lo"], FS)
            ffn_down(k + 3, k + 3, 0, False, True)
            if upto < 3:
                return
            turn_rows(h, 0, 0, h_waits(2, 0))
            for g in range(6):
                row_group(N_QKV + 2 * g, 2 + g % 2, ("z_out", 4 + g - 1) if g >= 2 else None,
                          3 if g == 0 else None,
                          {(0, 2): lambda: turn_rows(h, 0, 1, h_waits(2, 1))} if g == 0 else None)
            for w, src in enumerate((zq1, zk1)):
                pe.wait_ge(S["qk_rows_done"], w + 2)
                if w == 1:
                    pe.wait_ge(S["z_out"], 10)
                for hp in range(4):
                    for hh in (2 * hp, 2 * hp + 1):
                        for t in range(NT):
                            at = (hh % 2) * TOK + t * P
                            m = pe.transpose(bank[4 * w + hp][:, at:at + P], src[:, t, hh * P:(hh + 1) * P], ident)
                    m.then_inc(S["qk_tr"], 1)
            pe.wait_ge(S["qk_T"], 12)
            attention(H1, qT1, kT1, zv1, H0,
                      {6: lambda: turn_rows(rows_out1, 6, 0, [(S["o_done"], H0 + 4)] * NT),
                       7: lambda: (x_ready(4, 3), row_part(N_WO, 0, 6, (0, 1), used=False)),
                       8: lambda: row_part(N_WO, 0, 6, (2, 3))})
            row_part(N_WO + 1, 0, 0, (0, 1, 2), used=False)
            pe.wait_ge(S["o_done"], H0 + H1)
            turn_rows(rows_out1, 0, 1)
            row_part(N_WO + 1, 0, 0, (3,))
            x_ready(4, KC - 1)
            row_part(N_WO + 2, 1, 6, range(4))
            row_part(N_WO + 3, 1, 0, (0, 1), used=False)
            if upto >= 4:
                turn_rows(h, 4, 0, h_waits(3, 0))
            row_part(N_WO + 3, 1, 0, (2, 3))
            if upto < 4:
                return
            turn_rows(h, 0, 1, h_waits(3, 1))
            x_ready(5, KC - 1)
            narrow(bank[0][0:NE, 0:TOK], NE, wr_hi, wr_lo)
            pe.wait_ge(S["narrow_done"], 2)
            for t in range(NT):
                m = pe.transpose(bank[1][:, 8 * t:8 * t + 8], turned_small[0:NE, t * P:(t + 1) * P],
                                 ident[0:NE, 0:NE])
            m.then_inc(S["lg_ps"], 1)
            pe.wait_ge(S["route_done"], 1)
            pe.matmul(bank[2][:, 0:8], cst(C_US), lg[:, 0, :], start=True, stop=True)
            pe.matmul(bank[2][:, 8:16], cst(C_ONE), lg[:, 0, :], start=True, stop=False)
            pe.matmul(bank[2][:, 8:16], cst(C_US), lg[:, 1, :], start=False, stop=True)
            pe.matmul(bank[2][:, 16:24], cst(C_ONE), lg[:, 0, :], start=True, stop=False)
            pe.matmul(bank[2][:, 16:24], cst(C_ONE), lg[:, 1, :], start=False, stop=True).then_inc(S["rank_ps"], 1)

            def gather(done):
                pe.wait_ge(S["perm_done"], done)
                for kc in range(KC):
                    b = bank[1 + 2 * (kc // 4)][:, (kc % 4) * P:(kc % 4 + 1) * P]
                    for t in range(NT):
                        m = pe.matmul(b, hn[:, t, kc * P:(kc + 1) * P], perm[:, t, :], start=(t == 0), stop=(t == 1))
                m.then_inc(S["g_ps"], 1)

            def scatter(i, done, b=7):
                t, half = divmod(i, 2)
                pe.wait_ge(S["sc_add"], done)
                pe.matmul(bank[b][:, :], permT[:, t, :], y_sb[:, half * BLK:(half + 1) * BLK],
                          start=True, stop=True).then_inc(S["sc_ps"], 1)

            def experts(p, e):
                base = N_MOE + p * NE * PER_E
                c = [0]

                def chunk():
                    k = base + c[0]
                    c[0] += 1
                    pe.wait_ge(S["lo_done"], e * PER_E + (k + 1))
                    return k

                def steps(n):
                    return e * ES + (FS + p * NE * ES + n)

                def down(j):
                    pe.wait_ge(S["aT_lo"], steps(j + 1))
                    if j == 0:
                        pe.wait_ge(S["y_done"], e + (p * (NE + 1) + 1))
                    for part in range(2):
                        k = chunk()
                        for q in range(2):
                            at = (2 * part + q) * P
                            lhs = (a_hi[:, j % 2, at:at + P], a_lo[:, j % 2, at:at + P])
                            for half in range(2):
                                m = passes(bank[4 + half][:, :], lhs, split_w(k, q * DM + half * BLK, BLK),
                                           j == 0 and part == 0 and q == 0, j == ES - 1 and part == 1 and q == 1)
                        m.then_inc(S["chunk_used"], 1)

                def turn_act(j):
                    pe.wait_ge(S["act_done"], steps(j + 1))
                    pe.wait_ge(S["aT_lo"], steps(j))
                    for q in range(4):
                        m = pe.transpose(bank[6][:, q * P:(q + 1) * P], act[:, j % 2, q * P:(q + 1) * P], ident)
                    m.then_inc(S["a_tr"], 1)

                for j in range(ES):
                    if j == 0:
                        pe.wait_ge(S["xl_done"], e + (p * (NE + 1) + 49))
                        pe.wait_ge(S["act_done"], steps(0))
                    elif j >= 2:
                        pe.wait_ge(S["act_done"], steps(j - 1))
                    for w in range(2):
                        for half in range(2):
                            k = chunk()
                            if w == 1 and half == 0 and j == 1:
                                turn_act(0)
                            for kc in range(4):
                                at = (4 * half + kc) * P
                                m = passes(bank[2 * w + j % 2][:, :], (x_hi[:, at:at + P], x_lo[:, at:at + P]),
                                           split_w(k, kc * BLK, BLK),
                                           half == 0 and kc == 0, half == 1 and kc == 3)
                            m.then_inc(S["chunk_used"], 1)
                    if 1 <= j <= 4:
                        scatter(j - 1, e * 4 + (p * 4 * (NE + 1) + j))
                    if j >= 1:
                        down(j - 1)
                    if j >= 1:
                        turn_act(j)
                    if j == 5:
                        pe.wait_ge(S["sc_add"], e * 4 + (p * 4 * (NE + 1) + 5))
                        for t in range(NT):
                            m = pe.transpose(bank[7][:, t * P:(t + 1) * P], permc[:, t, :], ident)
                        m.then_inc(S["permT_ps"], 1)
                gather(e + (p * (NE + 1) + 2))
                down(ES - 1)

            def expert_pass(p):
                gather(p * (NE + 1) + 1)
                with pe.Fori(0, NE) as e:
                    experts(p, e)
                pe.wait_ge(S["y_done"], (p + 1) * (NE + 1))
                for i in range(4):
                    scatter(i, p * 4 * (NE + 1) + 4 * NE + max(i, 1), 7 - i % 2)

            expert_pass(0)
            pe.wait_ge(S["flag_done"], 1)
            over = pe.value_load(flag[0:1, 0:1], min_val=0, max_val=NE)
            with pe.If(over > 0):
                expert_pass(1)

        def kv_bank(c, t):
            i = 2 * c + t
            return bank[2 + i // 4][:, (i % 4) * P:(i % 4 + 1) * P]

        U_LAST = [3] + [4 * (j + 1) + 2 * (j - 1) - 1 for j in range(1, ES)]

        @block.scalar
        def _(act_e):
            n_step = [0]

            def link(ins):
                n_step[0] += 1
                ins.then_inc(S["act_step"], 1)
                act_e.wait_ge(S["act_step"], n_step[0])

            def split_at(k, n, uses):
                act_e.wait_ge(raw_in[k % RAW], uses)
                if not (isinstance(n, int) and n < SPL):
                    act_e.wait_ge(S["chunk_used"], n - SPL + 1)
                act_e.activation(w_hi[:, k % SPL, :], raw[:, k % RAW, :], ACT.Copy).then_inc(S["hi_done"], 1)

            def split(n):
                if n < chunk_limit:
                    split_at(n, n, 16 * (n // RAW + 1))

            def squares(r, half):
                for t in range(NT):
                    if r == 0:
                        act_e.wait_ge(x_in[t], 16)
                    else:
                        act_e.wait_ge(S["h_ready"], 4 * (r - 1) + 2 * half + t + 1)
                    cs = slice(half * BLK, (half + 1) * BLK)
                    act_e.activation(hn[:, t, cs], h[:, t, cs], ACT.Square,
                                     accum_out=ss[:, r, 2 * half + t:2 * half + t + 1]).then_inc(S["sq_done"], 1)

            def turned(r, tb, half, norm_at=None, both=(0, 1)):
                for b in [2 * half + q for q in both]:
                    act_e.wait_ge(S["tr_done"], 4 * r + b + 1)
                    if norm_at is None:
                        m = act_e.activation(x_hi[:, b * BLK:(b + 1) * BLK], bank[tb + b][:, :], ACT.Copy)
                    else:
                        for kc in (2 * b, 2 * b + 1):
                            m = act_e.activation(xT_hi[:, kc, :], bank[tb + b][:, (kc % 2) * TOK:(kc % 2 + 1) * TOK],
                                                 ACT.Copy, scale=gcol[:, norm_at, kc:kc + 1])
                    m.then_inc(S["xh_done"], 1)

            def softmax(heads, done, out_rows, fill=None):
                def weighted(i):
                    act_e.wait_ge(S["rl_done"], done + i + 1)
                    act_e.wait_ge(S["pv_ready"], done + i + 1)
                    for t in range(NT):
                        m = act_e.activation(out_rows[:, t, i * HD:(i + 1) * HD], bank[4 + i % 2][:, t * P:(t + 1) * P],
                                             ACT.Copy, scale=rl[:, i % 3, t:t + 1])
                    m.then_inc(S["o_done"], 1)

                def copy_T(i):
                    act_e.wait_ge(S["p_tr"], done + i + 1)
                    if i >= 2:
                        act_e.wait_ge(S["pv_ready"], done + i - 1)
                    act_e.activation(att_T[:, i % 2, :], bank[2 + i % 2][:, 0:384], ACT.Copy).then_inc(S["pT_done"], 1)
                for i in range(heads):
                    s = prob[i % 3]
                    act_e.wait_ge(S["sc_done"], done + i + 1)
                    act_e.activation(s[:, 0:P], s[:, 0:P], ACT.Exp,
                                     bias=nm[:, i % 3, 0:1], accum_out=ls[:, i % 3, 0:1])
                    act_e.activation(s[:, P:3 * P], s[:, P:3 * P], ACT.Exp,
                                     bias=nm[:, i % 3, 1:2], accum_out=ls[:, i % 3, 1:2]).then_inc(S["exp_done"], 1)
                    if i >= 1:
                        copy_T(i - 1)
                    if i >= 2:
                        weighted(i - 2)
                    if fill and i in fill:
                        fill[i]()
                copy_T(heads - 1)
                weighted(heads - 2)
                weighted(heads - 1)

            act_e.wait_ge(S["consts_done"], 1)
            act_e.activation(e8[:, 0:1], half_neg[:, 0:1], ACT.Copy)
            act_e.wait_ge(S["col_done"], 1)
            act_e.wait_ge(raw_in[0], 16)
            for q in range(4):
                if q % 2 == 0:
                    turned(0, 4, 0, 0, (q // 2,))
                act_e.activation(w_hi[:, 0, q * BLK:(q + 1) * BLK], raw[:, 0, q * BLK:(q + 1) * BLK], ACT.Copy)\
                    .then_inc(S["first_hi" if q < 3 else "hi_done"], 1)
            turned(0, 4, 1, 0)
            for n in range(N_IN + 1, N_OUT + SPL):
                if n <= N_OUT:
                    split(n)
                if n == 1:
                    for half in range(2):
                        squares(0, half)
                if n == 3:
                    act_e.wait_ge(S["narrow_ps"], 1)
                    act_e.activation(turned_small[:, :], bank[4][0:12, 0:TOK], ACT.Copy).then_inc(S["narrow_done"], 1)
                if n == 2:
                    act_e.wait_ge(S["wsmall_in"], 32)
                    act_e.activation(ws_hi[:, :, :], ws_raw[:, :, :], ACT.Copy).then_inc(S["ws_split"], 1)
                c = n - SPL
                if c in (2, 4, 6):
                    g = c // 2 - 1
                    act_e.wait_ge(S["zT_out"], g + 1)
                    for i in range(4 * g, 4 * g + 4):
                        m = act_e.activation(cT[:, i, :], zT[:, i, 0:TOK], ACT.Copy, scale=cw[:, 0, i:i + 1])
                    m.then_inc(S["tap_done"], 1)
                if c == 4:
                    act_e.wait_ge(S["pre_done"], 1)
                    act_e.activation(u24[:, :, :], t24[:, :, :], ACT.Exp).then_inc(S["softplus_e"], 1)
                if c == 6:
                    act_e.wait_ge(S["pre_done"], 2)
                    act_e.activation(t24[:, :, :], pre[:, :, :], ACT.Ln).then_inc(S["softplus_l"], 1)
                    act_e.wait_ge(S["small_in"], 16 * len(SMALL))
                    act_e.activation(coef[:, 4:8], smallv("al", 4), ACT.Exp).then_inc(S["softplus_l"], 1)
                if c >= 7 and c % 2 == 1:
                    g = c // 2
                    act_e.wait_ge(S["chunk_used"], 2 * g + 2)
                    for b in range(2):
                        m = act_e.activation((zq, zk, zv, gg)[g - 3][:, b, :], bank[2 * (g % 2) + b][:, :],
                                             ACT.Copy if g < 6 else ACT.Silu, scale=rstd[:, b:b + 1])
                    m.then_inc(S["z_out"], 1)
                if c in (4, 6, 8):
                    g = c // 2 - 2
                    act_e.wait_ge(S["cT_done"], g + 1)
                    act_e.activation(cT[:, 4 * g:4 * g + 4, :], cT[:, 4 * g:4 * g + 4, :], ACT.Silu)\
                        .then_inc(S["silu_g"], 1)
                if c == 6:
                    act_e.wait_ge(S["silu_g"], 2)
                    act_e.activation(sq8[:, :, :], cT[:, 0:8, :], ACT.Square).then_inc(S["sq_made"], 1)
                if c == 10:
                    act_e.wait_ge(S["cum_done"], 1)
                    act_e.activation(e8[:, 0:4], cols[:, 4:8], ACT.Exp)
                    act_e.activation(e8[:, 4:8], cols[:, 16:20], ACT.Exp)
                    act_e.activation(beta[:, :, :], gl[:, :, 8:12], ACT.Exp).then_inc(S["beta_done"], 1)
                if c in (7, 9):
                    w = (c - 7) // 2
                    act_e.wait_ge(S["z_out"], 1 + w)
                    if w == 1:
                        act_e.wait_ge(S["hs_done"], 1)
                    act_e.activation(area(12324, NT, BLK), (zq, zk)[w][:, :, :], ACT.Square).then_inc(S["head_sq"], 1)
                if c == 11:
                    act_e.wait_ge(S["wr_in"], 16)
                    act_e.activation(wr_hi[:, :, :], wr_raw[:, :, :], ACT.Copy).then_inc(S["ws_split"], 1)
            if upto < 1:
                return
            for w, dst in enumerate((qT, kT)):
                for t in range(NT):
                    act_e.wait_ge(S["qk_tr"], 2 * w + t + 1)
                    act_e.activation(dst[:, :, t * P:(t + 1) * P],
                                     bank[4 + 2 * w + t][:, :].rearrange("p (c t) -> p c t", c=H0), ACT.Copy,
                                     scale=qk_gain if w == 0 else 1.0)\
                        .then_inc(S["qk_T"], 1)
            act_e.wait_ge(S["kv_tr"], 1)
            act_e.wait_ge(S["norm_done"], 1)
            for hh in range(H0):
                act_e.activation(kg0[:, hh, :], kv_bank(hh, 0), ACT.Copy, scale=kgs[:, hh:hh + 1])
                m = act_e.activation(kb1[:, hh, :], kv_bank(hh, 1), ACT.Copy, scale=kbs[:, hh:hh + 1])
            m.then_inc(S["kv_done"], 1)
            act_e.wait_ge(S["diff_done"], 1)
            act_e.activation(DT[:, :, :], DT[:, :, :], ACT.Exp).then_inc(S["decay_done"], 1)
            softmax(H0, 0, rows_out)
            for lv in range(1, len(LEVELS)):
                for b in range(2):
                    act_e.wait_ge(S["z_ps"], 2 * lv + b + 1)
                    act_e.activation(Zi[:, 4 * b:4 * b + 4, :],
                                     bank[b][:, :].rearrange("p (c t) -> p c t", c=4), ACT.Copy)\
                        .then_inc(S["Zi_done"], 1)
                if lv == 1:
                    turned(1, 6, 0)
                if lv in (2, 3):
                    split(N_OUT + lv - 1)
            act_e.wait_ge(S["w_ps"], 1)
            act_e.activation(wT1[:, :, :], bank[4][:, :].rearrange("p (c t) -> p c t", c=4), ACT.Copy,
                             scale=-1.0).then_inc(S["wT_done"], 1)
            act_e.wait_ge(S["s_ps"], 1)
            act_e.activation(S1[:, :, :], bank[5][:, :].rearrange("p (c t) -> p c t", c=4), ACT.Copy)\
                .then_inc(S["S_done"], 1)
            split(N_OUT + SPL)
            turned(1, 0, 1)
            for n in range(N_OUT + SPL + 1, N_FFN + SPL):
                split(n)
                if n == N_OUT + SPL + 2 and upto >= 2:
                    turned(2, 2, 0, 1)
                    squares(1, 0)
            if upto < 2:
                return
            turned(2, 4, 1, 1)
            squares(1, 1)

            def ffn_post(q, j):
                act_e.wait_ge(S["act_norm"], j + 1)
                act_e.activation(sil[:, q, :], sil[:, q, :], ACT.Silu).then_inc(S["act_sil"], 1)
                act_e.wait_ge(S["act_done"], j + 1)
                act_e.activation(a_hi[:, q, :], act[:, q, :], ACT.Copy).then_inc(S["aT_hi"], 1)

            with act_e.Fori(0, (FS - 1) // 2) as i:
                for q in range(2):
                    for f in (3, 4, 5):
                        k = N_FFN + 3 * q + f
                        split_at(k, i * 6 + k, i * 16 + 16 * (k // RAW + 1))
                        if f == 3:
                            ffn_post(q, i * 2 + q)
            ffn_post(0, FS - 1)
            for n in range(N_QKV, N_QKV + SPL - 1):
                split(n)
            if upto < 3:
                return
            turned(3, 0, 0, 2)
            split(N_QKV + SPL - 1)
            turned(3, 0, 1, 2)
            squares(2, 0)
            squares(2, 1)
            for n in range(N_QKV + SPL, N_WO + SPL):
                split(n)
                c = n - SPL - N_QKV
                if c % 2 == 1:
                    g = c // 2
                    act_e.wait_ge(S["chunk_used"], N_QKV + 2 * g + 2)
                    if g == 0:
                        act_e.wait_ge(S["root_done"], 3)
                    for b in range(2):
                        m = act_e.activation((zq1, zk1, zv1)[g // 2][:, b, (g % 2) * BLK:(g % 2 + 1) * BLK],
                                             bank[4 + 2 * (g % 2) + b][:, :], ACT.Copy, scale=rstd[:, 4 + b:5 + b])
                    m.then_inc(S["z_out"], 1)
                if c in (3, 7):
                    w = (c - 3) // 4
                    act_e.wait_ge(S["z_out"], 4 + 2 * w + 2)
                    if w == 1:
                        act_e.wait_ge(S["hs_done"], 5)
                    act_e.activation(sq1, (zq1, zk1)[w][:, :, :], ACT.Square).then_inc(S["head_sq"], 1)
            for w, dst in enumerate((qT1, kT1)):
                for hp in range(4):
                    act_e.wait_ge(S["qk_tr"], 4 + 4 * w + hp + 1)
                    act_e.activation(dst[:, 2 * hp:2 * hp + 2, :],
                                     bank[4 * w + hp][:, :].rearrange("p (c t) -> p c t", c=2), ACT.Copy)\
                        .then_inc(S["qk_T"], 1)
            softmax(H1, H0, rows_out1, {6: lambda: turned(4, 6, 0)})
            split(N_WO + SPL)
            turned(4, 0, 1)
            if upto < 4:
                return
            turned(5, 4, 0, 3)
            squares(3, 0)
            act_e.wait_ge(S["chunk_used"], N_MOE)
            turned(5, 0, 1, 3)
            squares(3, 1)

            def split_expert(p, e, c, final):
                if c < PER_E or not final:
                    k = N_MOE + p * NE * PER_E + c
                    split_at(k, e * PER_E + k, e * (16 * PER_E // RAW) + 16 * (k // RAW + 1))

            split_expert(0, 0, 0, False)
            act_e.wait_ge(S["narrow_ps"], 2)
            act_e.activation(turned_small[0:NE, :], bank[0][0:NE, 0:TOK], ACT.Copy).then_inc(S["narrow_done"], 1)
            act_e.wait_ge(S["lg_done"], 1)
            act_e.activation(g2[:, :, 0:1], g2[:, :, 1:2], ACT.Exp).then_inc(S["g_exp"], 1)

            def gathered(n):
                act_e.wait_ge(S["g_ps"], n)
                for b in range(2):
                    m = act_e.activation(x_hi[:, b * BLK:(b + 1) * BLK], bank[1 + 2 * b][:, :], ACT.Copy)
                m.then_inc(S["xh_done"], 1)

            def experts(p, e, final):
                base = N_MOE + p * NE * PER_E

                def used(c):
                    return e * PER_E + (base + c + 1)

                def steps(n):
                    return e * ES + (FS + p * NE * ES + n)

                def turn_act(j):
                    act_e.wait_ge(S["a_tr"], e * ES + (p * NE * ES + j + 1))
                    act_e.activation(a_hi[:, j % 2, :], bank[6][:, :], ACT.Copy).then_inc(S["aT_hi"], 1)
                for c in range(PER_E):
                    if c in U_LAST:
                        j = U_LAST.index(c)
                        act_e.wait_ge(S["chunk_used"], used(c))
                        act_e.activation(sil[:, j % 2, :], bank[j % 2][:, :], ACT.Silu).then_inc(S["act_sil"], 1)
                    split_expert(p, e, c + SPL, final)
                    if c == 0:
                        act_e.wait_ge(S["y_zero"], 1)
                        for half in range(2):
                            m = act_e.activation(y_sb[:, half * BLK:(half + 1) * BLK], bank[4 + half][:, :], ACT.Copy)
                        m.then_inc(S["y_done"], 1)
                    if c - 2 in U_LAST:
                        turn_act(U_LAST.index(c - 2))
                    if c == U_LAST[-1] + 2:
                        gathered(e + (p * (NE + 1) + 2))

            def expert_pass(p):
                for c in range(1 if p == 0 else 0, SPL):
                    split_expert(p, 0, c, False)
                gathered(p * (NE + 1) + 1)
                with act_e.Fori(0, NE - 1) as e:
                    experts(p, e, False)
                experts(p, NE - 1, True)
                act_e.wait_ge(S["chunk_used"], N_MOE + (p + 1) * NE * PER_E)
                for half in range(2):
                    m = act_e.activation(y_sb[:, half * BLK:(half + 1) * BLK], bank[4 + half][:, :], ACT.Copy)
                m.then_inc(S["y_done"], 1)
            expert_pass(0)
            act_e.wait_ge(S["flag_done"], 1)
            over = act_e.value_load(flag[0:1, 0:1], min_val=0, max_val=NE)
            with act_e.If(over > 0):
                expert_pass(1)

        @block.vector
        def _(dve):
            n_step = [0]

            def link(ins):
                n_step[0] += 1
                ins.then_inc(S["dve_step"], 1)
                dve.wait_ge(S["dve_step"], n_step[0])

            def split_at(k, n):
                dve.wait_ge(S["hi_done"], n + 1)
                dve.tensor_tensor(w_lo[:, k % SPL, :], raw[:, k % RAW, :], w_hi[:, k % SPL, :].bitcast(f32),
                                  ALU.subtract).then_inc(S["lo_done"], 1)

            def split(n):
                if n < chunk_limit:
                    split_at(n, n)

            def mean_square(r):
                dve.wait_ge(S["sq_done"], 4 * r + 4)
                link(dve.tensor_tensor(ss[:, r, 0:2], ss[:, r, 0:2], ss[:, r, 2:4], ALU.add))
                dve.tensor_scalar(ss[:, r, 0:2], ss[:, r, 0:2], 1.0 / DM, EPS, ALU.mult, ALU.add)\
                    .then_inc(S["mean_done"], 1)

            def root(r, t):
                return rstd[:, 2 * r + t:2 * r + t + 1]

            def diagonal(r):
                dve.wait_ge(S["root_done"], r + 1)
                for t in range(NT):
                    m = dve.tensor_scalar(diag[:, t, :], ident, root(r, t), None, ALU.mult)
                m.then_inc(S["diag_done"], 1)

            def spread_roots(r):
                dve.wait_ge(S["rbc_ps"], r + 1)
                link(dve.tensor_copy(r_bc[:, :], bank[7 if r == 0 else 3][:, 0:TOK]))
                dve.memset(scr, 0.0).then_inc(S["rbc_done"], 1)

            def turned(r, tb, half, norm_at=None, both=(0, 1)):
                for b in [2 * half + q for q in both]:
                    dve.wait_ge(S["xh_done"], 4 * r + b + 1)
                    if norm_at is None:
                        dve.tensor_tensor(x_lo[:, b * BLK:(b + 1) * BLK], bank[tb + b][:, :],
                                          x_hi[:, b * BLK:(b + 1) * BLK].bitcast(f32), ALU.subtract)\
                            .then_inc(S["xl_done"], 2)
                        continue
                    for kc in (2 * b, 2 * b + 1):
                        dve.scalar_tensor_tensor(xT_lo[:, kc, :], bank[tb + b][:, (kc % 2) * TOK:(kc % 2 + 1) * TOK],
                                                 gcol[:, norm_at, kc:kc + 1], xT_hi[:, kc, :].bitcast(f32),
                                                 ALU.mult, ALU.subtract).then_inc(S["xl_done"], 1)

            def head_sums(at, sq, nh):
                tiles = sq.shape[1]
                s = hs[:, at:at + tiles * nh].rearrange("p (t c) -> p t c", t=tiles)
                link(dve.tensor_reduce(s, sq.rearrange("p t (c d) -> p t c d", d=HD), axis=AX.X, op=ALU.add))
                dve.tensor_scalar(s, s, 1.0 / HD, EPS, ALU.mult, ALU.add).then_inc(S["hs_done"], 1)

            def head_scale(w, at, src, nh):
                tiles = src.shape[1]
                s = hs[:, at:at + tiles * nh].rearrange("p (t c) -> p t c", t=tiles)
                dve.wait_ge(S["hr_root"], w + 1)
                v = src.rearrange("p t (c d) -> p t c d", d=HD)
                return dve.tensor_tensor(v, v, s.unsqueeze(3).to_broadcast([P, tiles, nh, HD]), ALU.mult)

            def query_scale(w, at, nh):
                dve.wait_ge(S["hr_root"], w + 1)
                link(dve.tensor_scalar(q_scale[:, :, 0:nh], hs[:, at:at + NT * nh]
                                       .rearrange("p (t c) -> p t c", t=NT), SCALE, None, ALU.mult))

            def head_gain(src, nh, gname):
                v = src.rearrange("p t (c d) -> p t c d", d=HD)
                g = smallv(gname, HD).unsqueeze(1).unsqueeze(1).to_broadcast([P, NT, nh, HD])
                return dve.tensor_tensor(v, v, g, ALU.mult)

            def softmax(heads, done, bias, fill=None):
                def inverse(i):
                    dve.wait_ge(S["exp_done"], done + i + 1)
                    dve.reciprocal(rl[:, i % 3, :], ls[:, i % 3, :]).then_inc(S["rl_done"], 1)
                for i in range(heads):
                    dve.wait_ge(S["scores_ready"], done + i + 1)
                    if i >= 3:
                        dve.wait_ge(S["p_tr"], done + i - 2)
                    s = prob[i % 3]
                    for t, cs in enumerate((slice(0, P), slice(P, 3 * P))):
                        m = dve.scalar_tensor_tensor(s[:, cs], bank[i % 2][:, cs], q_scale[:, t, i:i + 1],
                                                     bias(i)[:, cs], ALU.mult, ALU.add)
                    link(m)
                    dve.reduce_max(nm[:, i % 3, 0:1], s[:, 0:P], AX.X)
                    link(dve.reduce_max(nm[:, i % 3, 1:2], s[:, P:3 * P], AX.X))
                    dve.tensor_scalar(nm[:, i % 3, :], nm[:, i % 3, :], -1.0, None, ALU.mult).then_inc(S["sc_done"], 1)
                    if i >= 1:
                        inverse(i - 1)
                    if fill and i in fill:
                        fill[i]()
                inverse(heads - 1)

            def add_group(n0, g, banks):
                dve.wait_ge(S["chunk_used"], n0 + g + 3)
                for t in range(NT):
                    v = h[:, t, g * BLK:(g + 1) * BLK]
                    dve.tensor_tensor(v, v, bank[banks + t][:, :], ALU.add).then_inc(S["h_ready"], 1)

            link(dve.memset(zT[:, :, 0:3], 0.0))
            link(dve.memset(coef[:, :], -1.0))
            dve.wait_ge(S["col_T"], 1)
            link(dve.tensor_copy(col_all[:, :], bank[0][:, 0:82]))
            dve.tensor_tensor(qk_gain, col_all[:, 80:81], col_all[:, 81:82], ALU.mult).then_inc(S["col_done"], 1)
            dve.wait_ge(S["col_done"], 1)
            for q in range(4):
                if q % 2 == 0:
                    turned(0, 4, 0, 0, (q // 2,))
                dve.wait_ge(*((S["first_hi"], q + 1) if q < 3 else (S["hi_done"], 1)))
                cs = slice(q * BLK, (q + 1) * BLK)
                dve.tensor_tensor(w_lo[:, 0, cs], raw[:, 0, cs], w_hi[:, 0, cs].bitcast(f32), ALU.subtract)\
                    .then_inc(S["first_lo" if q < 3 else "lo_done"], 1)
            turned(0, 4, 1, 0)
            for n in range(N_IN + 1, N_OUT + SPL):
                if n <= N_OUT and n - SPL < 10:
                    split(n)
                if n == 2:
                    mean_square(0)
                    diagonal(0)
                if n == 2:
                    dve.wait_ge(S["ws_split"], 1)
                    dve.tensor_tensor(ws_lo[:, :, :], ws_raw[:, :, :], ws_hi[:, :, :].bitcast(f32), ALU.subtract)\
                        .then_inc(S["ws_split"], 1)
                c = n - SPL
                if 2 <= c <= 7:
                    g = c // 2 - 1
                    if c % 2 == 0:
                        dve.wait_ge(S["tap_done"], g + 1)
                    for tap in ((1, 2) if c % 2 == 0 else (3,)):
                        for i in range(4 * g, 4 * g + 4):
                            m = dve.scalar_tensor_tensor(cT[:, i, :], zT[:, i, tap:tap + TOK], cw[:, tap, i:i + 1],
                                                         cT[:, i, :], ALU.mult, ALU.add)
                        if tap < 3:
                            link(m)
                        else:
                            m.then_inc(S["cT_done"], 1)
                if c in (1, 3, 5):
                    g = c // 2
                    if g == 0:
                        spread_roots(0)
                        dve.wait_ge(S["rbc_done"], 1)
                    dve.wait_ge(S["chunk_used"], 2 * g + 2)
                    for b in range(2):
                        m = dve.tensor_tensor(zT[:, 4 * g + 2 * b:4 * g + 2 * b + 2, 3:259],
                                              bank[2 * (g % 2) + b][:, :].rearrange("p (c t) -> p c t", c=2),
                                              r_bc[:, :].unsqueeze(1).to_broadcast([P, 2, TOK]), ALU.mult)
                    m.then_inc(S["zT_out"], 1)
                if c == 3:
                    dve.wait_ge(S["small_in"], 16 * len(SMALL))
                    dve.wait_ge(S["pre_ps"], 1)
                    for t in range(NT):
                        b6 = bank[6][:, 12 * t:12 * t + 12]
                        dve.scalar_tensor_tensor(pre[:, t, 0:4], b6[:, 0:4], root(0, t), smallv("fb", 4),
                                                 ALU.mult, ALU.add)
                        dve.scalar_tensor_tensor(pre[:, t, 4:8], b6[:, 4:8], root(0, t), smallv("dt", 4),
                                                 ALU.mult, ALU.add)
                        m = dve.tensor_scalar(pre[:, t, 8:12], b6[:, 8:12], root(0, t), None, ALU.mult)
                    link(m)
                    dve.tensor_scalar(pre[:, :, 0:4], pre[:, :, 0:4], -1.0, None, ALU.mult)
                    link(dve.tensor_scalar(pre[:, :, 8:12], pre[:, :, 8:12], -1.0, None, ALU.mult))
                    link(dve.tensor_scalar(u24[:, :, :], pre[:, :, :], -1.0, None, ALU.mult))
                    dve.tensor_tensor(t24[:, :, :], pre[:, :, :], u24[:, :, :], ALU.min).then_inc(S["pre_done"], 1)
                    dve.wait_ge(S["pre_done"], 1)
                    link(dve.tensor_scalar(gl[:, :, :], pre[:, :, :], 0.0, None, ALU.max))
                if c == 5:
                    dve.wait_ge(S["softplus_e"], 1)
                    dve.tensor_scalar(pre[:, :, :], u24[:, :, :], 1.0, None, ALU.add).then_inc(S["pre_done"], 1)
                    dve.wait_ge(S["pre_done"], 2)
                    link(dve.scalar_tensor_tensor(u24[:, :, :], pre[:, :, :], -1.0, u24[:, :, :], ALU.add, ALU.subtract))
                if c == 7:
                    dve.wait_ge(S["softplus_l"], 1)
                    link(dve.reciprocal(pre[:, :, :], pre[:, :, :]))
                    link(dve.tensor_tensor(u24[:, :, :], u24[:, :, :], pre[:, :, :], ALU.mult))
                    link(dve.tensor_tensor(t24[:, :, :], t24[:, :, :], u24[:, :, :], ALU.subtract))
                    link(dve.tensor_tensor(gl[:, :, :], gl[:, :, :], t24[:, :, :], ALU.add))
                    dve.wait_ge(S["softplus_l"], 2)
                    link(dve.tensor_scalar(coef[:, 4:8], coef[:, 4:8], -1.0, None, ALU.mult))
                    dve.tensor_tensor(gl[:, :, :], gl[:, :, :], coef.unsqueeze(1).to_broadcast([P, NT, 12]), ALU.mult)\
                        .then_inc(S["gates_done"], 1)
                    dve.wait_ge(S["gates_done"], 1)
                if c == 7:
                    dve.wait_ge(S["cT_done"], 3)
                    dve.tensor_copy(bc8.rearrange("p (t c) n -> p t c n", t=NT),
                                    gl[:, :, 0:4].unsqueeze(3).to_broadcast([P, NT, 4, P])).then_inc(S["bc_done"], 1)
                if c == 8:
                    dve.wait_ge(S["head_sq"], 1)
                    head_sums(0, area(12324, NT, BLK), H0)
                if c == 9:
                    dve.wait_ge(S["norm_ps"], 1)
                    dve.tensor_scalar(rqk, bank[4][:, 256:272], EPS, None, ALU.add).then_inc(S["norm_add"], 1)
                    dve.wait_ge(S["cum_ps"], 1)
                    dve.tensor_copy(cols, bank[5][:, 0:20]).then_inc(S["cum_done"], 1)
                if c == 10:
                    dve.wait_ge(S["head_sq"], 2)
                    head_sums(16, area(12324, NT, BLK), H0)
                    dve.wait_ge(S["cum_ps"], 2)
                    dve.tensor_copy(bc8.rearrange("p (t c) n -> p t c n", t=NT),
                                    gl[:, :, 4:8].unsqueeze(3).to_broadcast([P, NT, 4, P])).then_inc(S["bc_done"], 1)
                if c == 11:
                    head_scale(1, 16, zk, H0).then_inc(S["qk_rows_done"], 1)
                    query_scale(0, 0, H0)
                if c == 11:
                    dve.wait_ge(S["cum_ps"], 2)
                    for hh in range(H0):
                        b = bank[6 + hh // 2][:, (hh % 2) * TOK:(hh % 2 + 1) * TOK]
                        dve.scalar_tensor_tensor(bias0[:, hh, 0:P], b[:, 0:P], cols[:, 8 + hh:9 + hh], cst(C_BIAS),
                                                 ALU.subtract, ALU.subtract)
                        m = dve.scalar_tensor_tensor(bias0[:, hh, P:3 * P], b, cols[:, 12 + hh:13 + hh],
                                                     cst(C_BIAS + P, 2 * P), ALU.subtract, ALU.subtract)
                    link(m)
                    dve.tensor_scalar(bias0[:, :, :], bias0[:, :, :], -1.0, None, ALU.mult).then_inc(S["bias_done"], 1)
                    dve.wait_ge(S["bias_done"], 1)
                if c == 12:
                    dve.wait_ge(S["norm_root"], 1)
                    dve.wait_ge(S["beta_done"], 1)
                    r4 = rqk.rearrange("p (w c t) -> p w t c", w=2, t=NT)
                    link(dve.tensor_tensor(be1, beta[:, 1, :], e8[:, 0:4], ALU.mult))
                    dve.tensor_tensor(kgs, e8[:, 4:8], r4[:, 1, 0, :], ALU.mult)
                    dve.tensor_tensor(kbs, be1, r4[:, 1, 1, :], ALU.mult)
                    dve.tensor_tensor(betar[:, :, :], beta[:, :, :], r4[:, 1, :, :], ALU.mult)
                    link(dve.tensor_scalar(okq[:, :, :], r4[:, 0, :, :], SCALE, None, ALU.mult))
                    dve.tensor_tensor(e1q, okq[:, 1, :], e8[:, 0:4], ALU.mult).then_inc(S["norm_done"], 1)
                if c in (10, 11):
                    split(n)
                if c == 13:
                    dve.wait_ge(S["ws_split"], 3)
                    dve.tensor_tensor(wr_lo[:, :, :], wr_raw[:, :, :], wr_hi[:, :, :].bitcast(f32), ALU.subtract)\
                        .then_inc(S["ws_split"], 1)
            if upto < 1:
                dve.wait_ge(S["z_out"], 4)
                dve.memset(scr, 0.0).then_inc(S["h_out"], 1)
                return
            dve.wait_ge(S["gcb_ps"], 1)
            for i in range(8):
                m = dve.tensor_scalar(DT[:, i, :], bank[i // 4][:, (i % 4) * P:(i % 4 + 1) * P],
                                      cols[:, i:i + 1], 0.0, ALU.subtract, ALU.min)
            m.then_inc(S["diff_done"], 1)
            dve.tensor_copy(bc8.rearrange("p (t c) n -> p t c n", t=NT),
                            betar.unsqueeze(3).to_broadcast([P, NT, 4, P])).then_inc(S["bc_done"], 1)
            def weighted_values():
                dve.wait_ge(S["kv_tr"], 1)
                for i in range(8):
                    t, hh = divmod(i, H0)
                    m = dve.tensor_scalar(bv[:, i, :], kv_bank(4 + hh, t), beta[:, t, hh:hh + 1], None, ALU.mult)
                m.then_inc(S["v_done"], 1)

            def causal_decay():
                dve.wait_ge(S["decay_done"], 1)
                dve.tensor_tensor(DT[:, :, :], DT[:, :, :], cst(C_U).unsqueeze(1).to_broadcast([P, 8, P]), ALU.mult)\
                    .then_inc(S["decay_done"], 1)
            softmax(H0, 0, lambda i: bias0[:, i, :],
                    {0: weighted_values, 1: causal_decay, 2: lambda: head_gain(gg, H0, "on")})
            dve.wait_ge(S["decay_done"], 2)

            def rk(i):
                c = 2 * (4 + i % H0) + i // H0
                return rqk[:, c:c + 1]
            for b in range(2):
                dve.wait_ge(S["gcb_ps"], 2 + b)
                m = dve.tensor_tensor(MT[:, 4 * b:4 * b + 4, :], DT[:, 4 * b:4 * b + 4, :],
                                      bank[2 + b][:, :].rearrange("p (c t) -> p c t", c=4), ALU.mult)
            link(m)
            dve.wait_ge(S["kk_ps"], 1)
            for i in range(8):
                m = dve.scalar_tensor_tensor(MT[:, i, :], bank[4 + i // 4][:, (i % 4) * P:(i % 4 + 1) * P], rk(i),
                                             MT[:, i, :], ALU.mult, ALU.mult)
            m.then_inc(S["MT_done"], 1)
            dve.wait_ge(S["MT_done"], 1)

            def level(lv):
                if lv >= 2:
                    dve.wait_ge(S["z_ps"], 2 * (lv - 1))
                mask = cst(C_LEV + lv * P).unsqueeze(1).to_broadcast([P, 8, P])
                dve.tensor_tensor(NTl[lv % 2][:, :, :], MT[:, :, :], mask, ALU.mult).then_inc(S["nt_done"], 1)
            level(0)
            level(1)
            eye = ident.unsqueeze(1)
            dve.wait_ge(S["nt_done"], 1)
            link(dve.tensor_tensor(Yi[:, :, :], eye.to_broadcast([P, 8, P]), NTl[0][:, :, :], ALU.subtract))
            dve.wait_ge(S["z_ps"], 2)
            for b in range(2):
                dve.tensor_tensor(Xi[:, 4 * b:4 * b + 4, :], eye.to_broadcast([P, 4, P]),
                                  bank[b][:, :].rearrange("p (c t) -> p c t", c=4), ALU.subtract)\
                    .then_inc(S["xy_done"], 1)
            dve.wait_ge(S["kq_ps"], 1)
            for i in range(8):
                m = dve.scalar_tensor_tensor(AT[:, i, :], bank[6 + i // 4][:, (i % 4) * P:(i % 4 + 1) * P], rk(i),
                                             DT[:, i, :], ALU.mult, ALU.mult)
            m.then_inc(S["AT_done"], 1)
            for lv in range(1, len(LEVELS)):
                if lv + 1 < len(LEVELS):
                    level(lv + 1)
                last_lv = lv == len(LEVELS) - 1
                for b in range(2):
                    dve.wait_ge(S["xy_done"], 2 * (lv - 1) + b + 1)
                    dve.wait_ge(S["xy_ps"], 2 * (lv - 1) + b + 1)
                    y = Yi[:, 4 * b:4 * b + 4, :]
                    m = dve.tensor_tensor(y, y, bank[2 + b][:, :].rearrange("p (c t) -> p c t", c=4), ALU.subtract)
                    if not last_lv:
                        x = Xi[:, 4 * b:4 * b + 4, :]
                        link(m)
                        m = dve.tensor_tensor(x, x, bank[4 + b][:, :].rearrange("p (c t) -> p c t", c=4), ALU.subtract)
                    m.then_inc(S["xy_done"], 1)
                if lv == 1:
                    turned(1, 6, 0)
                if lv in (2, 3):
                    split(N_OUT + lv - 1)
            dve.wait_ge(S["u_ps"], 1)
            dve.tensor_copy(vn[:, 0, :], bank[0][:, :]).then_inc(S["vn_done"], 1)
            dve.wait_ge(S["u_ps"], 2)
            dve.tensor_copy(vn[:, 1, :], bank[1][:, :]).then_inc(S["vn_done"], 1)
            od = rows_out[:, :, 512:1024]
            osq = area(4096, NT, BLK)

            def head_columns(hh):
                return slice(hh * P, (hh + 1) * P)

            def gated(t):
                link(dve.tensor_tensor(osq[:, t, :], od[:, t, :], od[:, t, :], ALU.mult))
                head_sums(4 * t, osq[:, t:t + 1, :], H0)
                link(dve.tensor_tensor(od[:, t, :], od[:, t, :], gg[:, t, :], ALU.mult))
            dve.wait_ge(S["o_ps"], 1)
            for hh in range(H0):
                m = dve.tensor_scalar(od[:, 0, head_columns(hh)], bank[2][:, head_columns(hh)],
                                      okq[:, 0, hh:hh + 1], None, ALU.mult)
            link(m)
            gated(0)
            dve.wait_ge(S["o_ps"], 2)
            for hh in range(H0):
                m = dve.tensor_scalar(od[:, 1, head_columns(hh)], bank[0][:, head_columns(hh)],
                                      e1q[:, hh:hh + 1], None, ALU.mult)
            link(m)
            dve.wait_ge(S["o_ps"], 3)
            for hh in range(H0):
                m = dve.scalar_tensor_tensor(od[:, 1, head_columns(hh)], bank[3][:, head_columns(hh)],
                                             okq[:, 1, hh:hh + 1], od[:, 1, head_columns(hh)],
                                             ALU.mult, ALU.add)
            link(m)
            gated(1)
            head_scale(2, 0, od[:, 0:1, :], H0)
            head_scale(3, 4, od[:, 1:2, :], H0).then_inc(S["og_done"], 1)
            split(N_OUT + SPL)
            turned(1, 0, 1)
            for n in range(N_OUT + SPL + 1, N_FFN + SPL):
                c = n - SPL - N_OUT
                if c >= 2:
                    add_group(N_OUT, c - 2, 6 if c == 2 else 4)
                split(n)
                if c == 2 and upto >= 2:
                    turned(2, 2, 0, 1)

            def finish(n):
                dve.wait_ge(S["h_ready"], n)
                dve.memset(scr, 0.0).then_inc(S["h_out"], 1)
            if upto < 2:
                return finish(4)
            turned(2, 4, 1, 1)
            mean_square(1)
            diagonal(1)

            def ffn_post(q, n, j):
                r2 = r_bc[:, :].unsqueeze(1).to_broadcast([P, 2, TOK])

                def scaled(dst, b):
                    return dve.tensor_tensor(dst[:, q, :].rearrange("p (c t) -> p c t", c=2),
                                             bank[b][:, :].rearrange("p (c t) -> p c t", c=2), r2, ALU.mult)
                dve.wait_ge(S["chunk_used"], n)
                scaled(sil, 2 * q).then_inc(S["act_norm"], 1)
                scaled(act, 2 * q + 1).then_inc(S["up_norm"], 1)
                dve.wait_ge(S["up_norm"], j + 1)
                dve.wait_ge(S["act_sil"], j + 1)
                dve.tensor_tensor(act[:, q, :], sil[:, q, :], act[:, q, :], ALU.mult).then_inc(S["act_done"], 1)
                dve.wait_ge(S["aT_hi"], j + 1)
                dve.tensor_tensor(a_lo[:, q, :], act[:, q, :], a_hi[:, q, :].bitcast(f32), ALU.subtract)\
                    .then_inc(S["aT_lo"], 1)
            spread_roots(1)
            dve.wait_ge(S["rbc_done"], 2)
            with dve.Fori(0, (FS - 1) // 2) as i:
                for q in range(2):
                    for f in (3, 4, 5):
                        k = N_FFN + 3 * q + f
                        split_at(k, i * 6 + k)
                        if f == 3:
                            ffn_post(q, i * 6 + (N_FFN + 2 if q == 0 else N_FFN + 4), i * 2 + q)
            ffn_post(0, N_FFN + 3 * (FS - 1) + 1, FS - 1)
            for n in range(N_QKV, N_QKV + SPL - 1):
                split(n)
            for half in range(2):
                dve.wait_ge(*((S["sums_half"], 1) if half == 0 else (S["chunk_used"], N_QKV)))
                for t in range(NT):
                    v = h[:, t, half * BLK:(half + 1) * BLK]
                    dve.tensor_tensor(v, v, bank[4 + 2 * half + t][:, :], ALU.add).then_inc(S["h_ready"], 1)
            if upto < 3:
                return finish(8)
            turned(3, 0, 0, 2)
            split(N_QKV + SPL - 1)
            turned(3, 0, 1, 2)
            mean_square(2)

            def rotate_products(w, part):
                dve.tensor_tensor(by_cos[part], heads_halves((zq1, zk1)[w])[part], rotary_table(w, part), ALU.mult)\
                    .then_inc(S["cos_done"], 1)

            def rotate_sums(w):
                x = heads_halves((zq1, zk1)[w])
                dve.wait_ge(S["cos_done"], 2 * w + 2)
                dve.wait_ge(S["sin_done"], w + 1)
                dve.tensor_tensor(x[0], by_cos[0], by_sin[0], ALU.subtract)
                m = dve.tensor_tensor(x[1], by_cos[1], by_sin[1], ALU.add)
                if w == 0:
                    m.then_inc(S["qk_rows_done"], 1)
                else:
                    link(m)

            for w, gname in enumerate(("oq", "ok")):
                for part in range(4):
                    g = smallv(gname, HD)[:, (part % 2) * half_head:(part % 2 + 1) * half_head].unsqueeze(1)\
                        .to_broadcast([P, NT, half_head])
                    m = dve.tensor_tensor(rot[w][:, part, :, :], cst(C_COS if part < 2 else C_SIN)
                                          .rearrange("p (t d) -> p t d", t=NT), g, ALU.mult)
            m.then_inc(S["rot_done"], 1)
            dve.wait_ge(S["rot_done"], 1)
            def rotary_step(c):
                w = c // 4 - 1
                if c in (4, 8):
                    dve.wait_ge(S["z_out"], 6 + 2 * w)
                    dve.wait_ge(S["head_sq"], 3 + w)
                    head_sums(16 - 16 * w, sq1, H1)
                    rotate_products(w, 0)
                if c in (5, 9):
                    rotate_products(w, 1)
                if c == 5:
                    query_scale(4, 16, H1)
                if c in (6, 10):
                    rotate_sums(w)
                if c == 10:
                    head_scale(5, 0, zk1, H1).then_inc(S["qk_rows_done"], 1)
            for c in range(N_WO - N_QKV):
                if c < 9:
                    split(N_QKV + SPL + c)
                rotary_step(c)
                if c >= 9:
                    split(N_QKV + SPL + c)
            softmax(H1, H0, lambda i: cst(C_BIAS, 384), {7: lambda: turned(4, 6, 0)})
            split(N_WO + SPL)
            turned(4, 0, 1)
            add_group(N_WO, 0, 6)
            if upto >= 4:
                turned(5, 4, 0, 3)
            add_group(N_WO, 1, 0)
            if upto < 4:
                return finish(12)
            turned(5, 0, 1, 3)

            def split_expert(p, e, c, final):
                if c < PER_E or not final:
                    k = N_MOE + p * NE * PER_E + c
                    split_at(k, e * PER_E + k)

            mean_square(3)
            for b in (4, 5):
                m = dve.memset(bank[b][:, :], 0.0)
            m.then_inc(S["y_zero"], 1)
            dve.memset(permT[:, :, :], 0.0).then_inc(S["sc_add"], 1)
            link(dve.memset(rank[:, :, :], -1.0))
            link(dve.memset(comb[:, :, :], 0.0))
            dve.wait_ge(S["gain_in"], 16)
            dve.wait_ge(S["root_done"], 4)
            for t in range(NT):
                dve.scalar_tensor_tensor(hn[:, t, :], h[:, t, :], root(3, t), gain[:, :],
                                         ALU.mult, ALU.mult).then_inc(S["rows_done"], 1)
            dve.wait_ge(S["lg_ps"], 1)
            for t in range(NT):
                m = dve.tensor_scalar(lg[:, t, :], bank[1][:, 8 * t:8 * t + 8], root(3, t), None, ALU.mult)
            link(m)
            for t in range(NT):
                m = dve.max(m8[:, 8 * t:8 * t + 8], lg[:, t, :])
            link(m)
            for t in range(NT):
                dve.max_index(idx8[:, t, :], m8[:, 8 * t:8 * t + 8], lg[:, t, :])
                m = dve.tensor_tensor(g2[:, t, 1:2], m8[:, 8 * t + 1:8 * t + 2], m8[:, 8 * t:8 * t + 1], ALU.subtract)
            m.then_inc(S["lg_done"], 1)
            dve.wait_ge(S["g_exp"], 1)
            link(dve.tensor_scalar(g2[:, :, 1:2], g2[:, :, 0:1], 1.0, None, ALU.add))
            link(dve.reciprocal(g2[:, :, 2:3], g2[:, :, 1:2]))
            link(dve.tensor_tensor(g2[:, :, 3:4], g2[:, :, 0:1], g2[:, :, 2:3], ALU.mult))
            idf = t24
            link(dve.tensor_copy(idf[:, :, 0:2], idx8[:, :, 0:2]))
            for t in range(NT):
                dve.tensor_scalar(lg[:, t, :], cst(C_IO8, 8), idf[:, t, 0:1], None, ALU.is_equal)
                dve.tensor_scalar(rank[:, t, 0:8], cst(C_IO8, 8), idf[:, t, 1:2], None, ALU.is_equal)
                m = dve.tensor_scalar(comb[:, t, 0:8], cst(C_IO8, 8), idf[:, t, 0:1], g2[:, t, 2:3],
                                      ALU.is_equal, ALU.mult)
            link(m)
            for t in range(NT):
                m = dve.scalar_tensor_tensor(comb[:, t, 0:8], rank[:, t, 0:8], g2[:, t, 3:4], comb[:, t, 0:8],
                                             ALU.mult, ALU.add)
            link(m)
            dve.tensor_tensor(lg[:, :, :], lg[:, :, :], rank[:, :, 0:8], ALU.add).then_inc(S["route_done"], 1)
            dve.wait_ge(S["route_done"], 1)
            split_expert(0, 0, 0, False)
            dve.wait_ge(S["rank_ps"], 1)
            link(dve.tensor_scalar(rank[:, :, 0:8], bank[2][:, 0:16].rearrange("p (t e) -> p t e", t=NT), 1.0, None,
                                   ALU.add))
            link(dve.tensor_tensor(rank[:, :, 0:8], rank[:, :, 0:8], lg[:, :, :], ALU.mult))
            link(dve.tensor_scalar(rank[:, :, 0:8], rank[:, :, 0:8], -1.0, None, ALU.add))

            def permutation(e):
                for t in range(NT):
                    dve.tensor_scalar(perm[:, t, :], cst(C_IOTA), rank[:, t, bass.ds(e, 1)], None, ALU.is_equal)
                    m = dve.tensor_scalar(permc[:, t, :], cst(C_IOTA), rank[:, t, bass.ds(e, 1)],
                                          comb[:, t, bass.ds(e, 1)], ALU.is_equal, ALU.mult)
                m.then_inc(S["perm_done"], 1)

            def gathered(n):
                dve.wait_ge(S["xh_done"], n - 24)
                for b in range(2):
                    m = dve.tensor_tensor(x_lo[:, b * BLK:(b + 1) * BLK], bank[1 + 2 * b][:, :],
                                          x_hi[:, b * BLK:(b + 1) * BLK].bitcast(f32), ALU.subtract)
                m.then_inc(S["xl_done"], 1)

            def add_scattered(i, n, b=7):
                t, half = divmod(i, 2)
                dve.wait_ge(S["sc_ps"], n)
                v = h[:, t, half * BLK:(half + 1) * BLK]
                dve.tensor_tensor(v, v, bank[b][:, :], ALU.add).then_inc(S["sc_add"], 1)

            def experts(p, e, final):
                def turn_act(j):
                    dve.wait_ge(S["aT_hi"], e * ES + (FS + p * NE * ES + j + 1))
                    dve.tensor_tensor(a_lo[:, j % 2, :], bank[6][:, :], a_hi[:, j % 2, :].bitcast(f32), ALU.subtract)\
                        .then_inc(S["aT_lo"], 1)
                for c in range(PER_E):
                    if c in U_LAST:
                        j = U_LAST.index(c)
                        dve.wait_ge(S["act_sil"], e * ES + (FS + p * NE * ES + j + 1))
                        dve.tensor_tensor(act[:, j % 2, :], sil[:, j % 2, :], bank[2 + j % 2][:, :], ALU.mult)\
                            .then_inc(S["act_done"], 1)
                    if c == U_LAST[-1] + 2:
                        turn_act(ES - 1)
                    split_expert(p, e, c + SPL, final)
                    if c in U_LAST:
                        j = U_LAST.index(c)
                        if 1 <= j <= 4:
                            add_scattered(j - 1, e * 4 + (p * 4 * (NE + 1) + j))
                    if c - 2 in U_LAST and c != U_LAST[-1] + 2:
                        j = U_LAST.index(c - 2)
                        turn_act(j)
                        if j == 5:
                            dve.wait_ge(S["permT_ps"], e + (p * NE + 1))
                            dve.tensor_copy(permT[:, :, :].rearrange("p t n -> p (t n)"), bank[7][:, 0:2 * P])\
                                .then_inc(S["permT_done"], 1)
                            permutation(e + 1)
                    if c == U_LAST[-1] + 2:
                        gathered(e + (p * (NE + 1) + 50))

            def expert_pass(p):
                if p == 1:
                    dve.memset(permT[:, :, :], 0.0).then_inc(S["seed"], 1)
                permutation(0)
                if p == 0:
                    link(dve.reduce_max(scr[0:1, :], bank[2][0:1, 16:24], AX.X))
                    link(dve.tensor_scalar(scr[0:1, :], scr[0:1, :], float(P), None, ALU.is_gt))
                    dve.tensor_copy(flag[:, :], scr[0:1, :]).then_inc(S["flag_done"], 1)
                for c in range(1 if p == 0 else 0, SPL):
                    split_expert(p, 0, c, False)
                gathered(p * (NE + 1) + 49)
                with dve.Fori(0, NE - 1) as e:
                    experts(p, e, False)
                experts(p, NE - 1, True)
                for i in range(4):
                    add_scattered(i, p * 4 * (NE + 1) + 4 * NE + i + 1, 7 - i % 2)
            expert_pass(0)
            over = dve.value_load(flag[0:1, 0:1], min_val=0, max_val=NE)
            with dve.If(over > 0):
                link(dve.tensor_scalar(rank[:, :, 0:8], rank[:, :, 0:8], -float(P), None, ALU.add))
                expert_pass(1)
            dve.drain().then_inc(S["h_out"], 1)


INPUTS = ["x", "e_norm1", "e_w_in", "e_fox_f_bias", "e_fox_q_norm", "e_fox_k_norm", "e_gdn_conv", "e_gdn_a_log",
          "e_gdn_dt_bias", "e_gdn_o_norm", "e_w_out", "e_norm2", "e_ffn_w_gate_up", "e_ffn_w_down", "o_norm1",
          "o_w_qkv", "o_q_norm", "o_k_norm", "o_w_out", "o_norm2", "o_router", "o_exp_w_gate_up", "o_exp_w_down"]


LAST = "moe"


def kernel(**inputs):
    import numpy as np
    import concourse.bacc as bacc
    from concourse import mybir
    from concourse.bass_utils import run_bass_kernel_spmd

    nc = bacc.Bacc("TRN2", target_bir_lowering=False, num_devices=1,
                   dynamic_dma_scratch_size=4096)
    arrays, aps = {}, {}
    for name in INPUTS:
        v = np.ascontiguousarray(inputs[name])
        arrays[f"in_{name}_dram"] = v
        aps[name] = nc.dram_tensor(f"in_{name}_dram", v.shape, mybir.dt.from_np(v.dtype), kind="ExternalInput").ap()
    c = shape_constants()
    arrays["consts_dram"] = c
    aps["consts"] = nc.dram_tensor("consts_dram", c.shape, mybir.dt.from_np(c.dtype), kind="ExternalInput").ap()
    out = nc.dram_tensor("out_dram", (1, TOK, DM), mybir.dt.float32, kind="ExternalOutput").ap()
    build(nc, aps, out, LAST)
    r = run_bass_kernel_spmd(nc, [arrays], core_ids=[0])
    return r.results[0]["out_dram"]
```
